# Optimizing a Trainium2 kernel written in Bass

```python
import math
import jax, jax.numpy as jnp
from jax import lax
import numpy as np

D_MODEL = 2048
BATCH = 1
SEQ = 256
DEPTH = 2

HEAD_DIM = 128
MIX_WIDTH = 2048
Q_BLOCK = 128
ROPE_THETA = 10000.0
EPS = 1e-6
MASKED = -1e30
FORCED = 1e9
NSA_HEADS = 8
NSA_KV_GROUPS = 2
NSA_CMP_LEN = 32
NSA_CMP_STRIDE = 16
NSA_CMP_HIDDEN = 256
NSA_SEL_LEN = 64
NSA_SEL_TOPN = 16
NSA_WINDOW = 512
DIFF_HEADS = 4
DIFF_QK_DIM = 64
DIFF_V_DIM = 128
DSA_HEADS = 12
DSA_KV_HEADS = 4
IDX_HEADS = 16
IDX_DIM = 64
DSA_TOPK_MAX = 256
MEM_HEADS = 4
MEM_LEN = 256

EVEN_SPLITS = (
    NSA_HEADS * HEAD_DIM,
    6 * NSA_KV_GROUPS * HEAD_DIM,
    NSA_HEADS * 3,
    NSA_HEADS * HEAD_DIM,
    DIFF_HEADS * 2 * DIFF_QK_DIM,
    DIFF_HEADS * 2 * DIFF_QK_DIM,
    DIFF_HEADS * DIFF_V_DIM,
    DIFF_HEADS * DIFF_V_DIM,
    MEM_HEADS * HEAD_DIM,
    MEM_HEADS * HEAD_DIM,
)
ODD_SPLITS = (
    DSA_HEADS * HEAD_DIM,
    DSA_KV_HEADS * HEAD_DIM,
    DSA_KV_HEADS * HEAD_DIM,
    IDX_HEADS * IDX_DIM,
    IDX_DIM,
    IDX_HEADS,
    DSA_HEADS * HEAD_DIM,
    MEM_HEADS * HEAD_DIM,
    MEM_HEADS * HEAD_DIM,
)
EVEN_IN = sum(EVEN_SPLITS)
ODD_IN = sum(ODD_SPLITS)


def rms_norm(x, gain):
    xf = x.astype(jnp.float32)
    y = xf * lax.rsqrt(jnp.mean(xf * xf, axis=-1, keepdims=True) + EPS)
    return (y * gain.astype(jnp.float32)).astype(x.dtype)

def rope(x, pos):
    half = x.shape[-1] // 2
    inv = ROPE_THETA ** (-jnp.arange(half, dtype=jnp.float32) / half)
    ang = pos.astype(jnp.float32)[:, None] * inv[None, :]
    cos = jnp.cos(ang)[:, None, :]
    sin = jnp.sin(ang)[:, None, :]
    xf = x.astype(jnp.float32)
    x1, x2 = xf[..., :half], xf[..., half:]
    return jnp.concatenate([x1 * cos - x2 * sin, x2 * cos + x1 * sin], axis=-1).astype(x.dtype)

def masked_softmax(scores, mask):
    s = jnp.where(mask, scores.astype(jnp.float32), MASKED)
    m = jnp.max(s, axis=-1, keepdims=True)
    e = jnp.exp(s - m) * mask
    return e / jnp.maximum(jnp.sum(e, axis=-1, keepdims=True), 1e-30)

def split_cols(h, sizes):
    return jnp.split(h, np.cumsum(sizes)[:-1].tolist(), axis=-1)

def unblock(y):
    y = jnp.moveaxis(y, 0, 1)
    return y.reshape((y.shape[0], y.shape[1] * y.shape[2]) + y.shape[3:])

def nsa_attention(q, kv, gate_logits, pos, cmp_pos, cmp_w1, cmp_w2, qk_gain):
    B, S, H, Dh = q.shape
    G = NSA_KV_GROUPS
    R = H // G
    scale = Dh ** -0.5
    n_cmp = (S - NSA_CMP_LEN) // NSA_CMP_STRIDE + 1
    n_sel = S // NSA_SEL_LEN
    top_n = min(NSA_SEL_TOPN, n_sel)
    cmp_start = np.arange(n_cmp) * NSA_CMP_STRIDE
    cmp_last = jnp.asarray(cmp_start + NSA_CMP_LEN - 1, dtype=jnp.int32)
    cmp_gather = cmp_start[:, None] + np.arange(NSA_CMP_LEN)[None, :]
    sel_start = np.arange(n_sel) * NSA_SEL_LEN
    ov = np.clip(np.minimum(cmp_start[:, None] + NSA_CMP_LEN, sel_start[None, :] + NSA_SEL_LEN)
                 - np.maximum(cmp_start[:, None], sel_start[None, :]), 0, None) / NSA_CMP_LEN
    overlap = jnp.asarray(ov, dtype=jnp.float32)

    qg = rope(rms_norm(q, qk_gain[0]), pos).reshape(B, S, G, R, Dh)
    k_c_raw, v_c_raw, k_s, v_s, k_w, v_w = [kv[:, :, j] for j in range(6)]

    def compress(t, pe, w1, w2):
        blk = t[:, cmp_gather] + pe[:, None, :]
        blk = blk.transpose(0, 1, 3, 2, 4).reshape(B, n_cmp, G, NSA_CMP_LEN * Dh)
        hid = jax.nn.silu(jnp.einsum('bcgf,fh->bcgh', blk, w1))
        return jnp.einsum('bcgh,hd->bcgd', hid, w2)

    k_c = rope(rms_norm(compress(k_c_raw, cmp_pos[0], cmp_w1[0], cmp_w2[0]), qk_gain[1]), cmp_last)
    v_c = compress(v_c_raw, cmp_pos[1], cmp_w1[1], cmp_w2[1])
    k_s = rope(rms_norm(k_s, qk_gain[2]), pos)
    k_w = rope(rms_norm(k_w, qk_gain[3]), pos)

    def to_blocks(t):
        return t.reshape(B, n_sel, NSA_SEL_LEN, G, Dh).transpose(0, 3, 1, 2, 4)

    k_s_blk, v_s_blk = to_blocks(k_s), to_blocks(v_s)
    pad = ((0, 0), (NSA_WINDOW, 0), (0, 0), (0, 0))
    k_w_pad, v_w_pad = jnp.pad(k_w, pad), jnp.pad(v_w, pad)
    gather_blocks = jax.vmap(jax.vmap(lambda tb, ii: tb[ii]))
    sel_ids = jnp.arange(n_sel)
    sel_off = jnp.arange(NSA_SEL_LEN)
    win_off = jnp.arange(NSA_WINDOW + Q_BLOCK)
    vdt = v_c.dtype

    def block(bi):
        q0 = bi * Q_BLOCK
        t = q0 + jnp.arange(Q_BLOCK)
        qb = lax.dynamic_slice_in_dim(qg, q0, Q_BLOCK, 1)
        p_c = masked_softmax(jnp.einsum('btgrd,bcgd->bgrtc', qb, k_c) * scale,
                             cmp_last[None, :] <= t[:, None])
        o_c = jnp.einsum('bgrtc,bcgd->btgrd', p_c.astype(vdt), v_c)
        imp = jnp.einsum('bgrtc,cj->bgtj', p_c, overlap)
        cur = t // NSA_SEL_LEN
        visible = sel_ids[None, :] <= cur[:, None]
        forced = (sel_ids[None, :] == 0) | (sel_ids[None, :] >= cur[:, None] - 1)
        imp = jnp.where(visible, jnp.where(forced, FORCED, imp), MASKED)
        _, idx = lax.top_k(imp, top_n)
        k_sel = gather_blocks(k_s_blk, idx).reshape(B, G, Q_BLOCK, top_n * NSA_SEL_LEN, Dh)
        v_sel = gather_blocks(v_s_blk, idx).reshape(B, G, Q_BLOCK, top_n * NSA_SEL_LEN, Dh)
        tok = (idx[..., None] * NSA_SEL_LEN + sel_off).reshape(B, G, Q_BLOCK, top_n * NSA_SEL_LEN)
        mask_s = (tok <= t[None, None, :, None])[:, :, None]
        p_s = masked_softmax(jnp.einsum('btgrd,bgtkd->bgrtk', qb, k_sel) * scale, mask_s)
        o_s = jnp.einsum('bgrtk,bgtkd->btgrd', p_s.astype(vdt), v_sel)
        kw = lax.dynamic_slice_in_dim(k_w_pad, q0, NSA_WINDOW + Q_BLOCK, 1)
        vw = lax.dynamic_slice_in_dim(v_w_pad, q0, NSA_WINDOW + Q_BLOCK, 1)
        s_pos = q0 - NSA_WINDOW + win_off
        mask_w = ((s_pos[None, :] <= t[:, None]) & (s_pos[None, :] > t[:, None] - NSA_WINDOW)
                  & (s_pos[None, :] >= 0))
        p_w = masked_softmax(jnp.einsum('btgrd,bkgd->bgrtk', qb, kw) * scale, mask_w)
        o_w = jnp.einsum('bgrtk,bkgd->btgrd', p_w.astype(vdt), vw)
        g = jax.nn.sigmoid(lax.dynamic_slice_in_dim(gate_logits, q0, Q_BLOCK, 1).astype(jnp.float32))
        g = g.astype(vdt).reshape(B, Q_BLOCK, G, R, 3)
        return g[..., 0:1] * o_c + g[..., 1:2] * o_s + g[..., 2:3] * o_w

    out = unblock(lax.map(block, jnp.arange(S // Q_BLOCK)))
    return out.reshape(B, S, H * Dh)

def diff_attention(q, k, v, pos, qk_gain, lam_vecs, subln_gain, lambda_init):
    B, S, H, _, dq = q.shape
    q = rope(rms_norm(q, qk_gain[0]).reshape(B, S, 2 * H, dq), pos).reshape(B, S, H, 2, dq)
    k = rope(rms_norm(k, qk_gain[1]).reshape(B, S, 2 * H, dq), pos).reshape(B, S, H, 2, dq)
    lv = lam_vecs.astype(jnp.float32)
    lam = jnp.exp(jnp.sum(lv[0] * lv[1])) - jnp.exp(jnp.sum(lv[2] * lv[3])) + lambda_init
    key_pos = jnp.arange(S)

    def block(bi):
        q0 = bi * Q_BLOCK
        t = q0 + jnp.arange(Q_BLOCK)
        qb = lax.dynamic_slice_in_dim(q, q0, Q_BLOCK, 1)
        p = masked_softmax(jnp.einsum('bthcd,bshcd->bhcts', qb, k) * dq ** -0.5,
                           key_pos[None, :] <= t[:, None])
        a = p[:, :, 0] - lam * p[:, :, 1]
        return jnp.einsum('bhts,bshd->bthd', a.astype(v.dtype), v)

    o = unblock(lax.map(block, jnp.arange(S // Q_BLOCK)))
    o = rms_norm(o, subln_gain) * (1.0 - lambda_init)
    return o.reshape(B, S, H * v.shape[-1])

def dsa_attention(q, k, v, q_idx, k_idx, w_idx, pos, qk_gain):
    B, S, H, Dh = q.shape
    G = DSA_KV_HEADS
    R = H // G
    top_k = min(DSA_TOPK_MAX, S // 4)
    scale = Dh ** -0.5
    qg = rope(rms_norm(q, qk_gain[0]), pos).reshape(B, S, G, R, Dh)
    k = rope(rms_norm(k, qk_gain[1]), pos)
    q_idx = rope(q_idx, pos)
    k_idx = rope(k_idx[:, :, None, :], pos)[:, :, 0]
    w_idx = w_idx * (IDX_HEADS ** -0.5 * IDX_DIM ** -0.5)
    key_pos = jnp.arange(S)
    gather = jax.vmap(lambda tt, ii: tt[ii])

    def block(bi):
        q0 = bi * Q_BLOCK
        t = q0 + jnp.arange(Q_BLOCK)
        qb = lax.dynamic_slice_in_dim(qg, q0, Q_BLOCK, 1)
        qi = lax.dynamic_slice_in_dim(q_idx, q0, Q_BLOCK, 1)
        wi = lax.dynamic_slice_in_dim(w_idx, q0, Q_BLOCK, 1)
        rel = jax.nn.relu(jnp.einsum('bthd,bsd->bths', qi, k_idx)).astype(jnp.float32)
        score = jnp.einsum('bths,bth->bts', rel, wi.astype(jnp.float32))
        causal = key_pos[None, :] <= t[:, None]
        _, idx = lax.top_k(jnp.where(causal, score, MASKED), top_k)
        kg = gather(k, idx)
        vg = gather(v, idx)
        ok = (idx <= t[None, :, None])[:, None, None]
        p = masked_softmax(jnp.einsum('btgrd,btkgd->bgrtk', qb, kg) * scale, ok)
        return jnp.einsum('bgrtk,btkgd->btgrd', p.astype(v.dtype), vg)

    out = unblock(lax.map(block, jnp.arange(S // Q_BLOCK)))
    return out.reshape(B, S, H * Dh)

def memory_attention(q, mem_n, w_kv, qk_gain):
    B, S, H, Dh = q.shape
    kv = jnp.einsum('bmd,dc->bmc', mem_n, w_kv).reshape(B, mem_n.shape[1], 2, H, Dh)
    k = rms_norm(kv[:, :, 0], qk_gain[1])
    v = kv[:, :, 1]
    q = rms_norm(q, qk_gain[0])
    p = jax.nn.softmax((jnp.einsum('bshd,bmhd->bhsm', q, k) * Dh ** -0.5).astype(jnp.float32), axis=-1)
    return jnp.einsum('bhsm,bmhd->bshd', p.astype(v.dtype), v).reshape(B, S, H * Dh)

def first_inputs(seed: int = 0) -> dict:
    key = jax.random.key(seed)
    ks = jax.random.split(key, 17)
    n_even = (DEPTH + 1) // 2
    n_odd = DEPTH // 2

    def nrm(k, shape, scale):
        return jax.random.normal(k, shape, jnp.float32) * scale

    def gain(k, shape):
        return 1.0 + 0.02 * jax.random.normal(k, shape, jnp.float32)

    return {
        "x": nrm(ks[0], (BATCH, SEQ, D_MODEL), 1.0),
        "mem": nrm(ks[1], (BATCH, MEM_LEN, D_MODEL), 1.0),
        "norm_gain": gain(ks[2], (DEPTH, D_MODEL)),
        "mem_norm_gain": gain(ks[3], (D_MODEL,)),
        "mem_w_kv": nrm(ks[4], (DEPTH, D_MODEL, 2 * MEM_HEADS * HEAD_DIM), D_MODEL ** -0.5),
        "mem_qk_gain": gain(ks[5], (DEPTH, 2, HEAD_DIM)),
        "w_out": nrm(ks[6], (DEPTH, MIX_WIDTH, D_MODEL), MIX_WIDTH ** -0.5),
        "even_w_in": nrm(ks[7], (n_even, D_MODEL, EVEN_IN), D_MODEL ** -0.5),
        "nsa_qk_gain": gain(ks[8], (n_even, 4, HEAD_DIM)),
        "nsa_cmp_pos": nrm(ks[9], (n_even, 2, NSA_CMP_LEN, HEAD_DIM), 0.3),
        "nsa_cmp_w1": nrm(ks[10], (n_even, 2, NSA_CMP_LEN * HEAD_DIM, NSA_CMP_HIDDEN), (NSA_CMP_LEN * HEAD_DIM) ** -0.5),
        "nsa_cmp_w2": nrm(ks[11], (n_even, 2, NSA_CMP_HIDDEN, HEAD_DIM), NSA_CMP_HIDDEN ** -0.5),
        "diff_qk_gain": gain(ks[12], (n_even, 2, DIFF_QK_DIM)),
        "diff_lambda": nrm(ks[13], (n_even, 4, DIFF_QK_DIM), 0.1),
        "diff_subln_gain": gain(ks[14], (n_even, DIFF_V_DIM)),
        "odd_w_in": nrm(ks[15], (n_odd, D_MODEL, ODD_IN), D_MODEL ** -0.5),
        "dsa_qk_gain": gain(ks[16], (n_odd, 2, HEAD_DIM)),
    }

def first_block(x, mem, norm_gain, mem_norm_gain, mem_w_kv, mem_qk_gain, w_out, even_w_in,
              nsa_qk_gain, nsa_cmp_pos, nsa_cmp_w1, nsa_cmp_w2, diff_qk_gain, diff_lambda,
              diff_subln_gain, odd_w_in, dsa_qk_gain):
    B, S, _ = x.shape
    pos = jnp.arange(S)
    mem_n = rms_norm(mem, mem_norm_gain)
    for i in range(DEPTH):
        h = rms_norm(x, norm_gain[i])
        if i % 2 == 0:
            e = i // 2
            proj = jnp.einsum('bsd,dc->bsc', h, even_w_in[e])
            a_q, a_kv, a_g, a_z, b_q, b_k, b_v, b_z, m_q, m_z = split_cols(proj, EVEN_SPLITS)
            y_a = nsa_attention(a_q.reshape(B, S, NSA_HEADS, HEAD_DIM),
                                a_kv.reshape(B, S, 6, NSA_KV_GROUPS, HEAD_DIM),
                                a_g.reshape(B, S, NSA_HEADS, 3), pos,
                                nsa_cmp_pos[e], nsa_cmp_w1[e], nsa_cmp_w2[e], nsa_qk_gain[e])
            lambda_init = 0.8 - 0.6 * math.exp(-0.3 * i)
            y_b = diff_attention(b_q.reshape(B, S, DIFF_HEADS, 2, DIFF_QK_DIM),
                                 b_k.reshape(B, S, DIFF_HEADS, 2, DIFF_QK_DIM),
                                 b_v.reshape(B, S, DIFF_HEADS, DIFF_V_DIM), pos,
                                 diff_qk_gain[e], diff_lambda[e], diff_subln_gain[e], lambda_init)
            y_m = memory_attention(m_q.reshape(B, S, MEM_HEADS, HEAD_DIM), mem_n, mem_w_kv[i], mem_qk_gain[i])
            y = jnp.concatenate([y_a * jax.nn.silu(a_z), y_b * jax.nn.silu(b_z),
                                 y_m * jax.nn.silu(m_z)], axis=-1)
        else:
            o = i // 2
            proj = jnp.einsum('bsd,dc->bsc', h, odd_w_in[o])
            c_q, c_k, c_v, i_q, i_k, i_w, c_z, m_q, m_z = split_cols(proj, ODD_SPLITS)
            y_c = dsa_attention(c_q.reshape(B, S, DSA_HEADS, HEAD_DIM),
                                c_k.reshape(B, S, DSA_KV_HEADS, HEAD_DIM),
                                c_v.reshape(B, S, DSA_KV_HEADS, HEAD_DIM),
                                i_q.reshape(B, S, IDX_HEADS, IDX_DIM), i_k, i_w, pos, dsa_qk_gain[o])
            y_m = memory_attention(m_q.reshape(B, S, MEM_HEADS, HEAD_DIM), mem_n, mem_w_kv[i], mem_qk_gain[i])
            y = jnp.concatenate([y_c * jax.nn.silu(c_z), y_m * jax.nn.silu(m_z)], axis=-1)
        x = x + jnp.einsum('bsc,cd->bsd', y, w_out[i])
    return x


DEPTH_2 = 1

POOL_WIDTH = 1024
POOL_WINDOWS = (2, 4, 8, 16)
POOL_GROUPS = len(POOL_WINDOWS)
POOL_GROUP = POOL_WIDTH // POOL_GROUPS
ATTN_HEADS = 8
ATTN_WIDTH = ATTN_HEADS * HEAD_DIM
MIX_WIDTH_2 = POOL_WIDTH + ATTN_WIDTH
IN_COLS = POOL_WIDTH + 3 * ATTN_WIDTH
DILATED_PAIRS = ((128, 1), (512, 4), (2048, 16))
BLOCK = 128
ROPE_THETA_2 = 500000.0
ROPE_DIM = HEAD_DIM // 4
CROSS_HEADS = 4
CROSS_HEAD_DIM = 128
CROSS_WIDTH = CROSS_HEADS * CROSS_HEAD_DIM
PEER_KEYS = 128
PEER_EXPERTS = PEER_KEYS * PEER_KEYS
PEER_HEADS = 8
PEER_QUERY_DIM = 256
PEER_HALF = PEER_QUERY_DIM // 2
PEER_TOPK = 16
PEER_TOKEN_BLOCK = 128


def rmsnorm(x, g):
    xf = x.astype(jnp.float32)
    y = xf * lax.rsqrt(jnp.mean(xf * xf, axis=-1, keepdims=True) + EPS)
    return (y * g.astype(jnp.float32)).astype(x.dtype)

def rope_partial(t, positions):
    half = ROPE_DIM // 2
    inv = ROPE_THETA_2 ** (-jnp.arange(0, ROPE_DIM, 2, dtype=jnp.float32) / ROPE_DIM)
    ang = positions.astype(jnp.float32)[..., None] * inv
    cos = jnp.cos(ang)[:, :, None, :]
    sin = jnp.sin(ang)[:, :, None, :]
    tr = t[..., :ROPE_DIM].astype(jnp.float32)
    x1, x2 = tr[..., :half], tr[..., half:]
    rot = jnp.concatenate([x1 * cos - x2 * sin, x2 * cos + x1 * sin], axis=-1)
    return jnp.concatenate([rot.astype(t.dtype), t[..., ROPE_DIM:]], axis=-1)

def causal_pool_mixer(p, w_pool, pool_scale):
    B, S, _ = p.shape
    pg = p.reshape(B, S, POOL_GROUPS, POOL_GROUP)
    c = jnp.cumsum(pg.astype(jnp.float32), axis=1)
    t = jnp.arange(S)
    pooled = []
    for g, w in enumerate(POOL_WINDOWS):
        cg = c[:, :, g]
        prev = jnp.pad(cg, ((0, 0), (w, 0), (0, 0)))[:, :S]
        cnt = jnp.minimum(t + 1, w).astype(jnp.float32)[None, :, None]
        pooled.append((cg - prev) / cnt)
    mixed = (jnp.stack(pooled, axis=2) - pg.astype(jnp.float32)).astype(p.dtype)
    y = jnp.einsum('bsgc,gce->bsge', mixed, w_pool) * pool_scale
    return y.reshape(B, S, POOL_WIDTH)

def dilated_branch(q, k, v, window, dilation):
    B, S, H, Dh = q.shape
    L = S // dilation
    w_sub = window // dilation
    nb = -(-L // BLOCK)
    Lp = nb * BLOCK

    def to_sub(t):
        t = t.reshape(B, L, dilation, H, Dh).transpose(0, 2, 3, 1, 4).reshape(B * dilation, H, L, Dh)
        t = jnp.pad(t, ((0, 0), (0, 0), (0, Lp - L), (0, 0)))
        return t.reshape(B * dilation, H, nb, BLOCK, Dh)

    def with_prev(t):
        prev = jnp.pad(t, ((0, 0), (0, 0), (1, 0), (0, 0), (0, 0)))[:, :, :nb]
        return jnp.concatenate([prev, t], axis=3)

    qs = to_sub(q)
    kk = with_prev(to_sub(k))
    vv = with_prev(to_sub(v))
    s = jnp.einsum('ghnqd,ghnkd->ghnqk', qs, kk).astype(jnp.float32)
    ql = jnp.arange(BLOCK)[:, None]
    kl = jnp.arange(2 * BLOCK)[None, :]
    dist = ql + BLOCK - kl
    key_idx = jnp.arange(nb)[:, None, None] * BLOCK - BLOCK + kl[None]
    mask = (dist >= 0) & (dist <= w_sub) & (key_idx >= 0)
    s = jnp.where(mask, s, -jnp.inf)
    m = jnp.max(s, axis=-1, keepdims=True)
    pe = jnp.exp(s - m)
    l = jnp.sum(pe, axis=-1, keepdims=True)
    o = jnp.einsum('ghnqk,ghnkd->ghnqd', pe, vv.astype(jnp.float32)) / l
    lse = (m + jnp.log(l))[..., 0]
    o = o.reshape(B, dilation, H, Lp, Dh)[:, :, :, :L].transpose(0, 3, 1, 2, 4).reshape(B, S, H, Dh)
    lse = lse.reshape(B, dilation, H, Lp)[..., :L].transpose(0, 3, 1, 2).reshape(B, S, H)
    return o, lse

def dilated_attention(q, k, v):
    outs, lses = [], []
    for window, dilation in DILATED_PAIRS:
        o, lse = dilated_branch(q, k, v, window, dilation)
        outs.append(o)
        lses.append(lse)
    wts = jax.nn.softmax(jnp.stack(lses, axis=-1), axis=-1)
    o = sum(wts[..., i, None] * outs[i] for i in range(len(outs)))
    return o.astype(q.dtype)

def memory_cross_attention(h, memn, w_cq, w_ck, w_cv, w_co):
    B, S, _ = h.shape
    M = memn.shape[1]
    q = (h @ w_cq).reshape(B, S, CROSS_HEADS, CROSS_HEAD_DIM) * (CROSS_HEAD_DIM ** -0.5)
    k = (memn @ w_ck).reshape(B, M, CROSS_HEADS, CROSS_HEAD_DIM)
    v = (memn @ w_cv).reshape(B, M, CROSS_HEADS, CROSS_HEAD_DIM)
    s = jnp.einsum('bshd,bmhd->bhsm', q, k).astype(jnp.float32)
    p = jax.nn.softmax(s, axis=-1).astype(v.dtype)
    o = jnp.einsum('bhsm,bmhd->bshd', p, v).reshape(B, S, CROSS_WIDTH)
    return o @ w_co

def peer_ffn(h, w_pq, sub_keys_1, sub_keys_2, w_u, w_v):
    B, S, D = h.shape
    T = B * S
    hf = h.reshape(T, D)
    q = (hf @ w_pq).reshape(T, PEER_HEADS, 2, PEER_HALF)
    s1 = jnp.einsum('thd,kd->thk', q[:, :, 0], sub_keys_1).astype(jnp.float32)
    s2 = jnp.einsum('thd,kd->thk', q[:, :, 1], sub_keys_2).astype(jnp.float32)
    v1, i1 = lax.top_k(s1, PEER_TOPK)
    v2, i2 = lax.top_k(s2, PEER_TOPK)
    cand = (v1[..., :, None] + v2[..., None, :]).reshape(T, PEER_HEADS, PEER_TOPK * PEER_TOPK)
    sc, ci = lax.top_k(cand, PEER_TOPK)
    e1 = jnp.take_along_axis(i1, ci // PEER_TOPK, axis=-1)
    e2 = jnp.take_along_axis(i2, ci % PEER_TOPK, axis=-1)
    experts = e1 * PEER_KEYS + e2
    gates = jax.nn.softmax(sc, axis=-1).astype(h.dtype)
    nblk = T // PEER_TOKEN_BLOCK
    idx = experts.reshape(nblk, PEER_TOKEN_BLOCK, PEER_HEADS * PEER_TOPK)
    gts = gates.reshape(nblk, PEER_TOKEN_BLOCK, PEER_HEADS * PEER_TOPK)

    def expert_block(args):
        hb, ib, gb = args
        u = jnp.take(w_u, ib, axis=0)
        a = jnp.einsum('td,tkd->tk', hb, u)
        c = gb * jax.nn.gelu(a)
        vv = jnp.take(w_v, ib, axis=0)
        return jnp.einsum('tk,tkd->td', c, vv)

    y = lax.map(expert_block, (hf.reshape(nblk, PEER_TOKEN_BLOCK, D), idx, gts))
    return y.reshape(B, S, D)

def second_inputs(seed: int = 0) -> dict:
    key = jax.random.key(seed)
    ks = jax.random.split(key, 24)
    f32 = jnp.float32

    def nrm(k, shape, scale):
        return jax.random.normal(k, shape, f32) * scale

    def gain(k, shape):
        return 1.0 + 0.02 * jax.random.normal(k, shape, f32)

    offset = jax.random.randint(ks[2], (BATCH, 1), 0, 1024, dtype=jnp.int32)
    positions = offset + jnp.arange(SEQ, dtype=jnp.int32)[None, :]
    return {
        "x": nrm(ks[0], (BATCH, SEQ, D_MODEL), 1.0),
        "mem": nrm(ks[1], (BATCH, MEM_LEN, D_MODEL), 1.0),
        "positions": positions,
        "g_mix": gain(ks[3], (DEPTH_2, D_MODEL)),
        "w_in": nrm(ks[4], (DEPTH_2, D_MODEL, IN_COLS), D_MODEL ** -0.5),
        "w_pool": nrm(ks[5], (DEPTH_2, POOL_GROUPS, POOL_GROUP, POOL_GROUP), POOL_GROUP ** -0.5),
        "pool_scale": 1.0 + 0.1 * jax.random.normal(ks[6], (DEPTH_2, POOL_GROUPS, POOL_GROUP), f32),
        "w_out": nrm(ks[7], (DEPTH_2, MIX_WIDTH_2, D_MODEL), MIX_WIDTH_2 ** -0.5),
        "g_cross": gain(ks[8], (DEPTH_2, D_MODEL)),
        "g_mem": gain(ks[9], (DEPTH_2, D_MODEL)),
        "w_cq": nrm(ks[10], (DEPTH_2, D_MODEL, CROSS_WIDTH), D_MODEL ** -0.5),
        "w_ck": nrm(ks[11], (DEPTH_2, D_MODEL, CROSS_WIDTH), D_MODEL ** -0.5),
        "w_cv": nrm(ks[12], (DEPTH_2, D_MODEL, CROSS_WIDTH), D_MODEL ** -0.5),
        "w_co": nrm(ks[13], (DEPTH_2, CROSS_WIDTH, D_MODEL), CROSS_WIDTH ** -0.5),
        "g_ffn": gain(ks[14], (DEPTH_2, D_MODEL)),
        "w_pq": nrm(ks[15], (DEPTH_2, D_MODEL, PEER_HEADS * PEER_QUERY_DIM), D_MODEL ** -0.5),
        "sub_keys_1": nrm(ks[16], (DEPTH_2, PEER_KEYS, PEER_HALF), PEER_HALF ** -0.5),
        "sub_keys_2": nrm(ks[17], (DEPTH_2, PEER_KEYS, PEER_HALF), PEER_HALF ** -0.5),
        "w_u": nrm(ks[18], (DEPTH_2, PEER_EXPERTS, D_MODEL), D_MODEL ** -0.5),
        "w_v": nrm(ks[19], (DEPTH_2, PEER_EXPERTS, D_MODEL), (PEER_HEADS * PEER_TOPK) ** -0.5),
        "g_final": gain(ks[20], (D_MODEL,)),
    }

def second_block(x, mem, positions, g_mix, w_in, w_pool, pool_scale, w_out, g_cross, g_mem,
              w_cq, w_ck, w_cv, w_co, g_ffn, w_pq, sub_keys_1, sub_keys_2, w_u, w_v, g_final):
    B, S, _ = x.shape
    for i in range(DEPTH_2):
        h = rmsnorm(x, g_mix[i])
        z = h @ w_in[i]
        p = z[..., :POOL_WIDTH]
        q = z[..., POOL_WIDTH:POOL_WIDTH + ATTN_WIDTH].reshape(B, S, ATTN_HEADS, HEAD_DIM)
        k = z[..., POOL_WIDTH + ATTN_WIDTH:POOL_WIDTH + 2 * ATTN_WIDTH].reshape(B, S, ATTN_HEADS, HEAD_DIM)
        v = z[..., POOL_WIDTH + 2 * ATTN_WIDTH:].reshape(B, S, ATTN_HEADS, HEAD_DIM)
        pool_out = causal_pool_mixer(p, w_pool[i], pool_scale[i])
        q = rope_partial(q, positions) * (HEAD_DIM ** -0.5)
        k = rope_partial(k, positions)
        attn_out = dilated_attention(q, k, v).reshape(B, S, ATTN_WIDTH)
        x = x + jnp.concatenate([pool_out, attn_out], axis=-1) @ w_out[i]
        memn = rmsnorm(mem, g_mem[i])
        x = x + memory_cross_attention(rmsnorm(x, g_cross[i]), memn, w_cq[i], w_ck[i], w_cv[i], w_co[i])
        x = x + peer_ffn(rmsnorm(x, g_ffn[i]), w_pq[i], sub_keys_1[i], sub_keys_2[i], w_u[i], w_v[i])
    return rmsnorm(x, g_final)


def setup_inputs(seed=0):
    out = dict(first_inputs(seed))
    for name, value in second_inputs(seed + 1).items():
        if name != "x":
            out[name + "_2"] = value
    return out


def reference(
    x, mem, norm_gain, mem_norm_gain, mem_w_kv, mem_qk_gain, w_out, even_w_in, nsa_qk_gain,
    nsa_cmp_pos, nsa_cmp_w1, nsa_cmp_w2, diff_qk_gain, diff_lambda, diff_subln_gain, odd_w_in,
    dsa_qk_gain, mem_2, positions_2, g_mix_2, w_in_2, w_pool_2, pool_scale_2, w_out_2,
    g_cross_2, g_mem_2, w_cq_2, w_ck_2, w_cv_2, w_co_2, g_ffn_2, w_pq_2, sub_keys_1_2,
    sub_keys_2_2, w_u_2, w_v_2, g_final_2,
):
    x = first_block(
        x, mem, norm_gain, mem_norm_gain, mem_w_kv, mem_qk_gain, w_out, even_w_in, nsa_qk_gain,
        nsa_cmp_pos, nsa_cmp_w1, nsa_cmp_w2, diff_qk_gain, diff_lambda, diff_subln_gain,
        odd_w_in, dsa_qk_gain,
    )
    return second_block(
        x, mem_2, positions_2, g_mix_2, w_in_2, w_pool_2, pool_scale_2, w_out_2, g_cross_2,
        g_mem_2, w_cq_2, w_ck_2, w_cv_2, w_co_2, g_ffn_2, w_pq_2, sub_keys_1_2, sub_keys_2_2,
        w_u_2, w_v_2, g_final_2,
    )


_drawn_inputs = setup_inputs


def setup_inputs(seed=0):
    import zlib

    import numpy as np

    out = dict(_drawn_inputs(seed))
    spreads = {}
    factors = {'norm_gain': 3.049,
     'mem_norm_gain': 8.0,
     'mem_qk_gain': 8.0,
     'nsa_qk_gain': 8.0,
     'diff_qk_gain': 5.539,
     'diff_lambda': 7.103,
     'diff_subln_gain': 6.381,
     'dsa_qk_gain': 8.0,
     'g_mix_2': 4.806,
     'g_cross_2': 8.0,
     'g_mem_2': 8.0,
     'g_ffn_2': 64.0,
     'g_final_2': 7.839}
    for name, (base, spread) in spreads.items():
        noise = np.random.default_rng([zlib.crc32(name.encode()), seed]).standard_normal(out[name].shape)
        drawn = base * np.exp(spread * noise) if base else spread * noise
        out[name] = __import__('jax').numpy.asarray(drawn.astype(out[name].dtype))
    for name, factor in factors.items():
        out[name] = (out[name] * factor).astype(out[name].dtype)
    return out
```

```python
import math
from contextlib import ExitStack

import concourse.bass as bass
from concourse import mybir
import numpy as np

F32 = mybir.dt.float32
F32R = mybir.dt.float32r
BF16 = mybir.dt.bfloat16
I32 = mybir.dt.int32
U32 = mybir.dt.uint32
ALU = mybir.AluOpType
ACT = mybir.ActivationFunctionType
AX = mybir.AxisListType.X

P = 128
D = 2048
S = 256
NT = S // P
KC = D // P
DH = 128
EPS = 1e-6
MASKED = -1e30
TAKEN = -3e38
RAW = 4
COLS = 512
N_CMP, CMP_STRIDE, CMP_LEN, CMP_HID = 15, 16, 32, 256
E1 = 128
NH = 8
TOPK = 16

EA_Q, EA_KV, EA_G, EA_Z, EB, EM, EVEN_IN = 0, 1024, 2560, 2584, 3608, 5656, 6680
OC, OI, OK_IDX, OZ, OM, ODD_IN = 0, 2560, 3584, 3664, 5200, 6224


def tables():
    f = np.float32
    out = {}
    out["ident"] = np.eye(P, dtype=f)
    t = np.arange(S)

    def rot(pos, half, theta):
        inv = (f(theta) ** (-np.arange(half, dtype=f) / f(half))).astype(f)
        ang = pos.astype(f)[:, None] * inv[None, :]
        c, s = np.cos(ang), np.sin(ang)
        return np.concatenate([c, c, -s, s], axis=1).astype(f)

    def tiled(a):
        return np.ascontiguousarray(a.reshape(NT, P, -1).transpose(1, 0, 2))

    out["rope128"] = tiled(rot(t, 64, 10000.0))
    out["rope64"] = tiled(rot(t, 32, 10000.0))
    cmp_last = np.arange(N_CMP) * CMP_STRIDE + CMP_LEN - 1
    rc = np.zeros((P, 256), f)
    rc[:N_CMP] = rot(cmp_last, 64, 10000.0)
    out["rope_cmp"] = rc
    inv2 = (f(500000.0) ** (-np.arange(0, 32, 2, dtype=f) / f(32))).astype(f)
    out["inv2"] = np.tile(inv2[None], (P, 1))
    dist = t[:, None] - t[None, :]
    causal = dist >= 0
    out["causal"] = tiled(np.where(causal, 0.0, MASKED).astype(f))
    vis = np.zeros((S, 16), f)
    vis[:, :N_CMP] = cmp_last[None] <= t[:, None]
    out["cmp_vis"] = tiled(vis)
    count = (causal & (dist <= 128)).astype(f) + (causal & (dist % 4 == 0)) + (causal & (dist % 16 == 0))
    out["dil_count"] = tiled(count.astype(f))
    out["dil_mask"] = tiled(np.where(count > 0, 0.0, MASKED).astype(f))
    pool = np.zeros((S, 4, S), f)
    for g, w in enumerate((2, 4, 8, 16)):
        for i in range(S):
            n = min(i + 1, w)
            pool[i - n + 1:i + 1, g, i] = f(1.0) / f(n)
            pool[i, g, i] -= f(1.0)
    out["pool"] = np.ascontiguousarray(pool.reshape(NT, P, 4, S).transpose(1, 0, 2, 3))
    out["iota"] = np.tile(np.arange(P, dtype=f)[None], (P, 1))
    return out


CONSTS = tables()


class Item:

    def __init__(self, src, shape):
        self.src, self.shape = src, shape
        self.size = int(np.prod(shape))


def build(nc, A, out, stop=None, dbg=None):
    with ExitStack() as ctx:
        _build(nc, A, out, ctx, stop, dbg)


def _build(nc, A, out, ctx, stop, dbg):
    def sb(name, shape, dt=F32):
        return ctx.enter_context(nc.sbuf_tensor(name, shape, dt))

    def sem(name):
        return ctx.enter_context(nc.semaphore(name))

    ps = ctx.enter_context(nc.psum_tensor("ps", [P, 8, 512], F32))
    x = sb("x", [P, NT, D])
    hT_hi = sb("hT_hi", [P, KC, S], F32R)
    hT_lo = sb("hT_lo", [P, KC, S], F32R)
    raw = sb("raw", [P, RAW, 2048])
    w_hi = sb("w_hi", [P, 2, 2048], F32R)
    w_lo = sb("w_lo", [P, 2, 2048], F32R)
    WORK = 20832
    work = sb("work", [P, WORK])
    ident = sb("ident", [P, P])
    identb = sb("identb", [P, P], BF16)
    causal = sb("causal", [P, NT, S], BF16)
    mask2 = sb("mask2", [P, NT, S], BF16)
    gains = sb("gains", [P, 7, KC])
    small = sb("small", [P, 256])

    def W(off, *shape):
        n = int(np.prod(shape))
        assert off + n <= WORK, (off, shape)
        v = work[:, off:off + n]
        if len(shape) == 2:
            v = v.rearrange("p (a b) -> p a b", a=shape[0])
        elif len(shape) == 3:
            v = v.rearrange("p (a b c) -> p a b c", a=shape[0], b=shape[1])
        return v

    landed = [sem(f"landed{s}") for s in range(RAW)]
    hi_done = sem("hi_done")
    lo_done = sem("lo_done")
    item_used = sem("item_used")
    group_done = sem("group_done")
    evac_act = sem("evac_act")
    evac_dve = sem("evac_dve")
    norm_sum = sem("norm_sum")
    norm_var = sem("norm_var")
    norm_sd = sem("norm_sd")
    norm_r = sem("norm_r")
    over = sem("over")
    act_step = sem("act_step")
    dve_step = sem("dve_step")
    sq_ready = sem("sq_ready")
    sq_free = sem("sq_free")
    turn_ready = sem("turn_ready")
    turn_act = sem("turn_act")
    turn_dve = sem("turn_dve")
    s_ready = sem("s_ready")
    m_ready = sem("m_ready")
    p_ready = sem("p_ready")
    a_ready = sem("a_ready")
    t_ready = sem("t_ready")
    pt_ready = sem("pt_ready")
    o_ready = sem("o_ready")
    o_used = sem("o_used")
    rel_ready = sem("rel_ready")
    relu_done = sem("relu_done")
    rel_used = sem("rel_used")
    const_in = sem("const_in")
    late_in = sem("late_in")
    moved = sem("moved")
    x_in = sem("x_in")
    dve_out = sem("dve_out")
    mix_hi = sem("mix_hi")
    gelu_done = sem("gelu_done")
    hv_ready = sem("hv_ready")
    hh_ready = sem("hh_ready")
    hot_ready = sem("hot_ready")
    gate_ready = sem("gate_ready")
    gate_used = sem("gate_used")
    c_hi_done = sem("c_hi_done")
    c_lo_done = sem("c_lo_done")
    c_used = sem("c_used")
    out_done = sem("out_done")

    items = []
    evacs = [(0, 0)]

    class Gemm:

        def __init__(self, w, c0, c1, dst):
            self.first = len(items) // 4
            self.dst = dst
            self.widths = []
            self.act0, self.dve0 = evacs[-1]
            self.adds = dst is None
            for c in range(c0, c1, COLS):
                n = min(COLS, c1 - c)
                self.widths.append(n)
                evacs.append((evacs[-1][0] + (not self.adds), evacs[-1][1] + 1))
                for j in range(4):
                    at = 4 * KC // 4 * P * c + j * P * 4 * n
                    items.append(Item(w[at:at + P * 4 * n].rearrange("(p x) -> p x", p=P), (4, n)))

    Y = W(0, NT, D)
    MK, MV = W(4096, 4, S), W(5120, NT, 512)
    M_PROJ = W(6144, NT, 1024)
    MQT = W(8192, 4, S)
    MKV = W(9216, NT, 512)
    B_PROJ = W(4096, NT, 2048)
    BQT, BKT = W(8192, 8, S), W(10240, 4, S)
    A_PROJ = W(4096, NT, 3608)
    AQT, AKT = W(11312, 8, S), W(13360, 8, S)
    SCR = 17728
    SQ, TA, TB_ = SCR, SCR + 768, SCR + 1536
    TAB = SCR + 2304
    C_PROJ = W(4096, NT, 5200)
    CQT, CKT = W(14496, 12, S), None
    IQT, IKZ = W(14496, 8, S), W(16544, 2, S)

    def cols(t, a, b):
        return t[:, :, a:b]

    def part(name, k):
        return A[f"{name}.{k}"]

    g_memkv = [None, None]
    g_m = [None, None]
    g_out = [None, None]
    g_memkv[0] = Gemm(part("mem_w_kv", 0), 0, 1024, ("split2", MKV, MV))
    g_m[0] = Gemm(part("even_w", EM), 0, EVEN_IN - EM, M_PROJ)
    g_b = Gemm(part("even_w", EB), 0, EM - EB, B_PROJ)
    g_a = Gemm(part("even_w", 0), 0, 2560 - 0, A_PROJ)
    g_az = Gemm(part("even_w", EA_Z), 0, EB - EA_Z, A_PROJ[:, :, 2584:3608])
    g_ag = Gemm(part("even_w", EA_G), 0, EA_Z - EA_G, A_PROJ[:, :, 2560:2584])
    cmp_first = len(items) // 4
    for j in range(2):
        for q in range(4):
            items.append(Item(A["cmp_w1"][j, q], (8, CMP_HID)))
    g_out[0] = Gemm(part("w_out", 0), 0, D, None)
    g_memkv[1] = Gemm(part("mem_w_kv", 1), 0, 1024, ("split2", MKV, MV))
    g_m[1] = Gemm(part("odd_w", OM), 0, ODD_IN - OM, M_PROJ)
    g_ci = Gemm(part("odd_w", OI), 0, OK_IDX - OI, C_PROJ[:, :, 2560:3584])
    g_ck = Gemm(part("odd_w", OK_IDX), 0, OZ - OK_IDX, C_PROJ[:, :, 3584:3664])
    g_c = Gemm(part("odd_w", 0), 0, 2560 - 0, C_PROJ)
    g_cz = Gemm(part("odd_w", OZ), 0, OM - OZ, C_PROJ[:, :, 3664:5200])
    g_out[1] = Gemm(part("w_out", 1), 0, D, None)
    D_PROJ = W(4096, NT, 4096)
    g_in2 = Gemm(part("w_in_2", 0), 0, 4096, D_PROJ)
    g_out2 = Gemm(part("w_out_2", 0), 0, D, None)
    XKV = W(4096, NT, 1024)
    XQ = W(6144, NT, 512)
    MIXT, WPOOL, POOLM = W(12288, 8, S), W(14336, 8, S), W(16384, 8, S)
    COUNT = W(16384, NT, S)
    XQT, XKT = W(8192, 4, S), W(9216, 4, S)
    g_xk = Gemm(part("w_ck_2", 0), 0, 512, XKV[:, :, 0:512])
    g_xv = Gemm(part("w_cv_2", 0), 0, 512, XKV[:, :, 512:1024])
    g_xq = Gemm(part("w_cq_2", 0), 0, 512, XQ)
    co_first = len(items) // 4
    co_dve0 = evacs[-1][1]
    evacs.append((evacs[-1][0], evacs[-1][1] + 4))
    for j in range(4):
        items.append(Item(A["w_co_2"][j], (4, 512)))
    pq_first = len(items) // 4
    pq_act0, pq_dve0 = evacs[-1]
    evacs.append((evacs[-1][0] + 4, evacs[-1][1] + 4))
    for g in range(4):
        for j in range(4):
            items.append(Item(A["w_pq_2"][g, j], (4, 512)))
    n_static = len(items)
    HALF = E1 // 2
    u_first = [n_static, n_static + 2 * HALF]
    v_first = [n_static + HALF, n_static + 3 * HALF]

    turn_counts = [(0, 0)]

    class Turn:

        def __init__(self, blocks, split=False):
            self.first, self.blocks, self.split = len(turn_counts) - 1, blocks, split
            for b, (_, outs) in enumerate(blocks):
                a, d = turn_counts[-1]
                n = len(outs)
                if split:
                    turn_counts.append((a + n, d + n))
                elif (self.first + b) % 2 == 0:
                    turn_counts.append((a + n, d))
                else:
                    turn_counts.append((a, d + n))

    def head_turn(srcs, dst, scale=None):
        blocks = []
        for h in range(0, len(srcs), 2):
            n = min(2, len(srcs) - h)
            blocks.append(([srcs[h + i][:, t] for i in range(n) for t in range(NT)],
                           [(dst[:, h:h + n], (0, P), (0, n * S), scale)]))
        return Turn(blocks)

    def row_turn(src, gain, chunks=KC, at=0):
        blocks = []
        for k in range(0, chunks, 2):
            blocks.append(([src[:, t, (k + i) * P:(k + i + 1) * P] for i in range(2) for t in range(NT)],
                           [(hT_hi[:, at + k + i], hT_lo[:, at + k + i], (i * S, (i + 1) * S),
                             gains[:, gain, k + i:k + i + 1] if gain is not None else None) for i in range(2)]))
        return Turn(blocks, split=True)

    units = []

    class Attention:

        def __init__(self, us):
            self.first, self.units = len(units), us
            units.extend(us)

    PB = W(SCR, 2, 2, S)
    PTB = W(SCR + 1024, 2, 4, P)

    def heads_of(t, c0, n, dh=DH):
        return [t[:, :, c0 + h * dh:c0 + (h + 1) * dh] for h in range(n)]

    def plain_units(n_heads, qT, kT, vs, dst, mask=None, causal_keys=False, kind="plain", gate=None):
        us = []
        for t in range(NT):
            for h in range(0, n_heads, 2):
                us.append(dict(tile=t, nk=(t + 1) if causal_keys else NT, kind=kind,
                               q=[qT(h + i)[:, t * P:(t + 1) * P] for i in range(2)],
                               k=[kT(h + i) for i in range(2)],
                               v=[vs(h + i) for i in range(2)], mask=mask,
                               dst=dst(t, h), gate=None if gate is None else gate(t, h)))
        return us

    G_MEM, G_X0, G_X1, G_MIX, G_MEM2, G_CROSS, G_FFN = range(7)

    plan = {}
    plan["mem0"] = row_turn(Y, G_MEM)
    plan["mk0"] = head_turn(heads_of(MKV, 0, 4), MK)
    plan["x0"] = row_turn(x, G_X0)
    plan["mq0"] = head_turn(heads_of(M_PROJ, 0, 4), MQT)

    def mem_units(c):
        return plain_units(4, lambda h: MQT[:, h], lambda h: MK[:, h],
                           lambda h: (lambda c_: MV[:, c_, h * DH:(h + 1) * DH]),
                           lambda t, h: Y[:, t, 1536 + h * DH:1536 + (h + 2) * DH])

    plan["am0"] = Attention(mem_units(0))

    def b_blocks():
        blocks = []
        for h in range(4):
            src = [B_PROJ[:, t, h * P:(h + 1) * P] for t in range(NT)]
            blocks.append((src, [(BQT[0:64, 2 * h], (0, 64), (0, S), None),
                                 (BQT[64:P, 2 * h + 1], (64, P), (0, S), None)]))
        return blocks

    plan["bq"] = Turn(b_blocks())
    plan["bk"] = head_turn([B_PROJ[:, :, 512 + h * P:512 + (h + 1) * P] for h in range(4)], BKT)
    bu = []
    for t in range(NT):
        for h in range(4):
            bu.append(dict(tile=t, nk=t + 1, kind="diff", q=[BQT[:, 2 * h + i, t * P:(t + 1) * P] for i in range(2)],
                           k=[BKT[:, h], BKT[:, h]],
                           v=[(lambda c_, h=h: B_PROJ[:, c_, 1024 + h * DH:1024 + (h + 1) * DH])],
                           mask=causal, dst=Y[:, t, 1024 + h * DH:1024 + (h + 1) * DH], gate=None))
    plan["ab"] = Attention(bu)
    plan["raw"] = head_turn(heads_of(A_PROJ, EA_KV, 4), AKT[:, 4:8])
    VBD = W(15408, 512)
    KCT = W(15920, 2, 16)
    GATE = W(15952, NT, 24)
    CHT = W(16000, 2, 2, 32)
    KCN = W(16128, 2, P)
    VCR = W(16384, 2, P)
    W2 = W(16640, 2, 2, P)
    PET = W(17152, 2, CMP_LEN)
    PC, PCT = W(17216, NT, P), W(17472, NT, P)
    ROPE_C = W(20544, 256)
    VIS = W(20800, NT, 16)
    blk_hi = hT_hi[:].rearrange("p k t -> p (k t)")
    blk_lo = hT_lo[:].rearrange("p k t -> p (k t)")
    CH = W(17216, 2, CMP_HID)
    plan["cht"] = Turn([([CH[0:32, j, c * P:(c + 1) * P] for c in range(2)],
                         [(CHT[:, j, c], (0, P), (c * P, c * P + 32), None) for c in range(2)]) for j in range(2)])
    plan["kct"] = Turn([([KCN[0:N_CMP, g] for g in range(2)], [(KCT[:, g, 0:N_CMP], (0, P), (g * P, g * P + N_CMP), None)
                                                             for g in range(2)])])
    plan["aq"] = head_turn(heads_of(A_PROJ, 0, 8), AQT)
    plan["ak"] = head_turn(heads_of(A_PROJ, EA_KV + 512, 2) + heads_of(A_PROJ, EA_KV + 1024, 2), AKT[:, 0:4])
    plan["pc"] = Turn([([PC[:, t] for t in range(NT)], [(PCT, (0, P), (0, S), None)])])

    def nsa_units(kv, comp):
        return plain_units(8, lambda h: AQT[:, h], lambda h: AKT[:, 2 * kv + h // 4],
                           lambda h: (lambda c_: A_PROJ[:, c_, EA_KV + 768 + 512 * kv + (h // 4) * DH:
                                                        EA_KV + 768 + 512 * kv + (h // 4 + 1) * DH]),
                           lambda t, h: Y[:, t, h * DH:(h + 2) * DH], mask=causal, causal_keys=True, kind="gated",
                           gate=lambda t, h: [GATE[:, t, 3 * (h + i) + comp:3 * (h + i) + comp + 1] for i in range(2)])

    plan["as"] = Attention(nsa_units(0, 1) + nsa_units(1, 2))
    plan["y0"] = row_turn(Y, None)
    plan["mem1"] = row_turn(Y, G_MEM)
    plan["mk1"] = head_turn(heads_of(MKV, 0, 4), MK)
    plan["x1"] = row_turn(x, G_X1)
    plan["mq1"] = head_turn(heads_of(M_PROJ, 0, 4), MQT)
    plan["am1"] = Attention(mem_units(1))
    plan["iq"] = head_turn([C_PROJ[:, :, 2560 + h * P:2560 + (h + 1) * P] for h in range(8)], IQT)
    IK2 = W(17056, NT, P)
    plan["ik"] = Turn([([IK2[:, t] for t in range(NT)],
                        [(IKZ[0:64, 0], (0, 64), (0, S), None), (IKZ[64:P, 1], (64, P), (0, S), None)])])
    plan["cq"] = head_turn(heads_of(C_PROJ, 0, 12), CQT)
    KT_ = C_PROJ[:, :, 2560:3584]
    CKT = [KT_[:, h // 2, (h % 2) * 512:(h % 2) * 512 + S] for h in range(4)]
    plan["ck"] = Turn([([C_PROJ[:, t, 1536 + h * DH:1536 + (h + 1) * DH] for t in range(NT)],
                        [(CKT[h], (0, P), (0, S), None)]) for h in range(4)])
    plan["ac"] = Attention(plain_units(
        12, lambda h: CQT[:, h], lambda h: CKT[h // 3],
        lambda h: (lambda c_: C_PROJ[:, c_, 2048 + (h // 3) * DH:2048 + (h // 3 + 1) * DH]),
        lambda t, h: Y[:, t, h * DH:(h + 2) * DH], mask=mask2, causal_keys=True))
    plan["y1"] = row_turn(Y, None)
    plan["x2"] = row_turn(x, G_MIX)
    DQT, DKT = W(12288, 8, S), W(14336, 8, S)
    plan["dq"] = head_turn(heads_of(D_PROJ, 1024, 8), DQT, DH ** -0.5)
    plan["dk"] = head_turn(heads_of(D_PROJ, 2048, 8), DKT)
    plan["ad"] = Attention(plain_units(
        8, lambda h: DQT[:, h], lambda h: DKT[:, h],
        lambda h: (lambda c_: D_PROJ[:, c_, 3072 + h * DH:3072 + (h + 1) * DH]),
        lambda t, h: Y[:, t, h * DH:(h + 2) * DH], mask=mask2, causal_keys=True, kind="dilated"))
    plan["y2"] = row_turn(Y, None, chunks=8, at=8)
    plan["mem2"] = row_turn(Y, G_MEM2)
    plan["xk"] = head_turn(heads_of(XKV, 0, 4), XKT)
    plan["x3"] = row_turn(x, G_CROSS)
    plan["xq"] = head_turn(heads_of(XQ, 0, 4), XQT, DH ** -0.5)
    plan["ax"] = Attention(plain_units(
        4, lambda h: XQT[:, h], lambda h: XKT[:, h],
        lambda h: (lambda c_: XKV[:, c_, 512 + h * DH:512 + (h + 1) * DH]),
        lambda t, h: Y[:, t, h * DH:(h + 2) * DH]))
    plan["y3"] = row_turn(Y, None, chunks=4)
    plan["x4"] = row_turn(Y, G_FFN)
    CT = work[:, 0:HALF * S].rearrange("p (e t) -> p e t", e=HALF)
    E1T = W(16384, S)
    E2T = W(16640, S)
    GT = W(16896, S)
    PQT = W(0, KC, S)
    SKT = W(4096, 2, P)
    SC = W(4352, NT, 16, P)
    NV = NT * 16
    V16 = W(8448, NT, 16, 16)
    I16F = W(8960, NT, 16, 16)
    CAND = W(9472, 8, 256)
    SC16 = W(11520, NT, 8, 16)
    CI16F = W(11776, NT, 8, 16)
    PICK = W(12032, 8, 256)
    KEYS = W(14080, NT, 3, P)
    SKN = W(14848, 2, P)
    I16U = W(15104, NT * 16, 16).bitcast(U32)
    CI16U = W(15616, 3, NT * 8, 16).bitcast(U32)
    HOTV = W(17152, 2, 4, HALF)
    IOTA = W(17664, P)
    plan["sk"] = Turn([([SKN[:, j] for j in range(2)], [(SKT, (0, P), (0, 2 * P), None)])])
    plan["keys"] = Turn([([KEYS[:, t, 0] for t in range(NT)] + [KEYS[:, t, 1] for t in range(NT)],
                          [(W(16384, 2 * S), (0, P), (0, 2 * S), None)]),
                         ([KEYS[:, t, 2] for t in range(NT)], [(GT, (0, P), (0, S), None)])])
    TG = 4
    hot_r = sb("hot_r", [P, 2, TG, P], F32R)
    hot_h = sb("hot_h", [P, 2, TG, HALF], F32R)
    hot_l = sb("hot_l", [P, 2, TG, HALF], F32R)
    c_hi = hot_h[:].rearrange("p b q e -> p b (q e)")
    c_lo = hot_l[:].rearrange("p b q e -> p b (q e)")
    YT = x
    x_dram = nc.dram_tensor("x_kept", (NT, P, D), F32, kind="Internal").ap()
    FIN = W(0, NT, D)
    plan["fin"] = Turn([([YT[:, k // 8, (k % 8) * S + t * P:(k % 8) * S + (t + 1) * P] for k in range(b * 4, b * 4 + 4)],
                         [(FIN[:, t, b * 512:(b + 1) * 512], (0, P), (0, 512), None)])
                        for t in range(NT) for b in range(4)])

    gsm = sb("gsm", [P, 4, P])
    LAM = W(11264, 4, 64)
    XD = W(4096, NT, D)
    GFIN = W(8192, D)
    posi = sb("posi", [P, NT], I32)
    inv2 = sb("inv2", [P, 16])

    block = ctx.enter_context(nc.Block())

    def bcast(ap1, n=None):
        return ap1.partition_broadcast(P)

    def stop_items():
        return {"L0": 4 * g_memkv[1].first, "L1": 4 * g_in2.first, "L2": 4 * g_xk.first, "L3": 4 * pq_first}[stop] + 2

    @block.sync
    def _(sp):
        for t in range(NT):
            sp.dma_start(x[:, t], A["x"][0, t * P:(t + 1) * P]).then_inc(x_in, 16)
        for n in range(n_static if stop is None else stop_items()):
            it = items[n]
            if n >= RAW:
                sp.wait_ge(lo_done, n - RAW + 1)
            dst = raw[:, n % RAW, 0:it.size]
            sp.dma_start(dst, it.src).then_inc(landed[n % RAW], 16)
        if stop is not None:
            return
        uu = A["w_u_t"]
        vv = A["w_v_2"][0].rearrange("(r c) d -> c r d", c=E1)
        for half in range(2):
            for base, src in ((u_first[half], uu), (v_first[half], vv)):
                with sp.Fori(0, HALF // RAW) as i:
                    for s in range(RAW):
                        sp.wait_ge(lo_done, 4 * i + (base + s - RAW + 1))
                        sp.dma_start(raw[:, s], src[bass.ds(4 * i + (half * HALF + s), 1)].rearrange("a p c -> p (a c)")
                                     ).then_inc(landed[s], 16)

    class Steps:

        def __init__(self, eng, s):
            self.eng, self.s, self.n, self.phase = eng, s, 0, 0
            self.sq = 0

        def done(self, ins):
            self.n += 1
            ins.then_inc(self.s, 1)
            self.eng.wait_ge(self.s, self.n)

        def meet(self):
            self.phase += 1
            self.eng.drain().then_inc(over, 1)
            self.eng.wait_ge(over, 3 * self.phase)

    @block.tensor
    def _(pe):
        st = Steps(pe, None)

        def gemm(g):
            n_full = sum(w == COLS for w in g.widths)

            def group(i, q, width):
                par = (g.first + q) % 2
                for j in range(4):
                    pe.wait_ge(lo_done, 4 * i + (4 * g.first + j + 1))
                    n = 4 * g.first + j
                    for k in range(4):
                        c = 4 * j + k
                        for t in range(NT):
                            o = ps[:, 2 * par + t, 0:width]
                            hi, lo = hT_hi[:, c, t * P:(t + 1) * P], hT_lo[:, c, t * P:(t + 1) * P]
                            wh = w_hi[:, j % 2, k * width:(k + 1) * width]
                            wl = w_lo[:, j % 2, k * width:(k + 1) * width]
                            pe.matmul(o, hi, wh, start=(c == 0), stop=False)
                            pe.matmul(o, hi, wl, start=False, stop=False)
                            mm = pe.matmul(o, lo, wh, start=False, stop=(c == KC - 1))
                    mm.then_inc(item_used, 1)
                return mm

            def emptied(i):
                if not isinstance(i, int) or g.dve0 + i - 1 > 0:
                    if not g.adds:
                        pe.wait_ge(evac_act, i + (g.act0 - 1))
                    pe.wait_ge(evac_dve, i + (g.dve0 - 1))

            pairs = n_full // 2 if n_full >= 4 else 0
            if pairs:
                first = 0
                if g.dve0 < 3:
                    first = 1
                    for i in range(2):
                        emptied(i)
                        group(i, i, COLS)
                with pe.Fori(first, pairs) as r:
                    for q in range(2):
                        emptied(2 * r + q)
                        group(2 * r + q, q, COLS)
            for i in range(2 * pairs, len(g.widths)):
                emptied(i)
                group(i, i, g.widths[i])

        def turn(T):
            for b, (srcs, outs) in enumerate(T.blocks):
                n = T.first + b
                if n >= 4:
                    a, d = turn_counts[n - 3]
                    if a:
                        pe.wait_ge(turn_act, a)
                    if d:
                        pe.wait_ge(turn_dve, d)
                for i, s in enumerate(srcs):
                    rows, w = s.shape[0], s.shape[-1]
                    mm = pe.transpose(ps[0:w, 4 + n % 4, i * P:i * P + rows], s, ident[0:rows, 0:rows])
                mm.then_inc(turn_ready, 1)

        def scores(n):
            u = units[n]
            w = u["nk"] * P
            if n >= 2:
                pe.wait_ge(p_ready, n - 1)
            for i in range(2):
                o = ps[:, 4 + n % 2, i * w:(i + 1) * w]
                if u["mask"] is not None:
                    pe.matmul(o, identb[:], u["mask"][:, u["tile"], 0:w], start=(i == 0), stop=False,
                              skip_group_check=True)
                    mm = pe.matmul(o, u["q"][i], u["k"][i][:, 0:w], start=False, stop=True, skip_group_check=True)
                else:
                    mm = pe.matmul(o, u["q"][i], u["k"][i][:, 0:w], start=(i == 0), stop=True,
                                   skip_group_check=True)
            mm.then_inc(s_ready, 1)

        reworked = [0]

        def attend(T):
            N = len(T.units)
            scores(T.first)
            for r in range(N + 1):
                n = T.first + r
                if r + 1 < N:
                    scores(n + 1)
                if r < N:
                    u = units[n]
                    if u["kind"] in ("diff", "dilated"):
                        reworked[0] += 1
                        pe.wait_ge(a_ready, reworked[0])
                    else:
                        pe.wait_ge(p_ready, n + 1)
                    if n >= 2:
                        pe.wait_ge(pt_ready, n - 1)
                    m = 0
                    for i in range(len(u["v"])):
                        for c in range(u["nk"]):
                            mm = pe.transpose(ps[:, 6 + n % 2, m * P:(m + 1) * P],
                                              PB[:, n % 2, i, c * P:(c + 1) * P], ident[:])
                            m += 1
                    mm.then_inc(t_ready, 1)
                if r >= 1:
                    n -= 1
                    u = units[n]
                    pe.wait_ge(pt_ready, n + 1)
                    if n >= 2:
                        pe.wait_ge(o_used, n - 1)
                    for i in range(len(u["v"])):
                        o = ps[:, n % 2, i * P:(i + 1) * P]
                        for c in range(u["nk"]):
                            mm = pe.matmul(o, PTB[:, n % 2, i * u["nk"] + c], u["v"][i](c),
                                           start=(c == 0), stop=(c == u["nk"] - 1))
                    mm.then_inc(o_ready, 1)

        def layer_head(name_mem, gmem, name_k, name_x, gm, name_q, name_a):
            st.meet()
            turn(plan[name_mem])
            st.meet()
            gemm(gmem)
            st.meet()
            qk_phases()
            turn(plan[name_k])
            turn(plan[name_x])
            st.meet()
            gemm(gm)
            st.meet()
            qk_phases()
            turn(plan[name_q])
            st.meet()
            attend(plan[name_a])

        def norm_phases():
            for _ in range(4):
                st.meet()

        def qk_phases():
            for _ in range(3):
                st.meet()

        def cmp_gemm():
            for j in range(2):
                for q in range(4):
                    n = 4 * cmp_first + 4 * j + q
                    pe.wait_ge(lo_done, n + 1)
                    for l in range(8):
                        o = ps[:, j, 0:CMP_HID]
                        a = j * 1024 + (8 * q + l) * 32
                        hi, lo = blk_hi[:, a:a + P], blk_lo[:, a:a + P]
                        wh = w_hi[:, n % 2, l * CMP_HID:(l + 1) * CMP_HID]
                        wl = w_lo[:, n % 2, l * CMP_HID:(l + 1) * CMP_HID]
                        first, last = q + l == 0, q == 3 and l == 7
                        pe.matmul(o, hi, wh, start=first, stop=False)
                        pe.matmul(o, hi, wl, start=False, stop=False)
                        mm = pe.matmul(o, lo, wh, start=False, stop=last)
                    mm.then_inc(item_used, 1)

        st.meet()
        layer_head("mem0", g_memkv[0], "mk0", "x0", g_m[0], "mq0", "am0")
        st.meet()
        gemm(g_b)
        st.meet()
        qk_phases()
        turn(plan["bq"])
        turn(plan["bk"])
        st.meet()
        attend(plan["ab"])
        st.meet()
        qk_phases()
        gemm(g_a)
        gemm(g_az)
        gemm(g_ag)
        st.meet()
        turn(plan["raw"])
        st.meet()
        st.meet()
        cmp_gemm()
        st.meet()
        st.meet()
        turn(plan["cht"])
        st.meet()
        for j in range(2):
            for g in range(2):
                for c in range(2):
                    pe.matmul(ps[0:N_CMP, 2 * j + g, 0:P], CHT[:, j, c, g * 16:g * 16 + N_CMP], W2[:, j, c],
                              start=(c == 0), stop=(c == 1))
        st.meet()
        st.meet()
        qk_phases()
        turn(plan["kct"])
        turn(plan["aq"])
        turn(plan["ak"])
        st.meet()
        for t in range(NT):
            for h in range(8):
                pe.matmul(ps[:, t, h * 16:h * 16 + N_CMP], AQT[:, h, t * P:(t + 1) * P], KCT[:, h // 4, 0:N_CMP],
                          start=True, stop=True)
        st.meet()
        st.meet()
        st.meet()
        st.meet()
        turn(plan["pc"])
        st.meet()
        for t in range(NT):
            for g in range(2):
                pe.matmul(ps[:, 2 * t + g, :], PCT[64 * g:64 * g + 64, t], VBD[64 * g:64 * g + 64, :],
                          start=True, stop=True)
        st.meet()
        st.meet()
        attend(plan["as"])
        st.meet()
        turn(plan["y0"])
        st.meet()
        gemm(g_out[0])
        st.meet()
        if stop == "L0":
            return
        layer_head("mem1", g_memkv[1], "mk1", "x1", g_m[1], "mq1", "am1")
        st.meet()
        gemm(g_ci)
        gemm(g_ck)
        gemm(g_c)
        gemm(g_cz)
        st.meet()
        st.meet()
        turn(plan["iq"])
        turn(plan["ik"])
        st.meet()
        for v in range(16):
            t, b = v // 8, v % 8
            if v >= 2:
                pe.wait_ge(relu_done, v - 1)
            for i in range(2):
                mm = pe.matmul(ps[:, 4 + v % 2, i * S:(i + 1) * S], IQT[:, b, t * P:(t + 1) * P], IKZ[:, i],
                               start=(i == 0), stop=True, skip_group_check=True)
            mm.then_inc(rel_ready, 1)
        st.meet()
        qk_phases()
        turn(plan["cq"])
        turn(plan["ck"])
        st.meet()
        attend(plan["ac"])
        st.meet()
        turn(plan["y1"])
        st.meet()
        gemm(g_out[1])
        st.meet()
        if stop == "L1":
            return
        turn(plan["x2"])
        st.meet()
        gemm(g_in2)
        st.meet()
        st.meet()
        for c in range(8):
            for s in range(NT):
                pe.matmul(ps[:, c // 2, (c % 2) * S:(c % 2 + 1) * S], D_PROJ[:, s, c * P:(c + 1) * P],
                          POOLM[:, 4 * s + c // 2], start=(s == 0), stop=(s == NT - 1))
        st.meet()
        st.meet()
        for g in range(4):
            for e in range(2):
                for c in range(2):
                    pe.matmul(ps[:, g, e * S:(e + 1) * S], WPOOL[:, 2 * g + c, e * P:(e + 1) * P], MIXT[:, 2 * g + c],
                              start=(c == 0), stop=(c == 1))
        st.meet()
        st.meet()
        turn(plan["dq"])
        turn(plan["dk"])
        st.meet()
        attend(plan["ad"])
        st.meet()
        turn(plan["y2"])
        st.meet()
        gemm(g_out2)
        st.meet()
        if stop == "L2":
            return
        st.meet()
        turn(plan["mem2"])
        st.meet()
        gemm(g_xk)
        gemm(g_xv)
        st.meet()
        turn(plan["xk"])
        turn(plan["x3"])
        st.meet()
        gemm(g_xq)
        st.meet()
        turn(plan["xq"])
        st.meet()
        attend(plan["ax"])
        st.meet()
        turn(plan["y3"])
        st.meet()
        for j in range(4):
            n = 4 * co_first + j
            pe.wait_ge(lo_done, n + 1)
            for t in range(NT):
                o = ps[:, 2 * (j % 2) + t, :]
                if j >= 2 and t == 0:
                    pe.wait_ge(evac_dve, co_dve0 + j - 1)
                for k in range(4):
                    hi, lo = hT_hi[:, k, t * P:(t + 1) * P], hT_lo[:, k, t * P:(t + 1) * P]
                    wh, wl = w_hi[:, n % 2, k * 512:(k + 1) * 512], w_lo[:, n % 2, k * 512:(k + 1) * 512]
                    pe.matmul(o, hi, wh, start=(k == 0), stop=False)
                    pe.matmul(o, hi, wl, start=False, stop=False)
                    mm = pe.matmul(o, lo, wh, start=False, stop=(k == 3))
            mm.then_inc(item_used, 1)
        st.meet()
        if stop == "L3":
            return
        norm_phases()
        turn(plan["x4"])
        st.meet()
        for g in range(4):
            if g >= 2:
                pe.wait_ge(evac_act, pq_act0 + g - 1)
                pe.wait_ge(evac_dve, pq_dve0 + g - 1)
            for j in range(4):
                n = 4 * (pq_first + g) + j
                pe.wait_ge(lo_done, n + 1)
                for k in range(4):
                    for c in range(4):
                        o = ps[:, 2 * (g % 2) + c // 2, (c % 2) * S:(c % 2 + 1) * S]
                        a = k * 512 + c * P
                        first = j + k == 0 and c % 2 == 0
                        last = j == 3 and k == 3
                        kc = 4 * j + k
                        pe.matmul(o, w_hi[:, n % 2, a:a + P], hT_hi[:, kc], start=first, stop=False,
                                  skip_group_check=True)
                        pe.matmul(o, w_hi[:, n % 2, a:a + P], hT_lo[:, kc], start=False, stop=False,
                                  skip_group_check=True)
                        mm = pe.matmul(o, w_lo[:, n % 2, a:a + P], hT_hi[:, kc], start=False, stop=last,
                                       skip_group_check=True)
                mm.then_inc(item_used, 1)
        st.meet()
        turn(plan["sk"])
        st.meet()
        for t in range(NT):
            for c in range(16):
                pe.matmul(ps[:, 4 * t + c // 4, (c % 4) * P:(c % 4 + 1) * P], PQT[:, c, t * P:(t + 1) * P],
                          SKT[:, c % 2], start=True, stop=True)
        st.meet()
        st.meet()
        st.meet()
        st.meet()
        st.meet()
        turn(plan["keys"])
        pe.drain().then_inc(gate_ready, 2)
        st.meet()
        for half in range(2):
            ub = u_first[half]
            with pe.Fori(0, HALF // RAW) as i:
                for s in range(RAW):
                    pe.wait_ge(lo_done, 4 * i + (ub + s + 1))
                    pe.wait_ge(gelu_done, 4 * i + (half * HALF + s + 1))
                    o = ps[:, s, 0:S]
                    for k in range(KC):
                        wh, wl = w_hi[:, s % 2, k * P:(k + 1) * P], w_lo[:, s % 2, k * P:(k + 1) * P]
                        pe.matmul(o, wh, hT_hi[:, k], start=(k == 0), stop=False)
                        pe.matmul(o, wh, hT_lo[:, k], start=False, stop=False)
                        mm = pe.matmul(o, wl, hT_hi[:, k], start=False, stop=(k == KC - 1))
                    mm.then_inc(item_used, 1)
            st.meet()
            gb = half * (S // TG)
            with pe.Fori(0, S // TG // 2) as i:
                for b in range(2):
                    pe.wait_ge(hot_ready, 2 * i + (gb + b + 1))
                    pe.wait_ge(gate_used, 2 * i + (gb + b + 1))
                    for q in range(TG):
                        o = ps[:, b, q * HALF:(q + 1) * HALF]
                        pe.matmul(o, hot_r[:, b, q], hot_h[:, b, q], start=True, stop=False)
                        mm = pe.matmul(o, hot_r[:, b, q], hot_l[:, b, q], start=False, stop=True)
                    mm.then_inc(gate_ready, 1)
            st.meet()

            def outputs(idx, s, first, last):
                pe.wait_ge(lo_done, idx + (v_first[half] - half * HALF + 1))
                pe.wait_ge(c_lo_done, idx + 1)
                for k in range(KC):
                    o = ps[:, k // 2, (k % 2) * S:(k % 2 + 1) * S]
                    wh, wl = w_hi[:, s % 2, k * P:(k + 1) * P], w_lo[:, s % 2, k * P:(k + 1) * P]
                    pe.matmul(o, wh, c_hi[:, s % 2], start=first and k % 2 == 0, stop=False, skip_group_check=True)
                    pe.matmul(o, wh, c_lo[:, s % 2], start=False, stop=False, skip_group_check=True)
                    mm = pe.matmul(o, wl, c_hi[:, s % 2], start=False, stop=last, skip_group_check=True)
                mm.then_inc(item_used, 1)

            for s in range(RAW):
                outputs(half * HALF + s, s, s == 0, False)
            with pe.Fori(1, HALF // RAW - 1) as i:
                for s in range(RAW):
                    outputs(4 * i + (half * HALF + s), s, False, False)
            for s in range(RAW):
                outputs(half * HALF + HALF - RAW + s, s, False, s == RAW - 1)
            st.meet()
            st.meet()
        turn(plan["fin"])
        for _ in range(5):
            st.meet()


    NSUM, NSD, NR = 186, 188, 190
    SS, RR, NEG, RSUM, RINV, LAMC, M8 = 0, 64, 132, 140, 148, 156, 168
    ANG_R, ANG_CS = W(18528, NT, 2, 16), W(19648 + 32, NT, 2, 16)
    MXK = W(14848, NT, 8)

    def finish(eng, t):
        for i in range(NT):
            eng.dma_start(out[0, i * P:(i + 1) * P], t[:, i]).then_inc(out_done, 16)
        eng.wait_ge(out_done, 32)

    def sm(a, n=1):
        return small[:, a:a + n]

    def hv(ap, h):
        return ap.rearrange("p (h d) -> p h d", h=h)

    class Norms:
        pass

    def head_jobs(t, c0, n, dh, g, scale=1.0, rope=True, step=None):
        step = step or n
        return [(t[:, tile, c0 + h * dh:c0 + (h + step) * dh], step, dh, g, scale, rope, tile)
                for h in range(0, n, step) for tile in range(NT)]

    SCALE = DH ** -0.5
    J_mk = head_jobs(MKV, 0, 4, DH, 1, 1.0, False)
    J_mq = head_jobs(M_PROJ, 0, 4, DH, 0, SCALE, False)
    J_b = head_jobs(B_PROJ, 0, 8, 64, 0, 64 ** -0.5) + head_jobs(B_PROJ, 512, 8, 64, 1)
    J_sub = head_jobs(Y, 1024, 4, DH, 2, 0.8, False)
    J_a = (head_jobs(A_PROJ, 0, 8, DH, 0, SCALE, step=4) + head_jobs(A_PROJ, EA_KV + 512, 2, DH, 2)
           + head_jobs(A_PROJ, EA_KV + 1024, 2, DH, 3) + [(KCN[0:N_CMP], 2, DH, 1, 1.0, True, "cmp")])
    J_c = head_jobs(C_PROJ, 0, 12, DH, 0, SCALE, step=6) + head_jobs(C_PROJ, 1536, 4, DH, 1)
    ROPE = W(SQ, NT, 256)
    ROPE64 = W(SQ, NT, 128)

    @block.scalar
    def _(act):
        st = Steps(act, act_step)
        late = [0]
        sqs = [0]
        norms = [0]

        def load(dst, src):
            act.dma_start(dst, src).then_inc(late_in, 16)
            late[0] += 16

        def loaded():
            act.wait_ge(late_in, late[0])

        def split(q, s, size):
            if not isinstance(q, int) or 4 * q + s >= 2:
                act.wait_ge(item_used, 4 * q + (s - 1))
            act.wait_ge(landed[s], 16 * q + 16)
            act.activation(w_hi[:, s % 2, 0:size], raw[:, s, 0:size], ACT.Copy).then_inc(hi_done, 1)

        def ahead(n):
            n += 2
            split(n // 4, n % 4, items[n].size if n < n_static else 2048)

        def gemm(g):
            def evac(i):
                if g.adds:
                    return
                act.wait_ge(item_used, 4 * (g.first + i) + 4)
                par, w = (g.first + i) % 2, g.widths[i]
                dst = g.dst[1 + i][:, 0, 0:w] if isinstance(g.dst, tuple) else g.dst[:, 0, i * COLS:i * COLS + w]
                act.wait_ge(norm_r, norms[0])
                act.activation(dst, ps[:, 2 * par, 0:w], ACT.Copy, scale=sm(NR)).then_inc(evac_act, 1)

            for i in range(len(g.widths)):
                for j in range(4):
                    ahead(4 * (g.first + i) + j)
                    if j == 1 and i > 0:
                        evac(i - 1)
            evac(len(g.widths) - 1)

        def turn(T):
            for b, (srcs, outs) in enumerate(T.blocks):
                n = T.first + b
                if T.split:
                    act.wait_ge(turn_ready, n + 1)
                    for hi, lo, (c0, c1), gain in outs:
                        act.activation(hi, ps[:, 4 + n % 4, c0:c1], ACT.Copy,
                                       scale=1.0 if gain is None else gain).then_inc(turn_act, 1)
                elif n % 2 == 0:
                    act.wait_ge(turn_ready, n + 1)
                    for dst, (r0, r1), (c0, c1), scale in outs:
                        src = ps[r0:r1, 4 + n % 4, c0:c1]
                        if len(dst.shape) == 3:
                            src = src.rearrange("p (a b) -> p a b", a=dst.shape[1])
                        act.activation(dst, src, ACT.Copy, scale=scale or 1.0).then_inc(turn_act, 1)

        def attend(T):
            N = len(T.units)
            for r in range(N + 1):
                if r < N:
                    n = T.first + r
                    u = units[n]
                    w = u["nk"] * P
                    act.wait_ge(m_ready, n + 1)
                    if n >= 2:
                        act.wait_ge(t_ready, n - 1)
                    for i in range(2):
                        e = act.activation(PB[:, n % 2, i, 0:w], ps[:, 4 + n % 2, i * w:(i + 1) * w], ACT.Exp,
                                           bias=sm(NEG + 2 * (n % 4) + i), accum_out=sm(RSUM + 2 * (n % 4) + i))
                    e.then_inc(p_ready, 1)
                if r >= 1:
                    n = T.first + r - 1
                    u = units[n]
                    m = len(u["v"]) * u["nk"]
                    act.wait_ge(t_ready, n + 1)
                    if n >= 2:
                        act.wait_ge(o_ready, n - 1)
                    act.activation(PTB[:, n % 2, 0:m], ps[:, 6 + n % 2, 0:m * P].rearrange("p (m q) -> p m q", m=m),
                                   ACT.Copy).then_inc(pt_ready, 1)

        def rows_in(src):
            for t in range(NT):
                load(Y[:, t], src[t * P:(t + 1) * P])
            loaded()
            st.meet()

        def factors(rows):
            for t in range(NT):
                act.activation(Y[:, t], rows[:, t], ACT.Square, accum_out=sm(NSUM + t)).then_inc(norm_sum, 1)
            norms[0] += 1
            act.wait_ge(norm_var, norms[0])
            act.activation(sm(NSD, 2), sm(NSUM, 2), ACT.Sqrt).then_inc(norm_sd, 1)

        def norm(src):
            rows = x if src is x else Y
            for t in range(NT):
                act.activation(W(SCR, D), rows[:, t], ACT.Square, accum_out=sm(128 + t)).then_inc(act_step, 1)
                st.n += 1
                act.wait_ge(act_step, st.n)
            st.meet()
            st.meet()
            act.activation(sm(130, 2), sm(128, 2), ACT.Sqrt)
            st.meet()
            st.meet()

        def qk(jobs, tables=(), mid=None, end=None):
            for j, (src, n, dh, *_, where) in enumerate(jobs):
                if sqs[0]:
                    act.wait_ge(sq_free, sqs[0])
                rows = src.shape[0]
                dst = W(SQ, n * dh)[0:rows]
                if len(src.shape) == 3:
                    dst = hv(dst, n)
                act.activation(dst, src, ACT.Square).then_inc(sq_ready, 1)
                sqs[0] += 1
            loaded()
            st.meet()
            for dst, src in tables:
                load(dst, src)
            tot = sum(j[1] for j in jobs)
            act.activation(sm(SS, tot), sm(SS, tot), ACT.Sqrt)
            if mid:
                mid()
            loaded()
            st.meet()
            if end:
                end()
            st.meet()

        def silu(ap):
            act.activation(ap, ap, ACT.Silu)

        def gain_rows(pairs):
            for slot, ap in pairs:
                load(gsm[:, slot, 0:ap.shape[-1]], ap.partition_broadcast(P))

        def layer_head(l, name_mem, gmem, name_k, name_x, gm, name_q, name_a):
            rows_in(A["mem"])
            gain_rows([(0, A["mem_qk_gain"][l, 0]), (1, A["mem_qk_gain"][l, 1])])
            turn(plan[name_mem])
            factors(Y)
            st.meet()
            gemm(gmem)
            st.meet()
            qk(J_mk)
            turn(plan[name_k])
            turn(plan[name_x])
            factors(x)
            st.meet()
            gemm(gm)
            st.meet()
            qk(J_mq, mid=lambda: silu(M_PROJ[:, :, 512:1024]))
            turn(plan[name_q])
            st.meet()
            attend(plan[name_a])

        act.wait_ge(x_in, 32)
        load(ident[:], A["ident"])
        load(gains[:], A["gains"])
        load(W(SCR, NT, S), A["causal"])
        act.dma_start(W(SCR + 1024, P), A["ident"]).then_inc(late_in, 16)
        late[0] += 16
        loaded()
        split(0, 0, 2048)
        split(0, 1, 2048)
        st.meet()
        layer_head(0, "mem0", g_memkv[0], "mk0", "x0", g_m[0], "mq0", "am0")
        st.meet()
        gain_rows([(0, A["diff_qk_gain"][0, 0]), (1, A["diff_qk_gain"][0, 1]), (2, A["diff_subln_gain"][0])])
        load(LAM.rearrange("p a b -> p (a b)"), A["diff_lambda"][0].rearrange("a b -> (a b)").partition_broadcast(P))
        gemm(g_b)
        st.meet()
        qk(J_b, tables=[(ROPE64, A["rope64"])],
           end=lambda: act.activation(sm(LAMC, 2), sm(LAMC + 2, 2), ACT.Exp))
        turn(plan["bq"])
        turn(plan["bk"])
        st.meet()
        attend(plan["ab"])
        st.meet()
        qk(J_sub, mid=lambda: silu(B_PROJ[:, :, 1536:2048]))
        gain_rows([(j, A["nsa_qk_gain"][0, j]) for j in range(4)])
        load(PET, A["pe_t"])
        load(W2, A["cmp_w2"])
        load(ROPE_C, A["rope_cmp"])
        load(VIS, A["cmp_vis"])
        gemm(g_a)
        gemm(g_az)
        gemm(g_ag)
        loaded()
        st.meet()
        turn(plan["raw"])
        st.meet()
        st.meet()
        for n in range(4 * cmp_first, 4 * cmp_first + 8):
            ahead(n)
        st.meet()
        for j in range(2):
            act.activation(CH[0:32, j], ps[0:32, j, 0:CMP_HID], ACT.Silu)
        st.meet()
        turn(plan["cht"])
        st.meet()
        st.meet()
        st.meet()

        def place_values():
            for g in range(2):
                for r in range(4):
                    load(VBD[64 * g + 16 * r:64 * g + 16 * r + N_CMP, r * P:(r + 1) * P], VCR[0:N_CMP, g])

        def gates():
            act.activation(GATE, A_PROJ[:, :, 2560:2584], ACT.Sigmoid)
            silu(A_PROJ[:, :, 2584:3608])
            place_values()

        qk(J_a, tables=[(ROPE, A["rope128"])], mid=gates)
        turn(plan["kct"])
        turn(plan["aq"])
        turn(plan["ak"])
        st.meet()
        st.meet()
        st.meet()
        act.activation(PC, PC, ACT.Exp)
        st.meet()
        st.meet()
        turn(plan["pc"])
        st.meet()
        st.meet()
        st.meet()
        attend(plan["as"])
        st.meet()
        turn(plan["y0"])
        st.meet()
        gemm(g_out[0])
        st.meet()
        if stop == "L0":
            return finish(act, x)
        layer_head(1, "mem1", g_memkv[1], "mk1", "x1", g_m[1], "mq1", "am1")
        st.meet()
        gain_rows([(0, A["dsa_qk_gain"][0, 0]), (1, A["dsa_qk_gain"][0, 1])])
        load(ROPE64, A["rope64"])
        gemm(g_ci)
        gemm(g_ck)
        gemm(g_c)
        gemm(g_cz)
        loaded()
        st.meet()
        silu(C_PROJ[:, :, 3664:5200])
        st.meet()
        turn(plan["iq"])
        turn(plan["ik"])
        st.meet()
        for v in range(16):
            act.wait_ge(rel_ready, v + 1)
            if v >= 2:
                act.wait_ge(rel_used, v - 1)
            act.activation(W(SCR + 512 * (v % 2), 512), ps[:, 4 + v % 2, :], ACT.Relu).then_inc(relu_done, 1)
        st.meet()
        qk(J_c, tables=[(ROPE, A["rope128"])])
        turn(plan["cq"])
        turn(plan["ck"])
        st.meet()
        attend(plan["ac"])
        st.meet()
        turn(plan["y1"])
        st.meet()
        gemm(g_out[1])
        st.meet()
        if stop == "L1":
            return finish(act, x)
        turn(plan["x2"])
        factors(x)
        st.meet()
        load(WPOOL.rearrange("p (g c) e -> p g c e", g=4), A["w_pool_2"][0].rearrange("g (c p) e -> p g c e", p=P))
        load(POOLM, A["pool"].rearrange("p s g t -> p (s g) t"))
        load(sm(176, 8), A["pool_scale_2"])
        act.dma_start(posi[:], A["positions_2"]).then_inc(late_in, 16)
        late[0] += 16
        load(inv2[:], A["inv2"])
        gemm(g_in2)
        loaded()
        st.meet()
        st.meet()
        act.activation(ANG_CS, ANG_R, ACT.Sin)
        st.meet()
        for b in range(2):
            act.activation(MIXT[:, 2 * b:2 * b + 2], ps[:, b, :].rearrange("p (a t) -> p a t", a=2), ACT.Copy)
        load(COUNT, A["dil_count"])
        load(W(16896, NT, S), A["dil_mask"])
        loaded()
        st.meet()
        st.meet()
        for c in range(8):
            act.activation(hT_hi[:, c], ps[:, c // 2, (c % 2) * S:(c % 2 + 1) * S], ACT.Copy,
                           scale=sm(176 + c)).then_inc(mix_hi, 1)
        st.meet()
        turn(plan["dq"])
        turn(plan["dk"])
        st.meet()
        attend(plan["ad"])
        st.meet()
        turn(plan["y2"])
        st.meet()
        gemm(g_out2)
        st.meet()
        if stop == "L2":
            return finish(act, x)
        rows_in(A["mem_2"])
        turn(plan["mem2"])
        factors(Y)
        st.meet()
        gemm(g_xk)
        gemm(g_xv)
        st.meet()
        turn(plan["xk"])
        turn(plan["x3"])
        factors(x)
        st.meet()
        gemm(g_xq)
        st.meet()
        turn(plan["xq"])
        st.meet()
        attend(plan["ax"])
        st.meet()
        turn(plan["y3"])
        st.meet()
        for j in range(4):
            ahead(4 * co_first + j)
        st.meet()
        if stop == "L3":
            return finish(act, x)
        norm(x)
        act.dma_start(x_dram.rearrange("t p d -> p t d"), x[:]).then_inc(moved, 16)
        load(IOTA, A["iota"])
        for j in range(2):
            load(SKN[:, j], A["sub_keys"][j])
        turn(plan["x4"])
        st.meet()

        def pq_evac(g):
            act.wait_ge(item_used, 4 * (pq_first + g) + 4)
            act.activation(PQT[:, 4 * g:4 * g + 2], ps[:, 2 * (g % 2), :].rearrange("p (a t) -> p a t", a=2),
                           ACT.Copy).then_inc(evac_act, 1)

        for g in range(4):
            for j in range(4):
                ahead(4 * (pq_first + g) + j)
                if j == 1 and g > 0:
                    pq_evac(g - 1)
        pq_evac(3)
        loaded()
        st.meet()
        turn(plan["sk"])
        st.meet()
        st.meet()
        for b in range(4):
            act.activation(SC[:, b // 4, (b % 4) * 4:(b % 4 + 1) * 4], ps[:, b, :].rearrange("p (a t) -> p a t", a=4),
                           ACT.Copy)
        st.meet()
        st.meet()
        act.activation(SC16, SC16, ACT.Exp)
        st.meet()
        st.meet()
        turn(plan["keys"])
        act.drain().then_inc(gelu_done, 4)
        st.meet()
        for half in range(2):
            base = half * HALF

            def activate(i, s):
                act.wait_ge(item_used, 4 * i + (u_first[half] + s + 1))
                act.activation(CT[:, bass.ds(4 * i + s, 1)].rearrange("p a t -> p (a t)"), ps[:, s, 0:S],
                               ACT.Gelu_apprx_tanh).then_inc(gelu_done, 1)

            def high(i, s):
                idx = 4 * i + s
                if not isinstance(i, int) or idx >= 2:
                    act.wait_ge(item_used, 4 * i + (v_first[half] + s - 1))
                act.activation(c_hi[:, s % 2], CT[:, bass.ds(idx, 1)].rearrange("p a t -> p (a t)"),
                               ACT.Copy).then_inc(c_hi_done, 1)

            with act.Fori(0, HALF // RAW) as i:
                for s in range(RAW):
                    split(i + (u_first[half] // 4 + (s + 2) // 4), (s + 2) % 4, 2048)
                    activate(i, s)
            st.meet()
            with act.Fori(0, S // TG // 2) as i:
                for b in range(2):
                    act.wait_ge(hv_ready, 2 * i + (half * (S // TG) + b + 1))
                    act.activation(hot_h[:, b], HOTV[:, b], ACT.Copy).then_inc(hh_ready, 1)
            st.meet()
            high(0, 0)

            def v_step(i, s, last):
                if not (last and s == 3):
                    high(i + (s + 1) // 4, (s + 1) % 4)
                if not (last and s >= 2 and half == 1):
                    split(i + (v_first[half] // 4 + (s + 2) // 4), (s + 2) % 4, 2048)

            for s in range(RAW):
                v_step(0, s, False)
            with act.Fori(1, HALF // RAW - 1) as i:
                for s in range(RAW):
                    v_step(i, s, False)
            for s in range(RAW):
                v_step(HALF // RAW - 1, s, True)
            st.meet()
            if half == 0:
                act.wait_ge(moved, 16)
                for b in range(4):
                    act.activation(YT[:, 0, b * 512:(b + 1) * 512], ps[:, b, :], ACT.Copy)
            st.meet()
        turn(plan["fin"])
        load(XD, x_dram.rearrange("t p d -> p t d"))
        load(GFIN, A["g_final_2"].partition_broadcast(P))
        loaded()
        st.meet()
        st.meet()
        for t in range(NT):
            act.activation(W(SCR, D), FIN[:, t], ACT.Square, accum_out=sm(128 + t)).then_inc(act_step, 1)
            st.n += 1
            act.wait_ge(act_step, st.n)
        st.meet()
        st.meet()
        act.activation(sm(130, 2), sm(128, 2), ACT.Sqrt)
        st.meet()
        act.wait_ge(dve_out, 1)
        for t in range(NT):
            act.dma_start(out[0, t * P:(t + 1) * P], FIN[:, t]).then_inc(out_done, 16)
        act.wait_ge(out_done, 32)

    @block.vector
    def _(dve):
        st = Steps(dve, dve_step)
        done = st.done
        sqs = [0]
        reworked = [0]
        norms = [0]

        def split(q, s, size):
            dve.wait_ge(hi_done, 4 * q + (s + 1))
            dve.tensor_tensor(w_lo[:, s % 2, 0:size], raw[:, s, 0:size], w_hi[:, s % 2, 0:size].bitcast(F32),
                              ALU.subtract).then_inc(lo_done, 1)

        def ahead(n):
            n += 2
            split(n // 4, n % 4, items[n].size if n < n_static else 2048)

        def gemm(g):
            def evac(i):
                dve.wait_ge(item_used, 4 * (g.first + i) + 4)
                par, w = (g.first + i) % 2, g.widths[i]
                if g.adds:
                    for t in range(NT):
                        xs = x[:, t, i * COLS:i * COLS + w]
                        e = dve.tensor_tensor(xs, xs, ps[:, 2 * par + t, 0:w], ALU.add)
                else:
                    dst = g.dst[1 + i][:, 1, 0:w] if isinstance(g.dst, tuple) else g.dst[:, 1, i * COLS:i * COLS + w]
                    e = dve.tensor_scalar(dst, ps[:, 2 * par + 1, 0:w], sm(NR + 1), None, ALU.mult)
                e.then_inc(evac_dve, 1)

            for i in range(len(g.widths)):
                for j in range(4):
                    ahead(4 * (g.first + i) + j)
                    if j == 1 and i > 0:
                        evac(i - 1)
            evac(len(g.widths) - 1)

        def turn(T):
            for b, (srcs, outs) in enumerate(T.blocks):
                n = T.first + b
                if T.split:
                    for m, (hi, lo, (c0, c1), gain) in enumerate(outs):
                        dve.wait_ge(turn_act, turn_counts[n + 1][0])
                        src = ps[:, 4 + n % 4, c0:c1]
                        if gain is None:
                            dve.tensor_tensor(lo, src, hi.bitcast(F32), ALU.subtract).then_inc(turn_dve, 1)
                        else:
                            dve.scalar_tensor_tensor(out=lo, in0=src, scalar=gain, in1=hi.bitcast(F32),
                                                     op0=ALU.mult, op1=ALU.subtract).then_inc(turn_dve, 1)
                elif n % 2 == 1:
                    dve.wait_ge(turn_ready, n + 1)
                    for dst, (r0, r1), (c0, c1), scale in outs:
                        src = ps[r0:r1, 4 + n % 4, c0:c1]
                        if len(dst.shape) == 3:
                            src = src.rearrange("p (a b) -> p a b", a=dst.shape[1])
                        if scale:
                            dve.tensor_scalar(dst, src, scale, None, ALU.mult).then_inc(turn_dve, 1)
                        else:
                            dve.tensor_copy(dst, src).then_inc(turn_dve, 1)

        def attend(T):
            N = len(T.units)
            for r in range(N + 2):
                if r < N:
                    n = T.first + r
                    w = units[n]["nk"] * P
                    dve.wait_ge(s_ready, n + 1)
                    dve.tensor_reduce(sm(NEG + 2 * (n % 4), 2), hv(ps[:, 4 + n % 2, 0:2 * w], 2), AX, ALU.max,
                                      negate=True).then_inc(m_ready, 1)
                if 1 <= r <= N:
                    n = T.first + r - 1
                    u = units[n]
                    w, c = u["nk"] * P, 2 * (n % 4)
                    dve.wait_ge(p_ready, n + 1)
                    if u["kind"] == "dilated":
                        pb = PB[:, n % 2, :, 0:w]
                        done(dve.tensor_tensor(pb, pb, COUNT[:, u["tile"], 0:w].unsqueeze(1).broadcast_to([P, 2, w]),
                                               ALU.mult))
                        dve.tensor_reduce(sm(RSUM + c, 2), pb, AX, ALU.add).then_inc(a_ready, 1)
                        reworked[0] += 1
                        dve.wait_ge(a_ready, reworked[0])
                    done(dve.reciprocal(sm(RINV + c, 2), sm(RSUM + c, 2)))
                    if u["kind"] == "diff":
                        done(dve.tensor_tensor(sm(RINV + c + 1), sm(RINV + c + 1), sm(LAMC + 4), ALU.mult))
                        p0, p1 = PB[:, n % 2, 0, 0:w], PB[:, n % 2, 1, 0:w]
                        done(dve.tensor_scalar(p0, p0, sm(RINV + c), None, ALU.mult))
                        dve.scalar_tensor_tensor(out=p0, in0=p1, scalar=sm(RINV + c + 1), in1=p0,
                                                 op0=ALU.mult, op1=ALU.add).then_inc(a_ready, 1)
                        reworked[0] += 1
                    if u["kind"] == "gated":
                        for i in range(2):
                            e = dve.tensor_tensor(sm(RINV + c + i), sm(RINV + c + i), u["gate"][i], ALU.mult)
                        done(e)
                if r >= 2:
                    n = T.first + r - 2
                    u = units[n]
                    c = 2 * (n % 4)
                    dve.wait_ge(o_ready, n + 1)
                    nv = len(u["v"])
                    o = hv(ps[:, n % 2, 0:nv * P], nv)
                    if u["kind"] == "gated":
                        for i in range(2):
                            y = u["dst"][:, i * P:(i + 1) * P]
                            e = dve.scalar_tensor_tensor(out=y, in0=o[:, i], scalar=sm(RINV + c + i), in1=y,
                                                         op0=ALU.mult, op1=ALU.add)
                    elif u["kind"] == "diff":
                        e = dve.tensor_copy(u["dst"], o[:, 0])
                    else:
                        e = dve.tensor_tensor(hv(u["dst"], 2), o,
                                              sm(RINV + c, 2).unsqueeze(2).broadcast_to([P, 2, P]), ALU.mult)
                    e.then_inc(o_used, 1)
            dve.wait_ge(o_used, T.first + N)

        def factors():
            norms[0] += 1
            dve.wait_ge(norm_sum, 2 * norms[0])
            dve.tensor_scalar(sm(NSUM, 2), sm(NSUM, 2), 1.0 / D, EPS, ALU.mult, ALU.add).then_inc(norm_var, 1)
            dve.wait_ge(norm_sd, norms[0])
            dve.reciprocal(sm(NR, 2), sm(NSD, 2)).then_inc(norm_r, 1)
            dve.wait_ge(norm_r, norms[0])

        def norm(src):
            st.meet()
            dve.tensor_scalar(sm(128, 2), sm(128, 2), 1.0 / D, EPS, ALU.mult, ALU.add)
            st.meet()
            st.meet()
            done(dve.reciprocal(sm(128, 2), sm(130, 2)))
            for t in range(NT):
                rows = x[:, t] if src is x else Y[:, t]
                dve.tensor_scalar(Y[:, t], rows, sm(128 + t), None, ALU.mult)
            st.meet()

        def rotate(src, dst, n, dh, C, Sn, r=None, rows=P):
            half = dh // 2
            if r is not None:
                na = hv(W(TA, n * dh)[0:rows], n)
                done(dve.tensor_tensor(na, src, r.unsqueeze(2).broadcast_to([rows, n, dh]), ALU.mult))
            else:
                na = src
            nb = hv(W(TB_, n * dh)[0:rows], n)
            nc_ = hv(W(TA, n * dh)[0:rows], n) if r is None else dst

            def b(ap, w):
                return ap.unsqueeze(1).broadcast_to([rows, n, w])

            dve.tensor_tensor(nb[:, :, 0:half], na[:, :, half:dh], b(Sn[:, 0:half], half), ALU.mult)
            dve.tensor_tensor(nb[:, :, half:dh], na[:, :, 0:half], b(Sn[:, half:dh], half), ALU.mult)
            done(dve.tensor_tensor(nc_, na, b(C, dh), ALU.mult))
            done(dve.tensor_tensor(dst, nc_, nb, ALU.add))

        def qk(jobs, rope_dh=None, mid=None, first=None):
            off = 0
            offs = []
            if first:
                first()
            for src, n, dh, g, scale, rope, where in jobs:
                sqs[0] += 1
                dve.wait_ge(sq_ready, sqs[0])
                rows = src.shape[0]
                dve.tensor_reduce(small[0:rows, SS + off:SS + off + n], hv(W(SQ, n * dh)[0:rows], n), AX,
                                  ALU.add).then_inc(sq_free, 1)
                offs.append(off)
                off += n
            dve.wait_ge(sq_free, sqs[0])
            for (src, n, dh, *_), o in zip(jobs, offs):
                rows = src.shape[0]
                v = small[0:rows, SS + o:SS + o + n]
                dve.tensor_scalar(v, v, 1.0 / dh, EPS, ALU.mult, ALU.add)
            st.meet()
            if mid:
                mid()
            st.meet()
            done(dve.reciprocal(sm(RR, off), sm(SS, off)))
            table_of = None
            for (src, n, dh, g, scale, rope, where), o in zip(jobs, offs):
                rows = src.shape[0]
                r = small[0:rows, RR + o:RR + o + n]
                src = src if len(src.shape) == 3 else hv(src, n)
                if rope:
                    if table_of != (g, where == "cmp"):
                        table_of = (g, where == "cmp")
                        tab = W(TAB, NT, 2 * dh)
                        gb = gsm[:, g, 0:dh]
                        base = ROPE if dh == DH else ROPE64
                        if where == "cmp":
                            tab, base = W(TAB, 1, 2 * dh), ROPE_C.unsqueeze(1)
                        k, half = tab.shape[1], dh // 2

                        def bb(ap):
                            return ap.unsqueeze(1).broadcast_to([P, k, ap.shape[-1]])

                        dve.tensor_tensor(tab[:, :, 0:dh], base[:, :, 0:dh], bb(gb), ALU.mult)
                        dve.tensor_tensor(tab[:, :, dh:dh + half], base[:, :, dh:dh + half], bb(gb[:, half:dh]),
                                          ALU.mult)
                        done(dve.tensor_tensor(tab[:, :, dh + half:2 * dh], base[:, :, dh + half:2 * dh],
                                               bb(gb[:, 0:half]), ALU.mult))
                        if scale != 1.0:
                            done(dve.tensor_scalar(tab, tab, scale, None, ALU.mult))
                    i = 0 if where == "cmp" else where
                    rotate(src, src, n, dh, tab[0:rows, i, 0:dh], tab[0:rows, i, dh:2 * dh], r, rows)
                else:
                    na = hv(W(TA, n * dh)[0:rows], n)
                    done(dve.scalar_tensor_tensor(out=na, in0=src, scalar=scale,
                                                  in1=r.unsqueeze(2).broadcast_to([rows, n, dh]),
                                                  op0=ALU.mult, op1=ALU.mult))
                    done(dve.tensor_tensor(src, na, gsm[:, g, 0:dh].unsqueeze(1).broadcast_to([rows, n, dh]),
                                           ALU.mult))
            if jobs is J_sub:
                gate_by(Y[:, :, 1024:1536], B_PROJ[:, :, 1536:2048])
            st.meet()

        def gate_by(y, z):
            dve.tensor_tensor(y, y, z, ALU.mult)

        def layer_head(name_mem, gmem, name_k, name_x, gm, name_q, name_a):
            st.meet()
            turn(plan[name_mem])
            factors()
            st.meet()
            gemm(gmem)
            st.meet()
            qk(J_mk)
            turn(plan[name_k])
            turn(plan[name_x])
            factors()
            st.meet()
            gemm(gm)
            st.meet()
            qk(J_mq)
            turn(plan[name_q])
            st.meet()
            attend(plan[name_a])
            gate_by(Y[:, :, 1536:2048], M_PROJ[:, :, 512:1024])

        split(0, 0, 2048)
        split(0, 1, 2048)
        dve.wait_ge(late_in, 64)
        dve.tensor_copy(causal[:], W(SCR, NT, S))
        dve.tensor_copy(identb[:], W(SCR + 1024, P))
        dve.memset(small[:], 0.0)
        st.meet()
        layer_head("mem0", g_memkv[0], "mk0", "x0", g_m[0], "mq0", "am0")
        st.meet()
        gemm(g_b)
        st.meet()

        def zero_halves():
            q4 = BQT.rearrange("p (h i) t -> p h i t", i=2)
            dve.memset(q4[64:P, :, 0], 0.0)
            dve.memset(q4[0:64, :, 1], 0.0)

        def lambdas():
            done(dve.tensor_tensor(LAM[:, 0], LAM[:, 0], LAM[:, 1], ALU.mult))
            done(dve.tensor_tensor(LAM[:, 2], LAM[:, 2], LAM[:, 3], ALU.mult))
            dve.tensor_reduce(sm(LAMC + 2), LAM[:, 0], AX, ALU.add)
            dve.tensor_reduce(sm(LAMC + 3), LAM[:, 2], AX, ALU.add)

        qk(J_b, mid=lambdas, first=zero_halves)
        done(dve.tensor_tensor(sm(LAMC + 4), sm(LAMC + 1), sm(LAMC), ALU.subtract))
        done(dve.tensor_scalar(sm(LAMC + 4), sm(LAMC + 4), -(0.8 - 0.6 * math.exp(0.0)), None, ALU.add))
        turn(plan["bq"])
        turn(plan["bk"])
        st.meet()
        attend(plan["ab"])
        st.meet()
        qk(J_sub)
        gemm(g_a)
        gemm(g_az)
        gemm(g_ag)
        st.meet()
        turn(plan["raw"])
        st.meet()
        tmp = W(SCR, 2, 1024)
        done(dve.memset(tmp, 0.0))
        done(dve.tensor_copy(blk_hi[:, 2048:2048 + P], tmp[:, 0, 0:P]))
        done(dve.tensor_copy(blk_lo[:, 2048:2048 + P], tmp[:, 0, 0:P]))
        for j in range(2):
            t4 = tmp[:, j].rearrange("p (l g c) -> p l g c", l=CMP_LEN, g=2)
            src = AKT[:, 4 + 2 * j:6 + 2 * j]
            for g in range(2):
                w = src[:, g].rearrange("p (c l) -> p l c", l=CMP_STRIDE)
                for h in range(2):
                    e = dve.tensor_tensor(t4[:, 16 * h:16 * h + 16, g, 0:N_CMP], w[:, :, h:h + N_CMP],
                                          PET[:, j, 16 * h:16 * h + 16].unsqueeze(2).broadcast_to([P, 16, N_CMP]),
                                          ALU.add)
            done(e)
            bh, bl = blk_hi[:, j * 1024:(j + 1) * 1024], blk_lo[:, j * 1024:(j + 1) * 1024]
            done(dve.tensor_copy(bh, tmp[:, j]))
            done(dve.tensor_tensor(bl, tmp[:, j], bh.bitcast(F32), ALU.subtract))
        st.meet()
        for n in range(4 * cmp_first, 4 * cmp_first + 8):
            ahead(n)
        st.meet()
        dve.memset(VBD, 0.0)
        st.meet()
        turn(plan["cht"])
        st.meet()
        dve.memset(PC, 0.0)
        st.meet()
        for g in range(2):
            dve.tensor_copy(KCN[0:N_CMP, g], ps[0:N_CMP, g, 0:P])
            dve.tensor_copy(VCR[0:N_CMP, g], ps[0:N_CMP, 2 + g, 0:P])
        st.meet()
        qk(J_a)
        turn(plan["kct"])
        turn(plan["aq"])
        turn(plan["ak"])
        st.meet()
        st.meet()
        VB = W(SCR, NT, 16)
        MX = W(SCR + 32, NT, 8)
        done(dve.tensor_scalar(VB, VIS, -1.0, -MASKED, ALU.add, ALU.mult))
        for t in range(NT):
            pc = PC[:, t].rearrange("p (h c) -> p h c", h=8)[:, :, 0:N_CMP]
            sc = ps[:, t, 0:P].rearrange("p (h c) -> p h c", h=8)[:, :, 0:N_CMP]

            def bh8(ap):
                return ap.unsqueeze(1).broadcast_to([P, 8, N_CMP])

            done(dve.tensor_tensor(pc, sc, bh8(VIS[:, t, 0:N_CMP]), ALU.mult))
            done(dve.tensor_tensor(pc, pc, bh8(VB[:, t, 0:N_CMP]), ALU.add))
            done(dve.tensor_reduce(MX[:, t], pc, AX, ALU.max))
            done(dve.tensor_tensor(pc, pc, MX[:, t].unsqueeze(2).broadcast_to([P, 8, N_CMP]), ALU.subtract))
        st.meet()
        st.meet()
        for t in range(NT):
            pc = PC[:, t].rearrange("p (h c) -> p h c", h=8)
            done(dve.tensor_tensor(pc, pc, VIS[:, t].unsqueeze(1).broadcast_to([P, 8, 16]), ALU.mult))
            done(dve.tensor_reduce(MX[:, t], pc, AX, ALU.add))
            done(dve.tensor_scalar(MX[:, t], MX[:, t], 1e-30, None, ALU.max))
            done(dve.reciprocal(MX[:, t], MX[:, t]))
            done(dve.tensor_tensor(pc, pc, MX[:, t].unsqueeze(2).broadcast_to([P, 8, 16]), ALU.mult))
        st.meet()
        turn(plan["pc"])
        st.meet()
        st.meet()
        for t in range(NT):
            for g in range(2):
                gt = GATE[:, t, 12 * g:12 * g + 12].rearrange("p (r k) -> p r k", k=3)[:, :, 0]
                dve.tensor_tensor(hv(Y[:, t, g * 512:(g + 1) * 512], 4), hv(ps[:, 2 * t + g, :], 4),
                                  gt.unsqueeze(2).broadcast_to([P, 4, P]), ALU.mult)
        st.meet()
        attend(plan["as"])
        gate_by(Y[:, :, 0:1024], A_PROJ[:, :, 2584:3608])
        st.meet()
        turn(plan["y0"])
        st.meet()
        gemm(g_out[0])
        st.meet()
        if stop == "L0":
            return
        layer_head("mem1", g_memkv[1], "mk1", "x1", g_m[1], "mq1", "am1")
        st.meet()
        gemm(g_ci)
        gemm(g_ck)
        gemm(g_c)
        gemm(g_cz)
        st.meet()
        for t in range(NT):
            for h in range(2):
                v = hv(C_PROJ[:, t, 2560 + 512 * h:3072 + 512 * h], 8)
                rotate(v, v, 8, 64, ROPE64[:, t, 0:64], ROPE64[:, t, 64:128])
            for i in range(2):
                rotate(C_PROJ[:, t, 3584:3648].unsqueeze(1), IK2[:, t, 64 * i:64 * i + 64].unsqueeze(1), 1, 64,
                       ROPE64[:, t, 0:64], ROPE64[:, t, 64:128])
        wi = C_PROJ[:, :, 3648:3664]
        done(dve.tensor_scalar(wi, wi, 16 ** -0.5 * 64 ** -0.5, None, ALU.mult))
        dve.memset(IKZ[64:P, 0], 0.0)
        dve.memset(IKZ[0:64, 1], 0.0)
        st.meet()
        turn(plan["iq"])
        turn(plan["ik"])
        st.meet()
        for v in range(16):
            t, b = v // 8, v % 8
            acc = W(SCR + 1024 + 256 * t, S)
            dve.wait_ge(relu_done, v + 1)
            for i in range(2):
                e = dve.scalar_tensor_tensor(
                    out=acc, in0=W(SCR + 512 * (v % 2) + S * i, S), scalar=C_PROJ[:, t, 3648 + 2 * b + i:3649 + 2 * b + i],
                    in1=causal[:, t] if b + i == 0 else acc, op0=ALU.mult, op1=ALU.add)
                if i == 0:
                    done(e)
            e.then_inc(rel_used, 1)
            dve.wait_ge(rel_used, v + 1)
            if b == 7:
                other = W(SCR + 1536, S)
                a, o = acc, other
                for r in range(8):
                    done(dve.max(sm(M8, 8), a))
                    done(dve.match_replace(o, sm(M8, 8), a, TAKEN))
                    a, o = o, a
                done(dve.tensor_scalar(a, a, TAKEN / 2, MASKED, ALU.is_gt, ALU.mult))
                done(dve.tensor_tensor(mask2[:, t], a, causal[:, t], ALU.min))
        st.meet()
        qk(J_c)
        turn(plan["cq"])
        turn(plan["ck"])
        st.meet()
        attend(plan["ac"])
        gate_by(Y[:, :, 0:1536], C_PROJ[:, :, 3664:5200])
        st.meet()
        turn(plan["y1"])
        st.meet()
        gemm(g_out[1])
        st.meet()
        if stop == "L1":
            return
        turn(plan["x2"])
        factors()
        st.meet()
        gemm(g_in2)
        st.meet()
        pf = sm(184, 2)
        done(dve.tensor_copy(pf, posi[:]))
        ang, kk, tmp2 = W(18432, NT, 16), W(18464, NT, 16), W(18496, NT, 16)
        for t in range(NT):
            e = dve.tensor_scalar(ang[:, t], inv2[:], sm(184 + t), None, ALU.mult)
        done(e)
        done(dve.tensor_scalar(kk, ang, 1.0 / (2 * math.pi), 12582912.0, ALU.mult, ALU.add))
        done(dve.tensor_scalar(kk, kk, -12582912.0, None, ALU.add))
        rest = 2 * math.pi
        parts = []
        for bits in (7, 11):
            c = math.floor(rest * 2 ** bits) / 2 ** bits
            if bits == 11:
                c = math.floor(rest * 2 ** 19) / 2 ** 19
            parts.append(c)
            rest -= c
        parts.append(rest)
        for c in parts:
            done(dve.scalar_tensor_tensor(out=ang, in0=kk, scalar=-c, in1=ang, op0=ALU.mult, op1=ALU.add))
        done(dve.tensor_scalar(ANG_R[:, :, 1], ang, math.pi, -math.pi, ALU.min, ALU.max))
        done(dve.tensor_scalar(tmp2, ang, math.pi / 2, None, ALU.is_gt))
        done(dve.scalar_tensor_tensor(out=ang, in0=tmp2, scalar=-2 * math.pi, in1=ang, op0=ALU.mult, op1=ALU.add))
        done(dve.tensor_scalar(ang, ang, math.pi / 2, None, ALU.add))
        done(dve.tensor_scalar(ANG_R[:, :, 0], ang, math.pi, -math.pi, ALU.min, ALU.max))
        st.meet()
        st.meet()
        for b in range(2, 4):
            dve.tensor_copy(MIXT[:, 2 * b:2 * b + 2], ps[:, b, :].rearrange("p (a t) -> p a t", a=2))
        st.meet()
        dve.tensor_copy(mask2[:], W(16896, NT, S))
        st.meet()
        for c in range(8):
            dve.wait_ge(mix_hi, c - c % 2 + 2)
            dve.scalar_tensor_tensor(out=hT_lo[:, c], in0=ps[:, c // 2, (c % 2) * S:(c % 2 + 1) * S],
                                     scalar=sm(176 + c), in1=hT_hi[:, c].bitcast(F32), op0=ALU.mult,
                                     op1=ALU.subtract)
        for t in range(NT):
            v = hv(D_PROJ[:, t, 1024:3072], 16)
            cs = ANG_CS[:, t, 0].unsqueeze(1).broadcast_to([P, 16, 16])
            sn = ANG_CS[:, t, 1].unsqueeze(1).broadcast_to([P, 16, 16])
            x1, x2 = v[:, :, 0:16], v[:, :, 16:32]
            r = [hv(W(18624 + 256 * i, 256), 16) for i in range(4)]
            dve.tensor_tensor(r[0], x1, cs, ALU.mult)
            dve.tensor_tensor(r[1], x2, sn, ALU.mult)
            dve.tensor_tensor(r[2], x2, cs, ALU.mult)
            done(dve.tensor_tensor(r[3], x1, sn, ALU.mult))
            dve.tensor_tensor(x1, r[0], r[1], ALU.subtract)
            done(dve.tensor_tensor(x2, r[2], r[3], ALU.add))
        st.meet()
        turn(plan["dq"])
        turn(plan["dk"])
        st.meet()
        attend(plan["ad"])
        st.meet()
        turn(plan["y2"])
        st.meet()
        gemm(g_out2)
        st.meet()
        if stop == "L2":
            return
        st.meet()
        turn(plan["mem2"])
        factors()
        st.meet()
        gemm(g_xk)
        gemm(g_xv)
        st.meet()
        turn(plan["xk"])
        turn(plan["x3"])
        factors()
        st.meet()
        gemm(g_xq)
        st.meet()
        turn(plan["xq"])
        st.meet()
        attend(plan["ax"])
        st.meet()
        turn(plan["y3"])
        st.meet()
        for j in range(4):
            ahead(4 * co_first + j)
            dve.wait_ge(item_used, 4 * co_first + j + 1)
            for t in range(NT):
                xs = x[:, t, j * 512:(j + 1) * 512]
                e = dve.tensor_tensor(xs, xs, ps[:, 2 * (j % 2) + t, :], ALU.add)
            e.then_inc(evac_dve, 1)
        st.meet()
        if stop == "L3":
            return
        norm(x)
        turn(plan["x4"])
        st.meet()

        def pq_evac(g):
            dve.wait_ge(item_used, 4 * (pq_first + g) + 4)
            dve.tensor_copy(PQT[:, 4 * g + 2:4 * g + 4], ps[:, 2 * (g % 2) + 1, :].rearrange("p (a t) -> p a t", a=2)
                            ).then_inc(evac_dve, 1)

        for g in range(4):
            for j in range(4):
                ahead(4 * (pq_first + g) + j)
                if j == 1 and g > 0:
                    pq_evac(g - 1)
        pq_evac(3)
        st.meet()
        turn(plan["sk"])
        st.meet()
        st.meet()
        for b in range(4, 8):
            dve.tensor_copy(SC[:, b // 4, (b % 4) * 4:(b % 4 + 1) * 4], ps[:, b, :].rearrange("p (a t) -> p a t", a=4))
        st.meet()

        def top16(vals, idx, data, other):
            done(dve.max(vals[:, 0:8], data))
            dve.max_index(idx[:, 0:8], vals[:, 0:8], data)
            done(dve.match_replace(other, vals[:, 0:8], data, TAKEN))
            done(dve.max(vals[:, 8:16], other))
            done(dve.max_index(idx[:, 8:16], vals[:, 8:16], other))

        for t in range(NT):
            for c in range(16):
                top16(V16[:, t, c], I16U[:, 16 * t + c], SC[:, t, c], W(12032, P))
        done(dve.tensor_copy(I16F.rearrange("p t c k -> p (t c) k"), I16U))
        for t in range(NT):
            vv = V16[:, t].rearrange("p (h j) k -> p h j k", j=2)
            done(dve.tensor_tensor(CAND.rearrange("p h (a b) -> p h a b", a=16),
                                   vv[:, :, 0].unsqueeze(3).broadcast_to([P, 8, 16, 16]),
                                   vv[:, :, 1].unsqueeze(2).broadcast_to([P, 8, 16, 16]), ALU.add))
            for h in range(8):
                top16(SC16[:, t, h], CI16U[:, 0, 8 * t + h], CAND[:, h], W(12032, 256))
        done(dve.tensor_scalar(CI16U[:, 1], CI16U[:, 0], 4, None, ALU.logical_shift_right))
        done(dve.tensor_scalar(CI16U[:, 2], CI16U[:, 0], 15, None, ALU.bitwise_and))
        for j in range(2):
            done(dve.tensor_copy(CI16F.rearrange("p t h k -> p (t h) k"), CI16U[:, 1 + j]))
            for t in range(NT):
                ii = I16F[:, t].rearrange("p (h j) k -> p h j k", j=2)[:, :, j]
                pk = PICK.rearrange("p h (a b) -> p h a b", a=16)
                done(dve.tensor_tensor(pk, CI16F[:, t].unsqueeze(3).broadcast_to([P, 8, 16, 16]),
                                       IOTA[:, 0:16].unsqueeze(1).unsqueeze(1).broadcast_to([P, 8, 16, 16]),
                                       ALU.is_equal))
                done(dve.tensor_tensor(pk, pk, ii.unsqueeze(2).broadcast_to([P, 8, 16, 16]), ALU.mult))
                done(dve.tensor_reduce(hv(KEYS[:, t, j], 8), pk, AX, ALU.add))
        for t in range(NT):
            done(dve.tensor_copy(MXK[:, t], SC16[:, t, :, 0]))
            done(dve.tensor_tensor(SC16[:, t], SC16[:, t], MXK[:, t].unsqueeze(2).broadcast_to([P, 8, 16]),
                                   ALU.subtract))
        st.meet()
        st.meet()
        for t in range(NT):
            done(dve.tensor_reduce(MXK[:, t], SC16[:, t], AX, ALU.add))
            done(dve.reciprocal(MXK[:, t], MXK[:, t]))
            done(dve.tensor_tensor(hv(KEYS[:, t, 2], 8), SC16[:, t], MXK[:, t].unsqueeze(2).broadcast_to([P, 8, 16]),
                                   ALU.mult))
        st.meet()
        turn(plan["keys"])
        dve.drain().then_inc(gate_used, 2)
        st.meet()
        for half in range(2):
            gb = half * (S // TG)
            with dve.Fori(0, HALF // RAW) as i:
                for s in range(RAW):
                    split(i + (u_first[half] // 4 + (s + 2) // 4), (s + 2) % 4, 2048)
            st.meet()

            def hots(i, b):
                dve.wait_ge(gate_ready, 2 * i + (gb + b + 1))
                for q in range(TG):
                    tok = 8 * i + (4 * b + q)
                    dve.tensor_scalar(hot_r[:, b, q], IOTA, E1T[:, bass.ds(tok, 1)], None, ALU.is_equal)
                    e = dve.tensor_scalar(HOTV[:, b, q], IOTA[:, half * HALF:(half + 1) * HALF],
                                          E2T[:, bass.ds(tok, 1)], GT[:, bass.ds(tok, 1)], ALU.is_equal, ALU.mult)
                e.then_inc(hv_ready, 1)

            def low(i, b):
                dve.wait_ge(hh_ready, 2 * i + (gb + b + 1))
                dve.tensor_tensor(hot_l[:, b], HOTV[:, b], hot_h[:, b].bitcast(F32), ALU.subtract
                                  ).then_inc(hot_ready, 1)

            def weigh(i, b):
                dve.wait_ge(gate_ready, 2 * i + (gb + b + 3))
                c = CT[:, :, bass.ds(8 * i + 4 * b, TG)]
                dve.tensor_tensor(c, c, ps[:, b, 0:TG * HALF].rearrange("p (t e) -> p e t", t=TG), ALU.mult
                                  ).then_inc(gate_used, 1)

            hots(0, 0)
            low(0, 0)
            hots(0, 1)
            weigh(0, 0)
            low(0, 1)
            with dve.Fori(1, S // TG // 2) as i:
                for b in range(2):
                    hots(i, b)
                    weigh(i + (b - 1), 1 - b)
                    low(i, b)
            weigh(S // TG // 2 - 1, 1)
            st.meet()

            def low_c(i, s):
                dve.wait_ge(c_hi_done, 4 * i + (half * HALF + s + 1))
                dve.tensor_tensor(c_lo[:, s % 2], CT[:, bass.ds(4 * i + s, 1)].rearrange("p a t -> p (a t)"),
                                  c_hi[:, s % 2].bitcast(F32), ALU.subtract).then_inc(c_lo_done, 1)

            low_c(0, 0)

            def v_step(i, s, last):
                if not (last and s == 3):
                    low_c(i + (s + 1) // 4, (s + 1) % 4)
                if not (last and s >= 2 and half == 1):
                    split(i + (v_first[half] // 4 + (s + 2) // 4), (s + 2) % 4, 2048)

            for s in range(RAW):
                v_step(0, s, False)
            with dve.Fori(1, HALF // RAW - 1) as i:
                for s in range(RAW):
                    v_step(i, s, False)
            for s in range(RAW):
                v_step(HALF // RAW - 1, s, True)
            st.meet()
            for b in range(4 if half == 0 else 0, 8):
                y = YT[:, b // 4, (b % 4) * 512:(b % 4 + 1) * 512]
                if half == 0:
                    dve.tensor_copy(y, ps[:, b, :])
                else:
                    dve.tensor_tensor(y, y, ps[:, b, :], ALU.add)
            st.meet()
        turn(plan["fin"])
        st.meet()
        dve.tensor_tensor(FIN, FIN, XD, ALU.add)
        st.meet()
        st.meet()
        dve.tensor_scalar(sm(128, 2), sm(128, 2), 1.0 / D, EPS, ALU.mult, ALU.add)
        st.meet()
        st.meet()
        done(dve.reciprocal(sm(128, 2), sm(130, 2)))
        for t in range(NT):
            e = dve.scalar_tensor_tensor(out=FIN[:, t], in0=FIN[:, t], scalar=sm(128 + t), in1=GFIN,
                                         op0=ALU.mult, op1=ALU.mult)
        e.then_inc(dve_out, 1)


_SHAPES = {}


def kernel(**inputs):
    from concourse import bacc as _bacc
    from concourse.bass_utils import run_bass_kernel_spmd as _run

    c = np.ascontiguousarray
    a = {k: np.asarray(v) for k, v in inputs.items()}
    rows = [a.pop("mem_norm_gain")[None], a.pop("norm_gain")] + [
        a.pop(k) for k in ("g_mix_2", "g_mem_2", "g_cross_2", "g_ffn_2")]
    a["gains"] = c(np.concatenate(rows).reshape(7, KC, P).transpose(2, 0, 1))
    a["pool_scale_2"] = c(a["pool_scale_2"].reshape(8, P).T)
    a["positions_2"] = c(a["positions_2"].reshape(NT, P).T)
    a["pe_t"] = c(a.pop("nsa_cmp_pos")[0].transpose(2, 0, 1))
    a["cmp_w2"] = c(a.pop("nsa_cmp_w2")[0].reshape(2, 2, P, P).transpose(2, 0, 1, 3))
    a["sub_keys"] = c(np.stack([a.pop("sub_keys_1_2")[0], a.pop("sub_keys_2_2")[0]]))
    a["mem"], a["mem_2"] = a["mem"][0], a["mem_2"][0]
    def cut(w):
        rows, width = w.shape
        out_ = []
        for c0 in range(0, width, COLS):
            g = w[:, c0:c0 + COLS]
            out_.append(g.reshape(rows // (4 * P), 4, P, g.shape[1]).transpose(0, 2, 1, 3).reshape(-1))
        return np.concatenate(out_)

    for l in range(2):
        a[f"mem_w_kv.{l}"] = cut(a["mem_w_kv"][l])
        a[f"w_out.{l}"] = cut(a["w_out"][l])
    del a["mem_w_kv"], a["w_out"]
    w = a.pop("even_w_in")[0]
    for c0, c1 in ((EM, EVEN_IN), (EB, EM), (0, 2560), (EA_Z, EB), (EA_G, EA_Z)):
        a[f"even_w.{c0}"] = cut(w[:, c0:c1])
    w = a.pop("odd_w_in")[0]
    for c0, c1 in ((OM, ODD_IN), (OI, OK_IDX), (OK_IDX, OZ), (0, 2560), (OZ, OM)):
        a[f"odd_w.{c0}"] = cut(w[:, c0:c1])
    for k in ("w_in_2", "w_out_2", "w_ck_2", "w_cv_2", "w_cq_2"):
        a[f"{k}.0"] = cut(a.pop(k)[0])
    a["w_co_2"] = cut(a["w_co_2"][0]).reshape(4, P, 2048)
    a["w_pq_2"] = cut(a["w_pq_2"][0]).reshape(4, 4, P, 2048)
    a["cmp_w1"] = c(a.pop("nsa_cmp_w1")[0].reshape(2, 4, 8, P, CMP_HID).transpose(0, 1, 3, 2, 4)).reshape(2, 4, P, 2048)
    a["w_u_t"] = c(a.pop("w_u_2")[0].reshape(E1, E1, KC, P).transpose(1, 3, 2, 0)).reshape(E1, P, KC * E1)
    a.update(CONSTS)

    nc = _bacc.Bacc("TRN2", target_bir_lowering=False, num_devices=1)
    arrays, aps = {}, {}
    for k, v in a.items():
        v = c(v)
        arrays[f"in_{k}"] = v
        aps[k] = nc.dram_tensor(f"in_{k}", v.shape, mybir.dt.from_np(v.dtype), kind="ExternalInput").ap()
    o = nc.dram_tensor("out_0", (1, S, D), F32, kind="ExternalOutput").ap()
    build(nc, aps, o)
    r = _run(nc, [arrays], core_ids=[0])
    return r.results[0]["out_0"]
```

```python
import math
from contextlib import ExitStack

import concourse.bass as bass
from concourse import mybir
import numpy as np

F32 = mybir.dt.float32
F32R = mybir.dt.float32r
BF16 = mybir.dt.bfloat16
I32 = mybir.dt.int32
U32 = mybir.dt.uint32
ALU = mybir.AluOpType
ACT = mybir.ActivationFunctionType
AX = mybir.AxisListType.X

P = 128
D = 2048
S = 256
NT = S // P
KC = D // P
DH = 128
EPS = 1e-6
MASKED = -1e30
TAKEN = -3e38
RAW = 4
COLS = 512
STEP_A, STEP_CI = 432, 368
N_CMP, CMP_STRIDE, CMP_LEN, CMP_HID = 15, 16, 32, 256
E1 = 128

EA_KV, EA_Z, EB, EM, EVEN_IN = 1024, 2584, 3608, 5656, 6680
OI, OZ, OM, ODD_IN = 2560, 3664, 5200, 6224


def tables():
    f = np.float32
    out = {}
    out["ident"] = np.eye(P, dtype=f)
    t = np.arange(S)

    def rot(pos, half, theta):
        inv = (f(theta) ** (-np.arange(half, dtype=f) / f(half))).astype(f)
        ang = pos.astype(f)[:, None] * inv[None, :]
        c, s = np.cos(ang), np.sin(ang)
        return np.concatenate([c, c, -s, s], axis=1).astype(f)

    def tiled(a):
        return np.ascontiguousarray(a.reshape(NT, P, -1).transpose(1, 0, 2))

    out["rope128"] = tiled(rot(t, 64, 10000.0))
    out["rope64"] = tiled(rot(t, 32, 10000.0))
    cmp_last = np.arange(N_CMP) * CMP_STRIDE + CMP_LEN - 1
    rc = np.zeros((P, 256), f)
    rc[:N_CMP] = rot(cmp_last, 64, 10000.0)
    out["rope_cmp"] = rc
    inv2 = (f(500000.0) ** (-np.arange(0, 32, 2, dtype=f) / f(32))).astype(f)
    out["inv2"] = np.tile(inv2[None], (P, 1))
    dist = t[:, None] - t[None, :]
    causal = dist >= 0
    out["causal"] = tiled(np.where(causal, 0.0, MASKED).astype(f))
    vis = np.zeros((S, 16), f)
    vis[:, :N_CMP] = cmp_last[None] <= t[:, None]
    out["cmp_vis"] = tiled(vis)
    count = (causal & (dist <= 128)).astype(f) + (causal & (dist % 4 == 0)) + (causal & (dist % 16 == 0))
    out["dil_count"] = tiled(count.astype(f))
    out["dil_mask"] = tiled(np.where(count > 0, 0.0, MASKED).astype(f))
    pool = np.zeros((S, 4, S), f)
    for g, w in enumerate((2, 4, 8, 16)):
        for i in range(S):
            n = min(i + 1, w)
            pool[i - n + 1:i + 1, g, i] = f(1.0) / f(n)
            pool[i, g, i] -= f(1.0)
    out["pool"] = np.ascontiguousarray(pool.reshape(NT, P, 4, S).transpose(1, 0, 2, 3))
    out["iota"] = np.tile(np.arange(P, dtype=f)[None], (P, 1))
    return out


CONSTS = tables()


class Item:

    def __init__(self, src, shape):
        self.src, self.shape = src, shape
        self.size = int(np.prod(shape))


def build(nc, A, out):
    with ExitStack() as ctx:
        build_in(nc, A, out, ctx)


def build_in(nc, A, out, ctx):
    def sb(name, shape, dt=F32):
        return ctx.enter_context(nc.sbuf_tensor(name, shape, dt))

    def sem(name):
        return ctx.enter_context(nc.semaphore(name))

    ps = ctx.enter_context(nc.psum_tensor("ps", [P, 8, 512], F32))
    x = sb("x", [P, NT, D])
    hT_hi = sb("hT_hi", [P, KC, S], F32R)
    hT_lo = sb("hT_lo", [P, KC, S], F32R)
    raw = sb("raw", [P, RAW, 2048])
    w_hi = sb("w_hi", [P, 2, 2048], F32R)
    w_lo = sb("w_lo", [P, 2, 2048], F32R)
    WORK = 20832
    work = sb("work", [P, WORK])
    ident = sb("ident", [P, P])
    identb = sb("identb", [P, P], BF16)
    causal = sb("causal", [P, NT, S], BF16)
    mask2 = sb("mask2", [P, NT, S], BF16)
    gains = sb("gains", [P, 7, KC])
    small = sb("small", [P, 256])

    def W(off, *shape):
        n = int(np.prod(shape))
        assert off + n <= WORK, (off, shape)
        v = work[:, off:off + n]
        if len(shape) == 2:
            v = v.rearrange("p (a b) -> p a b", a=shape[0])
        elif len(shape) == 3:
            v = v.rearrange("p (a b c) -> p a b c", a=shape[0], b=shape[1])
        return v

    landed = [sem(f"landed{s}") for s in range(RAW)]
    hi_done = sem("hi_done")
    lo_done = sem("lo_done")
    item_used = sem("item_used")
    evac_act = sem("evac_act")
    evac_dve = sem("evac_dve")
    norm_sum = sem("norm_sum")
    norm_var = sem("norm_var")
    norm_sd = sem("norm_sd")
    norm_r = sem("norm_r")
    over = sem("over")
    act_step = sem("act_step")
    dve_step = sem("dve_step")
    sq_ready = sem("sq_ready")
    sq_free = sem("sq_free")
    turn_ready = sem("turn_ready")
    turn_act = sem("turn_act")
    turn_dve = sem("turn_dve")
    s_ready = sem("s_ready")
    m_ready = sem("m_ready")
    p_ready = sem("p_ready")
    a_ready = sem("a_ready")
    t_ready = sem("t_ready")
    pt_ready = sem("pt_ready")
    o_ready = sem("o_ready")
    o_used = sem("o_used")
    rel_ready = sem("rel_ready")
    relu_done = sem("relu_done")
    rel_used = sem("rel_used")
    const_in = sem("const_in")
    mem_in = sem("mem_in")
    late_in = sem("late_in")
    moved = sem("moved")
    x_in = sem("x_in")
    fin_in = sem("fin_in")
    fin_sum = sem("fin_sum")
    fin_var = sem("fin_var")
    fin_sd = sem("fin_sd")
    dve_out = sem("dve_out")
    mix_hi = sem("mix_hi")
    gelu_done = sem("gelu_done")
    key_ready = sem("key_ready")
    key_act = sem("key_act")
    key_dve = sem("key_dve")
    hv_ready = sem("hv_ready")
    rows_ready = sem("rows_ready")
    iota_ready = sem("iota_ready")
    hot_ready = sem("hot_ready")
    flushed = sem("flushed")
    gate_ready = sem("gate_ready")
    gate_used = sem("gate_used")
    c_hi_done = sem("c_hi_done")
    c_lo_done = sem("c_lo_done")
    kv_out = sem("kv_out")
    out_done = sem("out_done")

    items = []
    evacs = [(0, 0)]

    class Gemm:

        def __init__(self, w, c0, c1, dst, step=COLS):
            self.step = step
            self.first = len(items) // 4
            self.dst = dst
            self.widths = []
            self.act0, self.dve0 = evacs[-1]
            self.adds = dst is None
            for c in range(c0, c1, step):
                n = min(step, c1 - c)
                self.widths.append(n)
                evacs.append((evacs[-1][0] + (not self.adds), evacs[-1][1] + 1))
                for j in range(4):
                    at = 4 * KC // 4 * P * c + j * P * 4 * n
                    items.append(Item(w[at:at + P * 4 * n].rearrange("(p x) -> p x", p=P), (4, n)))

    Y = W(0, NT, D)
    M_PROJ = Y[:, :, 0:1024]
    MK, MV = [W(11520, 4, S), W(15520, 4, S)], [W(12544, NT, 512), W(16544, NT, 512)]
    MQT = [W(15616, 4, S), W(14496, 4, S)]
    MKV, MKV1 = W(4096, NT, 512), W(5120, NT, 512)
    MV1, MK1 = W(13568, NT, 512), W(14592, 4, S)
    B_PROJ = W(4096, NT, 2048)
    BQT, BKT = W(8192, 8, S), W(10240, 4, S)
    A_PROJ = W(4096, NT, 3608)
    AQT, AKT = W(11312, 8, S), W(13360, 8, S)
    SCR = 17728
    SQ, TA, TB_ = SCR, SCR + 768, SCR + 1536
    TAB = SCR + 2304
    C_PROJ = W(4096, NT, 5200)
    CQT = W(14496, 12, S)
    IQT, IKZ = W(14496, 8, S), W(16544, 2, S)

    def part(name, k):
        return A[f"{name}.{k}"]

    g_memkv = [None, None]
    g_m = [None, None]
    g_out = [None, None]
    g_memkv[0] = Gemm(part("mem_w_kv", 0), 0, 1024, ("split2", MKV, MV[0]))
    g_memkv[1] = Gemm(part("mem_w_kv", 1), 0, 1024, ("split2", MKV1, MV1))
    g_m[0] = Gemm(part("even_w", EM), 0, EVEN_IN - EM, M_PROJ)
    g_b = Gemm(part("even_w", EB), 0, EM - EB, B_PROJ)
    g_a = Gemm(part("even_w", 0), 0, EA_Z, A_PROJ, STEP_A)
    g_az = Gemm(part("even_w", EA_Z), 0, EB - EA_Z, A_PROJ[:, :, EA_Z:EB])
    cmp_first = len(items) // 4
    for j in range(2):
        for q in range(4):
            items.append(Item(A["cmp_w1"][j, q], (8, CMP_HID)))
    g_out[0] = Gemm(part("w_out", 0), 0, D, None)
    g_m[1] = Gemm(part("odd_w", OM), 0, ODD_IN - OM, M_PROJ)
    g_ci = Gemm(part("odd_w", OI), 0, OZ - OI, C_PROJ[:, :, OI:OZ], STEP_CI)
    g_c = Gemm(part("odd_w", 0), 0, OI, C_PROJ)
    g_cz = Gemm(part("odd_w", OZ), 0, OM - OZ, C_PROJ[:, :, OZ:OM])
    g_out[1] = Gemm(part("w_out", 1), 0, D, None)
    D_PROJ = W(4096, NT, 4096)
    g_in2 = Gemm(part("w_in_2", 0), 0, 4096, D_PROJ)
    g_out2 = Gemm(part("w_out_2", 0), 0, D, None)
    XKV = W(4096, NT, 1024)
    XQ = W(6144, NT, 512)
    MIXT, WPOOL, POOLM = W(12288, 8, S), W(14336, 8, S), W(16384, 8, S)
    COUNT = W(16384, NT, S)
    XQT, XKT = W(8192, 4, S), W(9216, 4, S)
    g_xk = Gemm(part("w_ck_2", 0), 0, 512, XKV[:, :, 0:512])
    g_xv = Gemm(part("w_cv_2", 0), 0, 512, XKV[:, :, 512:1024])
    g_xq = Gemm(part("w_cq_2", 0), 0, 512, XQ)
    co_first = len(items) // 4
    co_dve0 = evacs[-1][1]
    evacs.append((evacs[-1][0], evacs[-1][1] + 4))
    for j in range(4):
        items.append(Item(A["w_co_2"][j], (4, 512)))
    pq_first = len(items) // 4
    pq_act0, pq_dve0 = evacs[-1]
    evacs.append((evacs[-1][0] + 4, evacs[-1][1] + 4))
    for g in range(4):
        for j in range(4):
            items.append(Item(A["w_pq_2"][g, j], (4, 512)))
    n_static = len(items)
    QTR = 32
    PARTS = E1 // QTR
    order = [("U", 0), ("U", 1)]
    for q in range(PARTS):
        order.append(("V", q))
        if q + 2 < PARTS:
            order.append(("U", q + 2))
    u_first = [n_static + QTR * order.index(("U", q)) for q in range(PARTS)]
    v_first = [n_static + QTR * order.index(("V", q)) for q in range(PARTS)]

    turn_counts = [(0, 0)]

    class Turn:

        def __init__(self, blocks, split=False, dve_only=False):
            self.first, self.blocks, self.split = len(turn_counts) - 1, blocks, split
            for b, (_, outs) in enumerate(blocks):
                a, d = turn_counts[-1]
                n = len(outs)
                if split:
                    turn_counts.append((a + n, d + n))
                elif (self.first + b) % 2 == 0 and not dve_only:
                    turn_counts.append((a + n, d))
                else:
                    turn_counts.append((a, d + n))

    def head_turn(srcs, dst, scale=None):
        blocks = []
        for h in range(0, len(srcs), 2):
            n = min(2, len(srcs) - h)
            blocks.append(([srcs[h + i][:, t] for i in range(n) for t in range(NT)],
                           [(dst[:, h:h + n], (0, P), (0, n * S), scale)]))
        return Turn(blocks)

    def row_turn(src, gain, chunks=KC, at=0):
        blocks = []
        for k in range(0, chunks, 2):
            blocks.append(([src[:, t, (k + i) * P:(k + i + 1) * P] for i in range(2) for t in range(NT)],
                           [(hT_hi[:, at + k + i], hT_lo[:, at + k + i], (i * S, (i + 1) * S),
                             gains[:, gain, k + i:k + i + 1] if gain is not None else None) for i in range(2)]))
        return Turn(blocks, split=True)

    units = []

    class Attention:

        def __init__(self, us, aside=False):
            self.aside = aside
            self.first, self.units = len(units), us
            units.extend(us)
            self.depth = 1 if aside else 2
            for n, u in enumerate(us, self.first):
                u["bank"], u["banks"] = (4 + n % 2, 2) if aside else ((4, 5, 2, 3)[n % 4], 4)

    PB = W(SCR, 2, 2, S)
    PTB = W(SCR + 1024, 2, 4, P)

    def heads_of(t, c0, n, dh=DH):
        return [t[:, :, c0 + h * dh:c0 + (h + 1) * dh] for h in range(n)]

    def plain_units(n_heads, qT, kT, vs, dst, mask=None, causal_keys=False, kind="plain", gate=None):
        us = []
        for t in range(NT):
            for h in range(0, n_heads, 2):
                us.append(dict(tile=t, nk=(t + 1) if causal_keys else NT, kind=kind,
                               q=[qT(h + i)[:, t * P:(t + 1) * P] for i in range(2)],
                               k=[kT(h + i) for i in range(2)],
                               v=[vs(h + i) for i in range(2)], mask=mask,
                               dst=dst(t, h), gate=None if gate is None else gate(t, h)))
        return us

    G_MEM, G_X0, G_X1, G_MIX, G_MEM2, G_CROSS, G_FFN = range(7)

    plan = {}
    plan["mem0"] = row_turn(Y, G_MEM)
    plan["mk0"] = head_turn(heads_of(MKV, 0, 4), MK[0])
    plan["mk1"] = head_turn(heads_of(MKV1, 0, 4), MK1)
    plan["x0"] = row_turn(x, G_X0)
    plan["mq0"] = head_turn(heads_of(M_PROJ, 0, 4), MQT[0])

    def mem_units(l):
        return plain_units(4, lambda h: MQT[l][:, h], lambda h: MK[l][:, h],
                           lambda h: (lambda c_: MV[l][:, c_, h * DH:(h + 1) * DH]),
                           lambda t, h: Y[:, t, 1536 + h * DH:1536 + (h + 2) * DH])

    plan["am0"] = Attention(mem_units(0), aside=True)

    def b_blocks():
        blocks = []
        for h in range(4):
            src = [B_PROJ[:, t, h * P:(h + 1) * P] for t in range(NT)]
            blocks.append((src, [(BQT[0:64, 2 * h], (0, 64), (0, S), None),
                                 (BQT[64:P, 2 * h + 1], (64, P), (0, S), None)]))
        return blocks

    plan["bq"] = Turn(b_blocks())
    plan["bk"] = head_turn([B_PROJ[:, :, 512 + h * P:512 + (h + 1) * P] for h in range(4)], BKT)
    bu = []
    for t in range(NT):
        for h in range(4):
            bu.append(dict(tile=t, nk=t + 1, kind="diff", q=[BQT[:, 2 * h + i, t * P:(t + 1) * P] for i in range(2)],
                           k=[BKT[:, h], BKT[:, h]],
                           v=[(lambda c_, h=h: B_PROJ[:, c_, 1024 + h * DH:1024 + (h + 1) * DH])],
                           mask=causal, dst=Y[:, t, 1024 + h * DH:1024 + (h + 1) * DH], gate=None))
    plan["ab"] = Attention(bu)
    plan["raw"] = head_turn(heads_of(A_PROJ, EA_KV, 4), AKT[:, 4:8])
    VBD = W(15408, 512)
    KCT = W(15920, 2, 16)
    GATE = W(15952, NT, 24)
    CHT = W(16000, 2, 2, 32)
    KCN = W(16128, 2, P)
    VCR = W(16384, 2, P)
    W2 = W(16640, 2, 2, P)
    PET = W(17152, 2, CMP_LEN)
    PC, PCT = W(17216, NT, P), W(17472, NT, P)
    ROPE_C = W(20544, 256)
    VIS = W(20800, NT, 16)
    blk_hi = hT_hi[:].rearrange("p k t -> p (k t)")
    blk_lo = hT_lo[:].rearrange("p k t -> p (k t)")
    CH = W(17216, 2, CMP_HID)
    plan["cht"] = Turn([([CH[0:32, j, c * P:(c + 1) * P] for c in range(2)],
                         [(CHT[:, j, c], (0, P), (c * P, c * P + 32), None) for c in range(2)]) for j in range(2)])
    plan["kct"] = Turn([([KCN[0:N_CMP, g] for g in range(2)], [(KCT[:, g, 0:N_CMP], (0, P), (g * P, g * P + N_CMP), None)
                                                             for g in range(2)])])
    plan["aq"] = head_turn(heads_of(A_PROJ, 0, 8), AQT)
    plan["ak"] = head_turn(heads_of(A_PROJ, EA_KV + 512, 2) + heads_of(A_PROJ, EA_KV + 1024, 2), AKT[:, 0:4])
    plan["pc"] = Turn([([PC[:, t] for t in range(NT)], [(PCT, (0, P), (0, S), None)])])

    def nsa_units(kv, comp):
        return plain_units(8, lambda h: AQT[:, h], lambda h: AKT[:, 2 * kv + h // 4],
                           lambda h: (lambda c_: A_PROJ[:, c_, EA_KV + 768 + 512 * kv + (h // 4) * DH:
                                                        EA_KV + 768 + 512 * kv + (h // 4 + 1) * DH]),
                           lambda t, h: Y[:, t, h * DH:(h + 2) * DH], mask=causal, causal_keys=True, kind="gated",
                           gate=lambda t, h: [GATE[:, t, 3 * (h + i) + comp:3 * (h + i) + comp + 1] for i in range(2)])

    plan["as"] = Attention(nsa_units(0, 1) + nsa_units(1, 2))
    plan["y0"] = row_turn(Y, None)
    plan["x1"] = row_turn(x, G_X1)
    plan["mq1"] = head_turn(heads_of(M_PROJ, 0, 4), MQT[1])
    plan["am1"] = Attention(mem_units(1), aside=True)
    plan["iq"] = head_turn([C_PROJ[:, :, 2560 + h * P:2560 + (h + 1) * P] for h in range(8)], IQT)
    IK2 = W(17056, NT, P)
    plan["ik"] = Turn([([IK2[:, t] for t in range(NT)],
                        [(IKZ[0:64, 0], (0, 64), (0, S), None), (IKZ[64:P, 1], (64, P), (0, S), None)])])
    plan["cq"] = head_turn(heads_of(C_PROJ, 0, 12), CQT)
    KT_ = C_PROJ[:, :, 2560:3584]
    CKT = [KT_[:, h // 2, (h % 2) * 512:(h % 2) * 512 + S] for h in range(4)]
    plan["ck"] = Turn([([C_PROJ[:, t, 1536 + h * DH:1536 + (h + 1) * DH] for t in range(NT)],
                        [(CKT[h], (0, P), (0, S), None)]) for h in range(4)])
    plan["ac"] = Attention(plain_units(
        12, lambda h: CQT[:, h], lambda h: CKT[h // 3],
        lambda h: (lambda c_: C_PROJ[:, c_, 2048 + (h // 3) * DH:2048 + (h // 3 + 1) * DH]),
        lambda t, h: Y[:, t, h * DH:(h + 2) * DH], mask=mask2, causal_keys=True))
    plan["y1"] = row_turn(Y, None)
    plan["x2"] = row_turn(x, G_MIX)
    DQT, DKT = W(12288, 8, S), W(14336, 8, S)
    plan["dq"] = head_turn(heads_of(D_PROJ, 1024, 8), DQT, DH ** -0.5)
    plan["dk"] = head_turn(heads_of(D_PROJ, 2048, 8), DKT)
    plan["ad"] = Attention(plain_units(
        8, lambda h: DQT[:, h], lambda h: DKT[:, h],
        lambda h: (lambda c_: D_PROJ[:, c_, 3072 + h * DH:3072 + (h + 1) * DH]),
        lambda t, h: Y[:, t, h * DH:(h + 2) * DH], mask=mask2, causal_keys=True, kind="dilated"))
    plan["y2"] = row_turn(Y, None, chunks=8, at=8)
    plan["mem2"] = row_turn(Y, G_MEM2)
    plan["xk"] = head_turn(heads_of(XKV, 0, 4), XKT)
    plan["x3"] = row_turn(x, G_CROSS)
    plan["xq"] = head_turn(heads_of(XQ, 0, 4), XQT, DH ** -0.5)
    plan["ax"] = Attention(plain_units(
        4, lambda h: XQT[:, h], lambda h: XKT[:, h],
        lambda h: (lambda c_: XKV[:, c_, 512 + h * DH:512 + (h + 1) * DH]),
        lambda t, h: Y[:, t, h * DH:(h + 2) * DH]))
    plan["y3"] = row_turn(Y, None, chunks=4)
    plan["x4"] = row_turn(Y, G_FFN)
    TG = 8
    STEPS = S // TG
    CTS = [W(QTR * S * q, QTR, S) for q in range(2)]
    E1T = W(19936, S)
    E2T = W(20192, S)
    GT = W(20448, S)
    IOTA = W(20704, P)

    def WB(off, *shape):
        return W(off, int(np.prod(shape)) // 2).bitcast(BF16)

    hot_r = WB(16384, 2, TG, P).rearrange("p (b t r) -> p b t r", b=2, t=TG)
    hot_e = WB(17408, 2, TG, QTR).rearrange("p (b t e) -> p b t e", b=2, t=TG)
    hot_g = WB(17664, 2, 3, TG, QTR).rearrange("p (b n t e) -> p b n t e", b=2, n=3, t=TG)
    GATES = WB(18432, 3, S).rearrange("p (n t) -> p n t", n=3)
    E1B, E2B, IOTA_B = WB(18816, S), WB(18944, S), WB(19072, P)
    REST = W(19136, 2, S)
    PQT = W(0, KC, S)
    SKT = W(4096, 2, P)
    SC = W(8192, NT, 16, P)
    V16 = W(12288, NT, 16, 16)
    I16F = W(12800, NT, 16, 16)
    CAND = W(13312, 8, 256)
    SC16 = W(15360, NT, 8, 16)
    CI16F = W(15616, NT, 8, 16)
    OTHER = 18432
    PICK = W(8192, 8, 256)
    KEYS = W(16128, NT, 3, P)
    SKN = W(16896, 2, P)
    MXK = W(16896, NT, 8)
    I16U = W(17152, NT * 16, 16).bitcast(U32)
    CI16U = W(17664, 3, NT * 8, 16).bitcast(U32)
    plan["sk"] = Turn([([SKN[:, j] for j in range(2)], [(SKT, (0, P), (0, 2 * P), None)])])
    plan["keys"] = Turn([([KEYS[:, t, 0] for t in range(NT)] + [KEYS[:, t, 1] for t in range(NT)],
                          [(W(19936, 2 * S), (0, P), (0, 2 * S), None)]),
                         ([KEYS[:, t, 2] for t in range(NT)], [(GT, (0, P), (0, S), None)])])
    c_hi = sb("c_hi", [P, 2, S], F32R)
    c_lo = sb("c_lo", [P, 2, S], F32R)
    YT = x
    x_dram = nc.dram_tensor("x_kept", (NT, P, D), F32, kind="Internal").ap()
    mk_kept = nc.dram_tensor("mk_kept", (P, 4, S), F32, kind="Internal").ap()
    mv_kept = nc.dram_tensor("mv_kept", (P, NT, 512), F32, kind="Internal").ap()
    FIN = W(0, NT, D)
    plan["fin"] = Turn([([YT[:, k // 8, (k % 8) * S + t * P:(k % 8) * S + (t + 1) * P] for k in range(b * 4, b * 4 + 4)],
                         [(FIN[:, t, b * 512:(b + 1) * 512], (0, P), (0, 512), None)])
                        for t in range(NT) for b in range(4)], dve_only=True)

    gsm = sb("gsm", [P, 4, P])
    LAM = W(11264, 4, 64)
    XD = W(4096, NT, D)
    GFIN = W(16384, D)
    posi = sb("posi", [P, NT], I32)
    inv2 = sb("inv2", [P, 16])

    block = ctx.enter_context(nc.Block())

    @block.sync
    def _(sp):
        for t in range(NT):
            sp.dma_start(Y[:, t], A["mem"][t * P:(t + 1) * P]).then_inc(mem_in, 16)
        for n in range(n_static):
            it = items[n]
            if n >= RAW:
                sp.wait_ge(lo_done, n - RAW + 1)
            dst = raw[:, n % RAW, 0:it.size]
            sp.dma_start(dst, it.src).then_inc(landed[n % RAW], 16)
            if n == RAW - 1:
                for t in range(NT):
                    sp.dma_start(x[:, t], A["x"][0, t * P:(t + 1) * P]).then_inc(x_in, 16)
        uu = A["w_u_t"]
        vv = A["w_v_2"][0].rearrange("(r c) d -> c r d", c=E1)
        for n, (what, q) in enumerate(order):
            base, src = n_static + QTR * n, uu if what == "U" else vv
            with sp.Fori(0, QTR // RAW) as i:
                for s in range(RAW):
                    sp.wait_ge(lo_done, 4 * i + (base + s - RAW + 1))
                    sp.dma_start(raw[:, s], src[bass.ds(4 * i + (q * QTR + s), 1)].rearrange("a p c -> p (a c)")
                                 ).then_inc(landed[s], 16)

    AT_MEM_ROOTS, AT_MEM_HEADS, AT_MEM_TURN, AT_MEM = 2, 3, 5, 7
    AT_A_SQUARES, AT_A_ROOTS, AT_A_HEADS = 1, 6, 7
    AT_ANGLES, AT_POOL, AT_POOLED, AT_DQ, AT_DK = 6, 10, 14, 18, 26
    AT_ROPE, AT_TURN, AT_SCORES, AT_SQUARES, AT_ROOTS, AT_HEADS = 14, 18, 21, 33, 36, 37

    class Steps:

        def __init__(self, eng, s):
            self.eng, self.s, self.n, self.phase = eng, s, 0, 0
            self.sq = 0

        def done(self, ins):
            self.n += 1
            ins.then_inc(self.s, 1)
            self.eng.wait_ge(self.s, self.n)

        def meet(self):
            self.arrive()
            self.wait_all()

        def arrive(self):
            self.phase += 1
            self.eng.drain().then_inc(over, 1)

        def wait_all(self):
            self.eng.wait_ge(over, 3 * self.phase)

        def begin(self, g):
            self.slot, self.base = -1, 4 * g.first

        def until(self, slot):
            while self.slot < slot:
                yield

        def meet_at(self, slot):
            self.arrive()
            yield from self.until(slot)
            self.wait_all()

        def side(self, program, n):
            if program is not None:
                self.slot = n - self.base
                next(program, None)

        def rest(self, program):
            self.slot = 10 ** 6
            for _ in program:
                pass

    @block.tensor
    def _(pe):
        st = Steps(pe, None)

        def gemm(g, side=None):
            n_full = sum(w == g.step for w in g.widths)

            def group(i, q, width):
                par = (g.first + q) % 2
                for j in range(4):
                    pe.wait_ge(lo_done, 4 * i + (4 * g.first + j + 1))
                    n = 4 * g.first + j
                    for k in range(4):
                        c = 4 * j + k
                        for t in range(NT):
                            o = ps[:, 2 * par + t, 0:width]
                            hi, lo = hT_hi[:, c, t * P:(t + 1) * P], hT_lo[:, c, t * P:(t + 1) * P]
                            wh = w_hi[:, j % 2, k * width:(k + 1) * width]
                            wl = w_lo[:, j % 2, k * width:(k + 1) * width]
                            pe.matmul(o, hi, wh, start=(c == 0), stop=False)
                            pe.matmul(o, hi, wl, start=False, stop=False)
                            mm = pe.matmul(o, lo, wh, start=False, stop=(c == KC - 1))
                    mm.then_inc(item_used, 1)
                    if side is not None:
                        st.side(side, 4 * (g.first + i) + j)

            def emptied(i):
                if not isinstance(i, int) or g.dve0 + i - 1 > 0:
                    if not g.adds:
                        pe.wait_ge(evac_act, i + (g.act0 - 1))
                    pe.wait_ge(evac_dve, i + (g.dve0 - 1))

            pairs = n_full // 2 if n_full >= 4 and side is None else 0
            if pairs:
                first = 0
                if g.dve0 < 3:
                    first = 1
                    for i in range(2):
                        emptied(i)
                        group(i, i, g.step)
                with pe.Fori(first, pairs) as r:
                    for q in range(2):
                        emptied(2 * r + q)
                        group(2 * r + q, q, g.step)
            for i in range(2 * pairs, len(g.widths)):
                emptied(i)
                group(i, i, g.widths[i])

        def turn(T):
            for _ in turn_steps(T):
                pass

        def turn_steps(T):
            for b, (srcs, outs) in enumerate(T.blocks):
                n = T.first + b
                if n >= 4:
                    a, d = turn_counts[n - 3]
                    if a:
                        pe.wait_ge(turn_act, a)
                    if d:
                        pe.wait_ge(turn_dve, d)
                for i, s in enumerate(srcs):
                    rows, w = s.shape[0], s.shape[-1]
                    mm = pe.transpose(ps[0:w, 4 + n % 4, i * P:i * P + rows], s, ident[0:rows, 0:rows])
                mm.then_inc(turn_ready, 1)
                if b % 2 == 1:
                    yield

        def scores(n):
            u = units[n]
            w = u["nk"] * P
            if n >= u["banks"]:
                pe.wait_ge(p_ready, n - u["banks"] + 1)
            for i in range(2):
                o = ps[:, u["bank"], i * w:(i + 1) * w]
                if u["mask"] is not None:
                    pe.matmul(o, identb[:], u["mask"][:, u["tile"], 0:w], start=(i == 0), stop=False,
                              skip_group_check=True)
                    mm = pe.matmul(o, u["q"][i], u["k"][i][:, 0:w], start=False, stop=True, skip_group_check=True)
                else:
                    mm = pe.matmul(o, u["q"][i], u["k"][i][:, 0:w], start=(i == 0), stop=True,
                                   skip_group_check=True)
            mm.then_inc(s_ready, 1)

        reworked = [0]

        def attend(T):
            for _ in attend_steps(T):
                pass

        def attend_steps(T):
            N = len(T.units)
            for d in range(T.depth):
                scores(T.first + d)
            if T.aside:
                yield
            for r in range(N + 1):
                n = T.first + r
                if r + T.depth < N:
                    scores(n + T.depth)
                if r < N:
                    u = units[n]
                    if u["kind"] in ("diff", "dilated"):
                        reworked[0] += 1
                        pe.wait_ge(a_ready, reworked[0])
                    else:
                        pe.wait_ge(p_ready, n + 1)
                    pt = 6 if T.aside else 6 + n % 2
                    if n >= (1 if T.aside else 2):
                        pe.wait_ge(pt_ready, n if T.aside else n - 1)
                    m = 0
                    for i in range(len(u["v"])):
                        for c in range(u["nk"]):
                            mm = pe.transpose(ps[:, pt, m * P:(m + 1) * P],
                                              PB[:, n % 2, i, c * P:(c + 1) * P], ident[:])
                            m += 1
                    mm.then_inc(t_ready, 1)
                if r >= 1:
                    n -= 1
                    u = units[n]
                    pe.wait_ge(pt_ready, n + 1)
                    if n >= (1 if T.aside else 2):
                        pe.wait_ge(o_used, n if T.aside else n - 1)
                    for i in range(len(u["v"])):
                        o = ps[:, 7 if T.aside else n % 2, i * P:(i + 1) * P]
                        for c in range(u["nk"]):
                            mm = pe.matmul(o, PTB[:, n % 2, i * u["nk"] + c], u["v"][i](c),
                                           start=(c == 0), stop=(c == u["nk"] - 1))
                    mm.then_inc(o_ready, 1)
                yield

        def layer_head(name_x, gm):
            turn(plan[name_x])
            st.meet()
            gemm(gm)
            st.meet()

        def memory_side(l):
            yield
            yield from st.meet_at(AT_MEM_ROOTS)
            yield from st.meet_at(AT_MEM_HEADS)
            yield from st.meet_at(AT_MEM_TURN)
            yield from turn_steps(plan[f"mq{l}"])
            yield from st.meet_at(AT_MEM)
            yield from attend_steps(plan[f"am{l}"])

        def qk_phases():
            for _ in range(3):
                st.meet()

        def cmp_gemm():
            for j in range(2):
                for q in range(4):
                    n = 4 * cmp_first + 4 * j + q
                    pe.wait_ge(lo_done, n + 1)
                    for l in range(8):
                        o = ps[:, j, 0:CMP_HID]
                        a = j * 1024 + (8 * q + l) * 32
                        hi, lo = blk_hi[:, a:a + P], blk_lo[:, a:a + P]
                        wh = w_hi[:, n % 2, l * CMP_HID:(l + 1) * CMP_HID]
                        wl = w_lo[:, n % 2, l * CMP_HID:(l + 1) * CMP_HID]
                        first, last = q + l == 0, q == 3 and l == 7
                        pe.matmul(o, hi, wh, start=first, stop=False)
                        pe.matmul(o, hi, wl, start=False, stop=False)
                        mm = pe.matmul(o, lo, wh, start=False, stop=last)
                    mm.then_inc(item_used, 1)

        def nsa_side():
            yield from st.meet_at(AT_A_SQUARES)
            yield from st.until(AT_A_ROOTS - 1)
            yield from st.meet_at(AT_A_ROOTS)
            yield from st.meet_at(AT_A_HEADS)

        def pool_side():
            yield from st.until(AT_ANGLES - 1)
            yield from st.meet_at(AT_ANGLES)
            yield from st.until(AT_POOL - 1)
            yield from st.meet_at(AT_POOL)
            for c in range(8):
                for s in range(NT):
                    pe.matmul(ps[:, 4 + c // 2, (c % 2) * S:(c % 2 + 1) * S], D_PROJ[:, s, c * P:(c + 1) * P],
                              POOLM[:, 4 * s + c // 2], start=(s == 0), stop=(s == NT - 1))
                if c % 2 == 1 and c < 7:
                    yield
            yield from st.meet_at(AT_POOLED)
            yield from st.until(AT_DQ - 1)
            yield from st.meet_at(AT_DQ)
            yield from st.until(AT_DK - 1)
            yield from st.meet_at(AT_DK)

        def index_side():
            yield from memory_side(1)
            yield from st.until(AT_ROPE - 1)
            yield from st.meet_at(AT_ROPE)
            yield from st.until(AT_TURN - 1)
            yield from st.meet_at(AT_TURN)
            yield from turn_steps(plan["iq"])
            yield from turn_steps(plan["ik"])
            yield from st.meet_at(AT_SCORES)
            for v in range(16):
                t, b = v // 8, v % 8
                if v >= 2:
                    pe.wait_ge(relu_done, v - 1)
                for i in range(2):
                    mm = pe.matmul(ps[:, 4 + v % 2, i * S:(i + 1) * S], IQT[:, b, t * P:(t + 1) * P], IKZ[:, i],
                                   start=(i == 0), stop=True, skip_group_check=True)
                mm.then_inc(rel_ready, 1)
                if v % 2 == 1:
                    yield
            yield from st.until(AT_SQUARES - 1)
            yield from st.meet_at(AT_SQUARES)
            yield from st.until(AT_ROOTS - 1)
            yield from st.meet_at(AT_ROOTS)
            yield from st.meet_at(AT_HEADS)

        st.meet()
        turn(plan["mem0"])
        st.meet()
        gemm(g_memkv[0])
        gemm(g_memkv[1])
        st.meet()
        qk_phases()
        turn(plan["mk0"])
        turn(plan["mk1"])
        layer_head("x0", g_m[0])
        side = memory_side(0)
        st.begin(g_b)
        gemm(g_b, side)
        st.rest(side)
        st.meet()
        qk_phases()
        turn(plan["bq"])
        turn(plan["bk"])
        st.meet()
        attend(plan["ab"])
        st.meet()
        qk_phases()
        gemm(g_a)
        side = nsa_side()
        st.begin(g_az)
        gemm(g_az, side)
        st.meet()
        turn(plan["raw"])
        st.meet()
        st.meet()
        cmp_gemm()
        st.meet()
        st.meet()
        turn(plan["cht"])
        st.meet()
        for j in range(2):
            for g in range(2):
                for c in range(2):
                    pe.matmul(ps[0:N_CMP, 2 * j + g, 0:P], CHT[:, j, c, g * 16:g * 16 + N_CMP], W2[:, j, c],
                              start=(c == 0), stop=(c == 1))
        st.meet()
        st.meet()
        qk_phases()
        turn(plan["kct"])
        turn(plan["aq"])
        turn(plan["ak"])
        st.meet()
        for t in range(NT):
            for h in range(8):
                pe.matmul(ps[:, t, h * 16:h * 16 + N_CMP], AQT[:, h, t * P:(t + 1) * P], KCT[:, h // 4, 0:N_CMP],
                          start=True, stop=True)
        st.meet()
        st.meet()
        st.meet()
        st.meet()
        turn(plan["pc"])
        st.meet()
        for t in range(NT):
            for g in range(2):
                pe.matmul(ps[:, 2 * t + g, :], PCT[64 * g:64 * g + 64, t], VBD[64 * g:64 * g + 64, :],
                          start=True, stop=True)
        st.meet()
        st.meet()
        attend(plan["as"])
        st.meet()
        turn(plan["y0"])
        st.meet()
        gemm(g_out[0])
        st.meet()
        layer_head("x1", g_m[1])
        side = index_side()
        st.begin(g_ci)
        gemm(g_ci, side)
        gemm(g_c, side)
        gemm(g_cz, side)
        st.meet()
        st.rest(side)
        st.meet()
        turn(plan["cq"])
        turn(plan["ck"])
        st.meet()
        attend(plan["ac"])
        st.meet()
        turn(plan["y1"])
        st.meet()
        gemm(g_out[1])
        st.meet()
        turn(plan["x2"])
        st.meet()
        side = pool_side()
        st.begin(g_in2)
        gemm(g_in2, side)
        st.rest(side)
        st.meet()
        for g in range(4):
            for e in range(2):
                for c in range(2):
                    pe.matmul(ps[:, g, e * S:(e + 1) * S], WPOOL[:, 2 * g + c, e * P:(e + 1) * P], MIXT[:, 2 * g + c],
                              start=(c == 0), stop=(c == 1))
        st.meet()
        st.meet()
        turn(plan["dq"])
        turn(plan["dk"])
        st.meet()
        attend(plan["ad"])
        st.meet()
        turn(plan["y2"])
        st.meet()
        gemm(g_out2)
        st.meet()
        turn(plan["mem2"])
        st.meet()
        gemm(g_xk)
        gemm(g_xv)
        st.meet()
        turn(plan["xk"])
        turn(plan["x3"])
        st.meet()
        gemm(g_xq)
        st.meet()
        turn(plan["xq"])
        st.meet()
        attend(plan["ax"])
        st.meet()
        turn(plan["y3"])
        st.meet()
        for j in range(4):
            n = 4 * co_first + j
            pe.wait_ge(lo_done, n + 1)
            for t in range(NT):
                o = ps[:, 2 * (j % 2) + t, :]
                if j >= 2 and t == 0:
                    pe.wait_ge(evac_dve, co_dve0 + j - 1)
                for k in range(4):
                    hi, lo = hT_hi[:, k, t * P:(t + 1) * P], hT_lo[:, k, t * P:(t + 1) * P]
                    wh, wl = w_hi[:, n % 2, k * 512:(k + 1) * 512], w_lo[:, n % 2, k * 512:(k + 1) * 512]
                    pe.matmul(o, hi, wh, start=(k == 0), stop=False)
                    pe.matmul(o, hi, wl, start=False, stop=False)
                    mm = pe.matmul(o, lo, wh, start=False, stop=(k == 3))
            mm.then_inc(item_used, 1)
        st.meet()
        st.meet()
        turn(plan["x4"])
        turn(plan["sk"])
        st.meet()

        def key_scores(g):
            pe.wait_ge(evac_act, pq_act0 + g + 1)
            pe.wait_ge(evac_dve, pq_dve0 + g + 1)
            if g >= 2:
                pe.wait_ge(key_act, g - 1)
                pe.wait_ge(key_dve, g - 1)
            for t in range(NT):
                for i in range(4):
                    c = 4 * g + i
                    mm = pe.matmul(ps[:, 4 + (2 * g + t) % 4, i * P:(i + 1) * P], PQT[:, c, t * P:(t + 1) * P],
                                   SKT[:, c % 2], start=True, stop=True)
                mm.then_inc(key_ready, 1)

        for g in range(4):
            if g >= 2:
                pe.wait_ge(evac_act, pq_act0 + g - 1)
                pe.wait_ge(evac_dve, pq_dve0 + g - 1)
            for j in range(4):
                n = 4 * (pq_first + g) + j
                pe.wait_ge(lo_done, n + 1)
                for k in range(4):
                    for c in range(4):
                        o = ps[:, 2 * (g % 2) + c // 2, (c % 2) * S:(c % 2 + 1) * S]
                        a = k * 512 + c * P
                        first = j + k == 0 and c % 2 == 0
                        last = j == 3 and k == 3
                        kc = 4 * j + k
                        pe.matmul(o, w_hi[:, n % 2, a:a + P], hT_hi[:, kc], start=first, stop=False,
                                  skip_group_check=True)
                        pe.matmul(o, w_hi[:, n % 2, a:a + P], hT_lo[:, kc], start=False, stop=False,
                                  skip_group_check=True)
                        mm = pe.matmul(o, w_lo[:, n % 2, a:a + P], hT_hi[:, kc], start=False, stop=last,
                                       skip_group_check=True)
                mm.then_inc(item_used, 1)
                if j == 2 and g > 0:
                    key_scores(g - 1)
        key_scores(3)
        st.meet()

        def activations(i, s, q):
            pe.wait_ge(lo_done, 4 * i + (u_first[q] + s + 1))
            pe.wait_ge(gelu_done, 4 * i + (q * QTR + s + 1))
            o = ps[:, s % 2, 0:S]
            for k in range(KC):
                wh, wl = w_hi[:, s % 2, k * P:(k + 1) * P], w_lo[:, s % 2, k * P:(k + 1) * P]
                pe.matmul(o, wh, hT_hi[:, k], start=(k == 0), stop=False)
                pe.matmul(o, wh, hT_lo[:, k], start=False, stop=False)
                mm = pe.matmul(o, wl, hT_hi[:, k], start=False, stop=(k == KC - 1))
            mm.then_inc(item_used, 1)

        def dense(i, s, g):
            n = g * STEPS + s + 1
            b = s % 2
            pe.wait_ge(rows_ready, 4 * i + n)
            pe.wait_ge(hot_ready, 4 * i + n)
            pe.wait_ge(gate_used, 4 * i + n)
            for k in range(TG):
                o = ps[:, 2 + b, k * QTR:(k + 1) * QTR]
                for n in range(3):
                    mm = pe.matmul(o, hot_r[:, b, k], hot_g[:, b, n, k], start=n == 0, stop=n == 2)
            mm.then_inc(gate_ready, 1)

        def outputs(i, s, q, first, last):
            pe.wait_ge(lo_done, 4 * i + (v_first[q] + s + 1))
            pe.wait_ge(c_lo_done, 4 * i + (q * QTR + s + 1))
            for k in range(KC):
                o = ps[:, k // 2, (k % 2) * S:(k % 2 + 1) * S]
                wh, wl = w_hi[:, s % 2, k * P:(k + 1) * P], w_lo[:, s % 2, k * P:(k + 1) * P]
                new = first and k % 2 == 0 and (q == 0 or k < 8)
                pe.matmul(o, wh, c_hi[:, s % 2], start=new, stop=False, skip_group_check=True)
                pe.matmul(o, wh, c_lo[:, s % 2], start=False, stop=False, skip_group_check=True)
                mm = pe.matmul(o, wl, c_hi[:, s % 2], start=False,
                               stop=last and (q == PARTS - 1 or k < 8), skip_group_check=True)
            mm.then_inc(item_used, 1)

        LOOPS = QTR // RAW
        with pe.Fori(0, LOOPS) as i:
            for s in range(RAW):
                activations(i, s, 0)
        st.meet()
        st.meet()
        st.meet()
        turn(plan["keys"])
        pe.drain().then_inc(gate_ready, 2)
        st.meet()
        with pe.Fori(0, LOOPS) as i:
            for s in range(RAW):
                activations(i, s, 1)
                dense(i, s, 0)
        st.meet()
        for q in range(PARTS):
            for s in range(RAW):
                outputs(0, s, q, s == 0, False)
            with pe.Fori(1, LOOPS - 1) as i:
                for s in range(RAW):
                    outputs(i, s, q, False, False)
            for s in range(RAW):
                outputs(LOOPS - 1, s, q, False, s == RAW - 1)
            st.meet()
            pe.wait_ge(flushed, 4 * q + (2 if q + 2 < PARTS else 4 if q + 1 < PARTS else 8))
            if q + 2 < PARTS:
                with pe.Fori(0, LOOPS) as i:
                    for s in range(RAW):
                        activations(i, s, q + 2)
                        dense(i, s, q + 1)
                st.meet()
            elif q + 1 < PARTS:
                with pe.Fori(0, LOOPS) as i:
                    for s in range(RAW):
                        dense(i, s, q + 1)
                st.meet()
        turn(plan["fin"])

    NSUM, NSD, NR = 186, 188, 190
    SS, RR, NEG, RSUM, RINV, LAMC, M8 = 0, 64, 132, 140, 148, 156, 168
    ANG_R, ANG_CS = W(18528, NT, 2, 16), W(19648 + 32, NT, 2, 16)

    def sm(a, n=1):
        return small[:, a:a + n]

    def hv(ap, h):
        return ap.rearrange("p (h d) -> p h d", h=h)

    def head_jobs(t, c0, n, dh, g, scale=1.0, rope=True, step=None):
        step = step or n
        return [(t[:, tile, c0 + h * dh:c0 + (h + step) * dh], step, dh, g, scale, rope, tile)
                for h in range(0, n, step) for tile in range(NT)]

    SCALE = DH ** -0.5
    J_mk = head_jobs(MKV, 0, 4, DH, 1, 1.0, False) + head_jobs(MKV1, 0, 4, DH, 2, 1.0, False)
    J_mq = head_jobs(M_PROJ, 0, 4, DH, 3, SCALE, False)
    J_b = head_jobs(B_PROJ, 0, 8, 64, 0, 64 ** -0.5) + head_jobs(B_PROJ, 512, 8, 64, 1)
    J_sub = head_jobs(Y, 1024, 4, DH, 2, 0.8, False)
    J_a = (head_jobs(A_PROJ, 0, 8, DH, 0, SCALE, step=4) + head_jobs(A_PROJ, EA_KV + 512, 2, DH, 2)
           + head_jobs(A_PROJ, EA_KV + 1024, 2, DH, 3))
    J_cmp = [(KCN[0:N_CMP], 2, DH, 1, 1.0, True, "cmp")]
    ROPE_A = W(11312, NT, 256)
    J_c = head_jobs(C_PROJ, 0, 12, DH, 0, SCALE, step=6) + head_jobs(C_PROJ, 1536, 4, DH, 1)
    ROPE = W(SQ, NT, 256)
    ROPE64 = W(SQ, NT, 128)
    ROPE_IN = W(14496, NT, 256)
    ROPE64_IN = W(20544, NT, 128)

    @block.scalar
    def _(act):
        st = Steps(act, act_step)
        late = [0]
        sqs = [0]
        norms = [0]

        def load(dst, src):
            act.dma_start(dst, src).then_inc(late_in, 16)
            late[0] += 16

        def loaded():
            act.wait_ge(late_in, late[0])

        def split(q, s, size):
            if not isinstance(q, int) or 4 * q + s >= 2:
                act.wait_ge(item_used, 4 * q + (s - 1))
            act.wait_ge(landed[s], 16 * q + 16)
            act.activation(w_hi[:, s % 2, 0:size], raw[:, s, 0:size], ACT.Copy).then_inc(hi_done, 1)

        deferred = []

        def settle():
            if deferred:
                n = deferred.pop() + 2
                split(n // 4, n % 4, items[n].size if n < n_static else 2048)

        def ahead(n, last=False):
            settle()
            if last:
                deferred.append(n)
                return
            n += 2
            split(n // 4, n % 4, items[n].size if n < n_static else 2048)

        def gemm(g, side=None):
            def evac(i):
                if g.adds:
                    return
                act.wait_ge(item_used, 4 * (g.first + i) + 4)
                par, w = (g.first + i) % 2, g.widths[i]
                dst = g.dst[1 + i][:, 0, 0:w] if isinstance(g.dst, tuple) else g.dst[:, 0, i * g.step:i * g.step + w]
                act.wait_ge(norm_r, norms[0])
                act.activation(dst, ps[:, 2 * par, 0:w], ACT.Copy, scale=sm(NR)).then_inc(evac_act, 1)

            for i in range(len(g.widths)):
                for j in range(4):
                    ahead(4 * (g.first + i) + j, i == len(g.widths) - 1 and j == 3)
                    if j == 1 and i > 0:
                        evac(i - 1)
                    if i == len(g.widths) - 1 and j == 3:
                        evac(i)
                    st.side(side, 4 * (g.first + i) + j)

        def turn(T):
            for _ in turn_steps(T):
                pass

        def turn_steps(T):
            for b, (srcs, outs) in enumerate(T.blocks):
                n = T.first + b
                if T.split:
                    act.wait_ge(turn_ready, n + 1)
                    for hi, lo, (c0, c1), gain in outs:
                        act.activation(hi, ps[:, 4 + n % 4, c0:c1], ACT.Copy,
                                       scale=1.0 if gain is None else gain).then_inc(turn_act, 1)
                elif n % 2 == 0:
                    act.wait_ge(turn_ready, n + 1)
                    for dst, (r0, r1), (c0, c1), scale in outs:
                        src = ps[r0:r1, 4 + n % 4, c0:c1]
                        if len(dst.shape) == 3:
                            src = src.rearrange("p (a b) -> p a b", a=dst.shape[1])
                        act.activation(dst, src, ACT.Copy, scale=scale or 1.0).then_inc(turn_act, 1)
                if b % 2 == 1:
                    yield

        def attend(T):
            for _ in attend_steps(T):
                pass

        def attend_steps(T):
            N = len(T.units)
            for r in range(N + 1):
                if r < N:
                    n = T.first + r
                    u = units[n]
                    w = u["nk"] * P
                    act.wait_ge(m_ready, n + 1)
                    if n >= 2:
                        act.wait_ge(t_ready, n - 1)
                    for i in range(2):
                        e = act.activation(PB[:, n % 2, i, 0:w], ps[:, u["bank"], i * w:(i + 1) * w], ACT.Exp,
                                           bias=sm(NEG + 2 * (n % 4) + i), accum_out=sm(RSUM + 2 * (n % 4) + i))
                    e.then_inc(p_ready, 1)
                if r >= 1:
                    n = T.first + r - 1
                    u = units[n]
                    m = len(u["v"]) * u["nk"]
                    act.wait_ge(t_ready, n + 1)
                    if n >= 2:
                        act.wait_ge(o_ready, n - 1)
                    pt = 6 if T.aside else 6 + n % 2
                    act.activation(PTB[:, n % 2, 0:m], ps[:, pt, 0:m * P].rearrange("p (m q) -> p m q", m=m),
                                   ACT.Copy).then_inc(pt_ready, 1)
                yield

        def factors(rows):
            for t in range(NT):
                act.activation(Y[:, t], rows[:, t], ACT.Square, accum_out=sm(NSUM + t)).then_inc(norm_sum, 1)
            norms[0] += 1
            act.wait_ge(norm_var, norms[0])
            act.activation(sm(NSD, 2), sm(NSUM, 2), ACT.Sqrt).then_inc(norm_sd, 1)

        def squares(jobs):
            for j, (src, n, dh, *_, where) in enumerate(jobs):
                if sqs[0]:
                    act.wait_ge(sq_free, sqs[0])
                rows = src.shape[0]
                dst = W(SQ, n * dh)[0:rows]
                if len(src.shape) == 3:
                    dst = hv(dst, n)
                act.activation(dst, src, ACT.Square).then_inc(sq_ready, 1)
                sqs[0] += 1
                if j % 2 == 1:
                    yield

        def qk(jobs, tables=(), mid=None, end=None):
            for _ in squares(jobs):
                pass
            loaded()
            st.meet()
            for dst, src in tables:
                load(dst, src)
            tot = sum(j[1] for j in jobs)
            act.activation(sm(SS, tot), sm(SS, tot), ACT.Sqrt)
            if mid:
                mid()
            loaded()
            st.meet()
            if end:
                end()
            st.meet()

        def silu(ap):
            act.activation(ap, ap, ACT.Silu)

        def gain_rows(pairs):
            for slot, ap in pairs:
                load(gsm[:, slot, 0:ap.shape[-1]], ap.partition_broadcast(P))

        def layer_head(name_x, gm):
            turn(plan[name_x])
            factors(x)
            st.meet()
            gemm(gm)
            loaded()
            st.meet()

        def memory_side(l):
            yield from squares(J_mq)
            yield from st.meet_at(AT_MEM_ROOTS)
            tot = sum(j[1] for j in J_mq)
            act.activation(sm(SS, tot), sm(SS, tot), ACT.Sqrt)
            yield from st.meet_at(AT_MEM_HEADS)
            silu(M_PROJ[:, :, 512:1024])
            yield from st.meet_at(AT_MEM_TURN)
            yield from turn_steps(plan[f"mq{l}"])
            yield from st.meet_at(AT_MEM)
            yield from attend_steps(plan[f"am{l}"])

        def nsa_side():
            yield from st.meet_at(AT_A_SQUARES)
            yield from squares(J_a)
            loaded()
            yield from st.until(AT_A_ROOTS - 1)
            yield from st.meet_at(AT_A_ROOTS)
            tot = sum(j[1] for j in J_a)
            act.activation(sm(SS, tot), sm(SS, tot), ACT.Sqrt)
            yield from st.meet_at(AT_A_HEADS)

        def pool_side():
            yield from st.until(AT_ANGLES - 1)
            loaded()
            yield from st.meet_at(AT_ANGLES)
            yield from st.until(AT_POOL - 1)
            yield from st.meet_at(AT_POOL)
            act.activation(ANG_CS, ANG_R, ACT.Sin)
            yield from st.until(AT_POOLED - 1)
            yield from st.meet_at(AT_POOLED)
            for b in range(2):
                act.activation(MIXT[:, 2 * b:2 * b + 2], ps[:, 4 + b, :].rearrange("p (a t) -> p a t", a=2), ACT.Copy)
            load(COUNT, A["dil_count"])
            load(W(16896, NT, S), A["dil_mask"])
            yield from st.until(AT_DQ - 1)
            loaded()
            yield from st.meet_at(AT_DQ)
            yield from st.until(AT_DK - 1)
            yield from st.meet_at(AT_DK)

        def index_side():
            yield from memory_side(1)
            yield from st.until(AT_ROPE - 1)
            loaded()
            yield from st.meet_at(AT_ROPE)
            yield from st.until(AT_TURN - 1)
            yield from st.meet_at(AT_TURN)
            yield from turn_steps(plan["iq"])
            yield from turn_steps(plan["ik"])
            yield from st.meet_at(AT_SCORES)
            for v in range(16):
                act.wait_ge(rel_ready, v + 1)
                if v >= 2:
                    act.wait_ge(rel_used, v - 1)
                act.activation(W(SCR + 512 * (v % 2), 512), ps[:, 4 + v % 2, :], ACT.Relu).then_inc(relu_done, 1)
                if v % 2 == 1:
                    yield
            yield from st.until(AT_SQUARES - 1)
            yield from st.meet_at(AT_SQUARES)
            load(ROPE_IN, A["rope128"])
            yield from squares(J_c)
            loaded()
            yield from st.until(AT_ROOTS - 1)
            yield from st.meet_at(AT_ROOTS)
            tot = sum(j[1] for j in J_c)
            act.activation(sm(SS, tot), sm(SS, tot), ACT.Sqrt)
            yield from st.meet_at(AT_HEADS)

        load(ident[:], A["ident"])
        load(gains[:], A["gains"])
        gain_rows([(3, A["mem_qk_gain"][0, 0]), (1, A["mem_qk_gain"][0, 1]), (2, A["mem_qk_gain"][1, 1])])
        loaded()
        act.wait_ge(mem_in, 32)
        st.meet()
        act.dma_start(W(SCR, NT, S), A["causal"]).then_inc(const_in, 16)
        act.dma_start(W(SCR + 1024, P), A["ident"]).then_inc(const_in, 16)
        turn(plan["mem0"])
        split(0, 0, 2048)
        split(0, 1, 2048)
        factors(Y)
        st.meet()
        gemm(g_memkv[0])
        gemm(g_memkv[1])
        act.wait_ge(x_in, 32)
        st.meet()
        qk(J_mk)
        turn(plan["mk0"])
        turn(plan["mk1"])
        layer_head("x0", g_m[0])
        for i, (kept, src) in enumerate(((mk_kept, MK1), (mv_kept, MV1))):
            act.dma_start(kept, src).then_inc(kv_out, 16)
        gain_rows([(0, A["diff_qk_gain"][0, 0]), (1, A["diff_qk_gain"][0, 1]), (2, A["diff_subln_gain"][0])])
        load(LAM.rearrange("p a b -> p (a b)"), A["diff_lambda"][0].rearrange("a b -> (a b)").partition_broadcast(P))
        side = memory_side(0)
        st.begin(g_b)
        gemm(g_b, side)
        st.rest(side)
        st.meet()
        qk(J_b, tables=[(ROPE64, A["rope64"])],
           end=lambda: act.activation(sm(LAMC, 2), sm(LAMC + 2, 2), ACT.Exp))
        turn(plan["bq"])
        turn(plan["bk"])
        st.meet()
        attend(plan["ab"])
        st.meet()
        qk(J_sub, mid=lambda: silu(B_PROJ[:, :, 1536:2048]))
        act.wait_ge(kv_out, 32)
        gain_rows([(j, A["nsa_qk_gain"][0, j]) for j in range(4)])
        load(PET, A["pe_t"])
        load(W2, A["cmp_w2"])
        load(ROPE_C, A["rope_cmp"])
        load(VIS, A["cmp_vis"])
        load(ROPE_A, A["rope128"])
        gemm(g_a)
        side = nsa_side()
        st.begin(g_az)
        gemm(g_az, side)
        loaded()
        st.meet()
        turn(plan["raw"])
        st.meet()
        st.meet()
        for n in range(4 * cmp_first, 4 * cmp_first + 8):
            ahead(n, n == 4 * cmp_first + 7)
        act.activation(GATE, A_PROJ[:, :, 2560:2584], ACT.Sigmoid)
        silu(A_PROJ[:, :, 2584:3608])
        st.meet()
        for j in range(2):
            act.activation(CH[0:32, j], ps[0:32, j, 0:CMP_HID], ACT.Silu)
        st.meet()
        turn(plan["cht"])
        st.meet()
        st.meet()
        st.meet()

        def place_values():
            for g in range(2):
                for r in range(4):
                    load(VBD[64 * g + 16 * r:64 * g + 16 * r + N_CMP, r * P:(r + 1) * P], VCR[0:N_CMP, g])

        qk(J_cmp, mid=place_values)
        turn(plan["kct"])
        turn(plan["aq"])
        turn(plan["ak"])
        st.meet()
        st.meet()
        st.meet()
        act.activation(PC, PC, ACT.Exp)
        st.meet()
        st.meet()
        turn(plan["pc"])
        st.meet()
        st.meet()
        st.meet()
        attend(plan["as"])
        st.meet()
        turn(plan["y0"])
        load(MK[1], mk_kept)
        load(MV[1], mv_kept)
        st.meet()
        gemm(g_out[0])
        st.meet()
        gain_rows([(3, A["mem_qk_gain"][1, 0])])
        layer_head("x1", g_m[1])
        gain_rows([(0, A["dsa_qk_gain"][0, 0]), (1, A["dsa_qk_gain"][0, 1])])
        load(ROPE64_IN, A["rope64"])
        side = index_side()
        st.begin(g_ci)
        gemm(g_ci, side)
        gemm(g_c, side)
        gemm(g_cz, side)
        st.meet()
        st.rest(side)
        silu(C_PROJ[:, :, 3664:5200])
        st.meet()
        turn(plan["cq"])
        turn(plan["ck"])
        st.meet()
        attend(plan["ac"])
        st.meet()
        turn(plan["y1"])
        st.meet()
        gemm(g_out[1])
        st.meet()
        turn(plan["x2"])
        factors(x)
        st.meet()
        load(WPOOL.rearrange("p (g c) e -> p g c e", g=4), A["w_pool_2"][0].rearrange("g (c p) e -> p g c e", p=P))
        load(POOLM, A["pool"].rearrange("p s g t -> p (s g) t"))
        load(sm(176, 8), A["pool_scale_2"])
        act.dma_start(posi[:], A["positions_2"]).then_inc(late_in, 16)
        late[0] += 16
        load(inv2[:], A["inv2"])
        side = pool_side()
        st.begin(g_in2)
        gemm(g_in2, side)
        st.rest(side)
        st.meet()
        st.meet()
        for c in range(8):
            act.activation(hT_hi[:, c], ps[:, c // 2, (c % 2) * S:(c % 2 + 1) * S], ACT.Copy,
                           scale=sm(176 + c)).then_inc(mix_hi, 1)
        st.meet()
        turn(plan["dq"])
        turn(plan["dk"])
        st.meet()
        attend(plan["ad"])
        st.meet()
        turn(plan["y2"])
        st.meet()
        for t in range(NT):
            load(Y[:, t], A["mem_2"][t * P:(t + 1) * P])
        gemm(g_out2)
        loaded()
        st.meet()
        turn(plan["mem2"])
        factors(Y)
        st.meet()
        gemm(g_xk)
        gemm(g_xv)
        st.meet()
        turn(plan["xk"])
        turn(plan["x3"])
        factors(x)
        st.meet()
        gemm(g_xq)
        st.meet()
        turn(plan["xq"])
        st.meet()
        attend(plan["ax"])
        st.meet()
        turn(plan["y3"])
        st.meet()
        load(IOTA, A["iota"])
        for j in range(2):
            load(SKN[:, j], A["sub_keys"][j])
        for j in range(4):
            ahead(4 * co_first + j, j == 3)
        loaded()
        st.meet()
        factors(x)
        act.wait_ge(norm_r, norms[0])
        act.activation(Y[:, 0], x[:, 0], ACT.Copy, scale=sm(NR))
        st.meet()
        act.dma_start(x_dram.rearrange("t p d -> p t d"), x[:]).then_inc(moved, 16)
        turn(plan["x4"])
        turn(plan["sk"])
        st.meet()

        def pq_evac(g):
            act.wait_ge(item_used, 4 * (pq_first + g) + 4)
            act.activation(PQT[:, 4 * g:4 * g + 2], ps[:, 2 * (g % 2), :].rearrange("p (a t) -> p a t", a=2),
                           ACT.Copy).then_inc(evac_act, 1)

        def take_scores(g):
            act.wait_ge(key_ready, 2 * g + 1)
            act.activation(SC[:, 0, 4 * g:4 * g + 4], ps[:, 4 + 2 * g % 4, :].rearrange("p (a t) -> p a t", a=4),
                           ACT.Copy).then_inc(key_act, 1)

        for g in range(4):
            for j in range(4):
                ahead(4 * (pq_first + g) + j, g == 3 and j == 3)
                if j == 1 and g > 0:
                    pq_evac(g - 1)
                if j == 2 and g > 0:
                    take_scores(g - 1)
        pq_evac(3)
        take_scores(3)
        act.drain().then_inc(gelu_done, 2)
        st.meet()

        def activate(i, s, q):
            act.wait_ge(item_used, 4 * i + (u_first[q] + s + 1))
            act.activation(CTS[q % 2][:, bass.ds(4 * i + s, 1)].rearrange("p a t -> p (a t)"), ps[:, s % 2, 0:S],
                           ACT.Gelu_apprx_tanh).then_inc(gelu_done, 1)

        def u_split(i, s, q):
            split(i + (u_first[q] // 4 + (s + 2) // 4), (s + 2) % 4, 2048)

        def u_part(q):
            with act.Fori(0, LOOPS - 1) as i:
                for s in range(RAW):
                    u_split(i, s, q)
                    activate(i, s, q)
            for s in range(RAW):
                if s < RAW - 1 or q == 0:
                    u_split(LOOPS - 1, s, q)
                activate(LOOPS - 1, s, q)

        def high(i, s, q):
            if not isinstance(i, int) or 4 * i + s >= 2:
                act.wait_ge(item_used, 4 * i + (v_first[q] + s - 1))
            act.activation(c_hi[:, s % 2], CTS[q % 2][:, bass.ds(4 * i + s, 1)].rearrange("p a t -> p (a t)"),
                           ACT.Copy).then_inc(c_hi_done, 1)

        LOOPS = QTR // RAW
        settle()
        u_part(0)
        st.meet()
        act.activation(SC16, SC16, ACT.Exp)
        st.meet()
        st.meet()
        turn(plan["keys"])
        st.meet()
        u_part(1)
        st.meet()
        for q in range(PARTS):
            def v_step(i, s, last):
                if not (last and s == 3):
                    high(i + (s + 1) // 4, (s + 1) % 4, q)
                if not (last and (s >= 2 and q == PARTS - 1 or s == 3)):
                    split(i + (v_first[q] // 4 + (s + 2) // 4), (s + 2) % 4, 2048)

            high(0, 0, q)
            if q + 1 < PARTS:
                u_split(LOOPS - 1, RAW - 1, q + 1)
            for s in range(RAW):
                v_step(0, s, False)
            with act.Fori(1, LOOPS - 1) as i:
                for s in range(RAW):
                    v_step(i, s, False)
            for s in range(RAW):
                v_step(LOOPS - 1, s, True)
            st.meet()
            if q + 1 < PARTS:
                split(LOOPS - 1 + v_first[q] // 4 + 1, 1, 2048)
                if q + 2 < PARTS:
                    u_part(q + 2)
                else:
                    act.dma_start(XD, x_dram.rearrange("t p d -> p t d")).then_inc(fin_in, 16)
                st.meet()
                if q + 2 == PARTS:
                    act.dma_start(GFIN, A["g_final_2"].partition_broadcast(P)).then_inc(fin_in, 16)
        for b in range(8):
            act.wait_ge(turn_dve, turn_counts[plan["fin"].first + b + 1][1])
            act.activation(W(8192 + 512 * b, 512), FIN[:, b // 4, (b % 4) * 512:(b % 4 + 1) * 512], ACT.Square,
                           accum_out=sm(128 + b)).then_inc(fin_sum, 1)
        act.wait_ge(fin_var, 1)
        act.activation(sm(138, 2), sm(136, 2), ACT.Sqrt).then_inc(fin_sd, 1)
        for t in range(NT):
            act.wait_ge(dve_out, t + 1)
            act.dma_start(out[0, t * P:(t + 1) * P], FIN[:, t]).then_inc(out_done, 16)
        act.wait_ge(out_done, 32)

    @block.gpsimd
    def _(pool):
        g = PARTS - 1
        with pool.Fori(0, STEPS // 4) as i:
            for s in range(4):
                tokens = bass.ds(4 * TG * i + TG * s, TG)
                pool.wait_ge(hv_ready, 4 * i + (g * STEPS + s + 1))
                pool.tensor_tensor(hot_g[:, s % 2], hot_e[:, s % 2].unsqueeze(1).broadcast_to([P, 3, TG, QTR]),
                                   GATES[:, :, tokens].unsqueeze(3).broadcast_to([P, 3, TG, QTR]), ALU.mult
                                   ).then_inc(hot_ready, 1)

    @block.vector
    def _(dve):
        st = Steps(dve, dve_step)
        done = st.done
        sqs = [0]
        reworked = [0]
        norms = [0]

        def split(q, s, size):
            dve.wait_ge(hi_done, 4 * q + (s + 1))
            dve.tensor_tensor(w_lo[:, s % 2, 0:size], raw[:, s, 0:size], w_hi[:, s % 2, 0:size].bitcast(F32),
                              ALU.subtract).then_inc(lo_done, 1)

        deferred = []

        def settle():
            if deferred:
                n = deferred.pop() + 2
                split(n // 4, n % 4, items[n].size if n < n_static else 2048)

        def ahead(n, last=False):
            settle()
            if last:
                deferred.append(n)
                return
            n += 2
            split(n // 4, n % 4, items[n].size if n < n_static else 2048)

        def gemm(g, side=None):
            def evac(i):
                dve.wait_ge(item_used, 4 * (g.first + i) + 4)
                par, w = (g.first + i) % 2, g.widths[i]
                if g.adds:
                    for t in range(NT):
                        xs = x[:, t, i * g.step:i * g.step + w]
                        e = dve.tensor_tensor(xs, xs, ps[:, 2 * par + t, 0:w], ALU.add)
                else:
                    dst = g.dst[1 + i][:, 1, 0:w] if isinstance(g.dst, tuple) else g.dst[:, 1, i * g.step:i * g.step + w]
                    e = dve.tensor_scalar(dst, ps[:, 2 * par + 1, 0:w], sm(NR + 1), None, ALU.mult)
                e.then_inc(evac_dve, 1)

            for i in range(len(g.widths)):
                for j in range(4):
                    ahead(4 * (g.first + i) + j, i == len(g.widths) - 1 and j == 3)
                    if j == 1 and i > 0:
                        evac(i - 1)
                    if i == len(g.widths) - 1 and j == 3:
                        evac(i)
                    st.side(side, 4 * (g.first + i) + j)

        def turn(T):
            for _ in turn_steps(T):
                pass

        def turn_steps(T):
            for b, (srcs, outs) in enumerate(T.blocks):
                n = T.first + b
                if T.split:
                    for m, (hi, lo, (c0, c1), gain) in enumerate(outs):
                        dve.wait_ge(turn_act, turn_counts[n + 1][0])
                        src = ps[:, 4 + n % 4, c0:c1]
                        if gain is None:
                            dve.tensor_tensor(lo, src, hi.bitcast(F32), ALU.subtract).then_inc(turn_dve, 1)
                        else:
                            dve.scalar_tensor_tensor(out=lo, in0=src, scalar=gain, in1=hi.bitcast(F32),
                                                     op0=ALU.mult, op1=ALU.subtract).then_inc(turn_dve, 1)
                elif n % 2 == 1:
                    dve.wait_ge(turn_ready, n + 1)
                    for dst, (r0, r1), (c0, c1), scale in outs:
                        src = ps[r0:r1, 4 + n % 4, c0:c1]
                        if len(dst.shape) == 3:
                            src = src.rearrange("p (a b) -> p a b", a=dst.shape[1])
                        if scale:
                            dve.tensor_scalar(dst, src, scale, None, ALU.mult).then_inc(turn_dve, 1)
                        else:
                            dve.tensor_copy(dst, src).then_inc(turn_dve, 1)
                if b % 2 == 1:
                    yield

        def attend(T):
            for _ in attend_steps(T):
                pass

        def attend_steps(T):
            N = len(T.units)
            lag = 2 if T.aside else 3
            for r in range(N + lag):
                if r < N:
                    n = T.first + r
                    w = units[n]["nk"] * P
                    dve.wait_ge(s_ready, n + 1)
                    dve.tensor_reduce(sm(NEG + 2 * (n % 4), 2), hv(ps[:, units[n]["bank"], 0:2 * w], 2), AX, ALU.max,
                                      negate=True).then_inc(m_ready, 1)
                if 1 <= r <= N:
                    n = T.first + r - 1
                    u = units[n]
                    w, c = u["nk"] * P, 2 * (n % 4)
                    dve.wait_ge(p_ready, n + 1)
                    if u["kind"] == "dilated":
                        pb = PB[:, n % 2, :, 0:w]
                        done(dve.tensor_tensor(pb, pb, COUNT[:, u["tile"], 0:w].unsqueeze(1).broadcast_to([P, 2, w]),
                                               ALU.mult))
                        dve.tensor_reduce(sm(RSUM + c, 2), pb, AX, ALU.add).then_inc(a_ready, 1)
                        reworked[0] += 1
                        dve.wait_ge(a_ready, reworked[0])
                    done(dve.reciprocal(sm(RINV + c, 2), sm(RSUM + c, 2)))
                    if u["kind"] == "diff":
                        done(dve.tensor_tensor(sm(RINV + c + 1), sm(RINV + c + 1), sm(LAMC + 4), ALU.mult))
                        p0, p1 = PB[:, n % 2, 0, 0:w], PB[:, n % 2, 1, 0:w]
                        done(dve.tensor_scalar(p0, p0, sm(RINV + c), None, ALU.mult))
                        dve.scalar_tensor_tensor(out=p0, in0=p1, scalar=sm(RINV + c + 1), in1=p0,
                                                 op0=ALU.mult, op1=ALU.add).then_inc(a_ready, 1)
                        reworked[0] += 1
                    if u["kind"] == "gated":
                        for i in range(2):
                            e = dve.tensor_tensor(sm(RINV + c + i), sm(RINV + c + i), u["gate"][i], ALU.mult)
                        done(e)
                if r >= lag:
                    n = T.first + r - lag
                    u = units[n]
                    c = 2 * (n % 4)
                    dve.wait_ge(o_ready, n + 1)
                    nv = len(u["v"])
                    o = hv(ps[:, 7 if T.aside else n % 2, 0:nv * P], nv)
                    if u["kind"] == "gated":
                        for i in range(2):
                            y = u["dst"][:, i * P:(i + 1) * P]
                            e = dve.scalar_tensor_tensor(out=y, in0=o[:, i], scalar=sm(RINV + c + i), in1=y,
                                                         op0=ALU.mult, op1=ALU.add)
                    elif u["kind"] == "diff":
                        e = dve.tensor_copy(u["dst"], o[:, 0])
                    else:
                        e = dve.tensor_tensor(hv(u["dst"], 2), o,
                                              sm(RINV + c, 2).unsqueeze(2).broadcast_to([P, 2, P]), ALU.mult)
                    e.then_inc(o_used, 1)
                yield
            dve.wait_ge(o_used, T.first + N)

        def factors():
            norms[0] += 1
            dve.wait_ge(norm_sum, 2 * norms[0])
            dve.tensor_scalar(sm(NSUM, 2), sm(NSUM, 2), 1.0 / D, EPS, ALU.mult, ALU.add).then_inc(norm_var, 1)
            dve.wait_ge(norm_sd, norms[0])
            dve.reciprocal(sm(NR, 2), sm(NSD, 2)).then_inc(norm_r, 1)
            dve.wait_ge(norm_r, norms[0])

        def rotate(*args):
            for _ in rotate_steps(*args):
                pass

        def rotate_steps(src, dst, n, dh, C, Sn, r=None, rows=P):
            half = dh // 2
            if r is not None:
                na = hv(W(TA, n * dh)[0:rows], n)
                done(dve.tensor_tensor(na, src, r.unsqueeze(2).broadcast_to([rows, n, dh]), ALU.mult))
            else:
                na = src
            nb = hv(W(TB_, n * dh)[0:rows], n)
            nc_ = hv(W(TA, n * dh)[0:rows], n) if r is None else dst

            def b(ap, w):
                return ap.unsqueeze(1).broadcast_to([rows, n, w])

            dve.tensor_tensor(nb[:, :, 0:half], na[:, :, half:dh], b(Sn[:, 0:half], half), ALU.mult)
            dve.tensor_tensor(nb[:, :, half:dh], na[:, :, 0:half], b(Sn[:, half:dh], half), ALU.mult)
            if n * dh > 512:
                yield
            done(dve.tensor_tensor(nc_, na, b(C, dh), ALU.mult))
            done(dve.tensor_tensor(dst, nc_, nb, ALU.add))

        def qk(jobs, mid=None):
            for _ in qk_steps(jobs, mid, ROPE):
                pass

        def qk_steps(jobs, mid, rope_table, at=None):
            off = 0
            offs = []
            for src, n, dh, g, scale, rope, where in jobs:
                sqs[0] += 1
                dve.wait_ge(sq_ready, sqs[0])
                rows = src.shape[0]
                dve.tensor_reduce(small[0:rows, SS + off:SS + off + n], hv(W(SQ, n * dh)[0:rows], n), AX,
                                  ALU.add).then_inc(sq_free, 1)
                offs.append(off)
                off += n
                if len(offs) % 2 == 0:
                    yield
            dve.wait_ge(sq_free, sqs[0])
            for (src, n, dh, *_), o in zip(jobs, offs):
                rows = src.shape[0]
                v = small[0:rows, SS + o:SS + o + n]
                dve.tensor_scalar(v, v, 1.0 / dh, EPS, ALU.mult, ALU.add)
            if at:
                yield from st.until(at[0] - 1)
                yield from st.meet_at(at[0])
                yield from st.meet_at(at[1])
            else:
                st.meet()
                if mid:
                    mid()
                st.meet()
            done(dve.reciprocal(sm(RR, off), sm(SS, off)))
            table_of = None
            for (src, n, dh, g, scale, rope, where), o in zip(jobs, offs):
                rows = src.shape[0]
                r = small[0:rows, RR + o:RR + o + n]
                src = src if len(src.shape) == 3 else hv(src, n)
                if rope:
                    if table_of != (g, where == "cmp"):
                        table_of = (g, where == "cmp")
                        tab = W(TAB, NT, 2 * dh)
                        gb = gsm[:, g, 0:dh]
                        base = rope_table if dh == DH else ROPE64
                        if where == "cmp":
                            tab, base = W(TAB, 1, 2 * dh), ROPE_C.unsqueeze(1)
                        k, half = tab.shape[1], dh // 2

                        def bb(ap):
                            return ap.unsqueeze(1).broadcast_to([P, k, ap.shape[-1]])

                        dve.tensor_tensor(tab[:, :, 0:dh], base[:, :, 0:dh], bb(gb), ALU.mult)
                        dve.tensor_tensor(tab[:, :, dh:dh + half], base[:, :, dh:dh + half], bb(gb[:, half:dh]),
                                          ALU.mult)
                        done(dve.tensor_tensor(tab[:, :, dh + half:2 * dh], base[:, :, dh + half:2 * dh],
                                               bb(gb[:, 0:half]), ALU.mult))
                        if scale != 1.0:
                            done(dve.tensor_scalar(tab, tab, scale, None, ALU.mult))
                    i = 0 if where == "cmp" else where
                    yield from rotate_steps(src, src, n, dh, tab[0:rows, i, 0:dh], tab[0:rows, i, dh:2 * dh], r, rows)
                    yield
                else:
                    na = hv(W(TA, n * dh)[0:rows], n)
                    done(dve.scalar_tensor_tensor(out=na, in0=src, scalar=scale,
                                                  in1=r.unsqueeze(2).broadcast_to([rows, n, dh]),
                                                  op0=ALU.mult, op1=ALU.mult))
                    done(dve.tensor_tensor(src, na, gsm[:, g, 0:dh].unsqueeze(1).broadcast_to([rows, n, dh]),
                                           ALU.mult))
            if jobs is J_sub:
                gate_by(Y[:, :, 1024:1536], B_PROJ[:, :, 1536:2048])
            if not at:
                st.meet()

        def gate_by(y, z):
            dve.tensor_tensor(y, y, z, ALU.mult)

        def layer_head(name_x, gm):
            turn(plan[name_x])
            factors()
            st.meet()
            gemm(gm)
            st.meet()

        def memory_side(l):
            yield from qk_steps(J_mq, None, None, at=(AT_MEM_ROOTS, AT_MEM_HEADS))
            yield from st.until(AT_MEM_TURN - 1)
            yield from st.meet_at(AT_MEM_TURN)
            yield from turn_steps(plan[f"mq{l}"])
            yield from st.meet_at(AT_MEM)
            yield from attend_steps(plan[f"am{l}"])
            gate_by(Y[:, :, 1536:2048], M_PROJ[:, :, 512:1024])
            if l == 0:
                yield
                q4 = BQT.rearrange("p (h i) t -> p h i t", i=2)
                dve.memset(q4[64:P, :, 0], 0.0)
                dve.memset(q4[0:64, :, 1], 0.0)

        def nsa_side():
            yield from st.meet_at(AT_A_SQUARES)
            yield from qk_steps(J_a, None, ROPE_A, at=(AT_A_ROOTS, AT_A_HEADS))

        def rotate_part(c0):
            for t in range(NT):
                v = hv(D_PROJ[:, t, c0:c0 + 1024], 8)
                cs = ANG_CS[:, t, 0].unsqueeze(1).broadcast_to([P, 8, 16])
                sn = ANG_CS[:, t, 1].unsqueeze(1).broadcast_to([P, 8, 16])
                x1, x2 = v[:, :, 0:16], v[:, :, 16:32]
                r = [hv(W(18624 + 128 * i, 128), 8) for i in range(4)]
                dve.tensor_tensor(r[0], x1, cs, ALU.mult)
                dve.tensor_tensor(r[1], x2, sn, ALU.mult)
                dve.tensor_tensor(r[2], x2, cs, ALU.mult)
                done(dve.tensor_tensor(r[3], x1, sn, ALU.mult))
                dve.tensor_tensor(x1, r[0], r[1], ALU.subtract)
                done(dve.tensor_tensor(x2, r[2], r[3], ALU.add))

        def pool_side():
            yield from st.until(AT_ANGLES - 1)
            yield from st.meet_at(AT_ANGLES)
            pf = sm(184, 2)
            done(dve.tensor_copy(pf, posi[:]))
            ang, kk, tmp2 = W(18432, NT, 16), W(18464, NT, 16), W(18496, NT, 16)
            for t in range(NT):
                e = dve.tensor_scalar(ang[:, t], inv2[:], sm(184 + t), None, ALU.mult)
            done(e)
            done(dve.tensor_scalar(kk, ang, 1.0 / (2 * math.pi), 12582912.0, ALU.mult, ALU.add))
            done(dve.tensor_scalar(kk, kk, -12582912.0, None, ALU.add))
            rest = 2 * math.pi
            parts = []
            for bits in (7, 11):
                c = math.floor(rest * 2 ** bits) / 2 ** bits
                if bits == 11:
                    c = math.floor(rest * 2 ** 19) / 2 ** 19
                parts.append(c)
                rest -= c
            parts.append(rest)
            for c in parts:
                done(dve.scalar_tensor_tensor(out=ang, in0=kk, scalar=-c, in1=ang, op0=ALU.mult, op1=ALU.add))
            done(dve.tensor_scalar(ANG_R[:, :, 1], ang, math.pi, -math.pi, ALU.min, ALU.max))
            done(dve.tensor_scalar(tmp2, ang, math.pi / 2, None, ALU.is_gt))
            done(dve.scalar_tensor_tensor(out=ang, in0=tmp2, scalar=-2 * math.pi, in1=ang, op0=ALU.mult, op1=ALU.add))
            done(dve.tensor_scalar(ang, ang, math.pi / 2, None, ALU.add))
            done(dve.tensor_scalar(ANG_R[:, :, 0], ang, math.pi, -math.pi, ALU.min, ALU.max))
            yield from st.until(AT_POOL - 1)
            yield from st.meet_at(AT_POOL)
            yield from st.until(AT_POOLED - 1)
            yield from st.meet_at(AT_POOLED)
            for b in range(2, 4):
                dve.tensor_copy(MIXT[:, 2 * b:2 * b + 2], ps[:, 4 + b, :].rearrange("p (a t) -> p a t", a=2))
            yield from st.until(AT_DQ - 1)
            yield from st.meet_at(AT_DQ)
            dve.tensor_copy(mask2[:], W(16896, NT, S))
            rotate_part(1024)
            yield from st.until(AT_DK - 1)
            yield from st.meet_at(AT_DK)
            rotate_part(2048)

        def index_side():
            yield from memory_side(1)
            yield from st.until(AT_ROPE - 1)
            yield from st.meet_at(AT_ROPE)
            for t in range(NT):
                for h in range(2):
                    v = hv(C_PROJ[:, t, 2560 + 512 * h:3072 + 512 * h], 8)
                    rotate(v, v, 8, 64, ROPE64_IN[:, t, 0:64], ROPE64_IN[:, t, 64:128])
                    rotate(C_PROJ[:, t, 3584:3648].unsqueeze(1), IK2[:, t, 64 * h:64 * h + 64].unsqueeze(1), 1, 64,
                           ROPE64_IN[:, t, 0:64], ROPE64_IN[:, t, 64:128])
                    if t + h < 2:
                        yield
            wi = C_PROJ[:, :, 3648:3664]
            done(dve.tensor_scalar(wi, wi, 16 ** -0.5 * 64 ** -0.5, None, ALU.mult))
            dve.memset(IKZ[64:P, 0], 0.0)
            dve.memset(IKZ[0:64, 1], 0.0)
            yield from st.until(AT_TURN - 1)
            yield from st.meet_at(AT_TURN)
            yield from turn_steps(plan["iq"])
            yield from turn_steps(plan["ik"])
            yield from st.meet_at(AT_SCORES)
            accs = [W(SCR + 1024 + 256 * t, S) for t in range(NT)]
            for v in range(16):
                t, b = v // 8, v % 8
                dve.wait_ge(relu_done, v + 1)
                for i in range(2):
                    e = dve.scalar_tensor_tensor(
                        out=accs[t], in0=W(SCR + 512 * (v % 2) + S * i, S),
                        scalar=C_PROJ[:, t, 3648 + 2 * b + i:3649 + 2 * b + i],
                        in1=causal[:, t] if b + i == 0 else accs[t], op0=ALU.mult, op1=ALU.add)
                    if i == 0:
                        done(e)
                e.then_inc(rel_used, 1)
                dve.wait_ge(rel_used, v + 1)
                if v % 2 == 1:
                    yield
            a, o = accs, [W(SCR + 1536, S), W(SCR, S)]
            best = [sm(M8, 8), sm(M8 + 8, 8)]
            for r in range(8):
                for t in range(NT):
                    e = dve.max(best[t], a[t])
                done(e)
                for t in range(NT):
                    e = dve.match_replace(o[t], best[t], a[t], TAKEN)
                done(e)
                a, o = o, a
                if r % 2 == 1:
                    yield
            for t in range(NT):
                done(dve.tensor_scalar(a[t], a[t], TAKEN / 2, MASKED, ALU.is_gt, ALU.mult))
                done(dve.tensor_tensor(mask2[:, t], a[t], causal[:, t], ALU.min))
            yield from st.until(AT_SQUARES - 1)
            yield from st.meet_at(AT_SQUARES)
            yield from qk_steps(J_c, None, ROPE_IN, at=(AT_ROOTS, AT_HEADS))

        dve.memset(small[:], 0.0)
        st.meet()
        turn(plan["mem0"])
        split(0, 0, 2048)
        split(0, 1, 2048)
        factors()
        st.meet()
        gemm(g_memkv[0])
        dve.wait_ge(const_in, 32)
        dve.tensor_copy(causal[:], W(SCR, NT, S))
        dve.tensor_copy(identb[:], W(SCR + 1024, P))
        gemm(g_memkv[1])
        st.meet()
        qk(J_mk)
        turn(plan["mk0"])
        turn(plan["mk1"])
        layer_head("x0", g_m[0])
        side = memory_side(0)
        st.begin(g_b)
        gemm(g_b, side)
        st.rest(side)
        st.meet()

        def lambdas():
            done(dve.tensor_tensor(LAM[:, 0], LAM[:, 0], LAM[:, 1], ALU.mult))
            done(dve.tensor_tensor(LAM[:, 2], LAM[:, 2], LAM[:, 3], ALU.mult))
            dve.tensor_reduce(sm(LAMC + 2), LAM[:, 0], AX, ALU.add)
            dve.tensor_reduce(sm(LAMC + 3), LAM[:, 2], AX, ALU.add)

        qk(J_b, mid=lambdas)
        done(dve.tensor_tensor(sm(LAMC + 4), sm(LAMC + 1), sm(LAMC), ALU.subtract))
        done(dve.tensor_scalar(sm(LAMC + 4), sm(LAMC + 4), -(0.8 - 0.6 * math.exp(0.0)), None, ALU.add))
        turn(plan["bq"])
        turn(plan["bk"])
        st.meet()
        attend(plan["ab"])
        st.meet()
        qk(J_sub)
        gemm(g_a)
        side = nsa_side()
        st.begin(g_az)
        gemm(g_az, side)
        st.meet()
        turn(plan["raw"])
        st.meet()
        tmp = W(SCR, 2, 1024)
        done(dve.memset(tmp, 0.0))
        done(dve.tensor_copy(blk_hi[:, 2048:2048 + P], tmp[:, 0, 0:P]))
        done(dve.tensor_copy(blk_lo[:, 2048:2048 + P], tmp[:, 0, 0:P]))
        for j in range(2):
            t4 = tmp[:, j].rearrange("p (l g c) -> p l g c", l=CMP_LEN, g=2)
            src = AKT[:, 4 + 2 * j:6 + 2 * j]
            for g in range(2):
                w = src[:, g].rearrange("p (c l) -> p l c", l=CMP_STRIDE)
                for h in range(2):
                    e = dve.tensor_tensor(t4[:, 16 * h:16 * h + 16, g, 0:N_CMP], w[:, :, h:h + N_CMP],
                                          PET[:, j, 16 * h:16 * h + 16].unsqueeze(2).broadcast_to([P, 16, N_CMP]),
                                          ALU.add)
            done(e)
            bh, bl = blk_hi[:, j * 1024:(j + 1) * 1024], blk_lo[:, j * 1024:(j + 1) * 1024]
            done(dve.tensor_copy(bh, tmp[:, j]))
            done(dve.tensor_tensor(bl, tmp[:, j], bh.bitcast(F32), ALU.subtract))
        st.meet()
        for n in range(4 * cmp_first, 4 * cmp_first + 8):
            ahead(n, n == 4 * cmp_first + 7)
            st.side(side, n)
        st.rest(side)
        st.meet()
        dve.memset(VBD, 0.0)
        st.meet()
        turn(plan["cht"])
        st.meet()
        dve.memset(PC, 0.0)
        st.meet()
        for g in range(2):
            dve.tensor_copy(KCN[0:N_CMP, g], ps[0:N_CMP, g, 0:P])
            dve.tensor_copy(VCR[0:N_CMP, g], ps[0:N_CMP, 2 + g, 0:P])
        st.meet()
        qk(J_cmp)
        turn(plan["kct"])
        turn(plan["aq"])
        turn(plan["ak"])
        st.meet()
        st.meet()
        VB = W(SCR, NT, 16)
        MX = W(SCR + 32, NT, 8)
        done(dve.tensor_scalar(VB, VIS, -1.0, -MASKED, ALU.add, ALU.mult))
        for t in range(NT):
            pc = PC[:, t].rearrange("p (h c) -> p h c", h=8)[:, :, 0:N_CMP]
            sc = ps[:, t, 0:P].rearrange("p (h c) -> p h c", h=8)[:, :, 0:N_CMP]

            def bh8(ap):
                return ap.unsqueeze(1).broadcast_to([P, 8, N_CMP])

            done(dve.tensor_tensor(pc, sc, bh8(VIS[:, t, 0:N_CMP]), ALU.mult))
            done(dve.tensor_tensor(pc, pc, bh8(VB[:, t, 0:N_CMP]), ALU.add))
            done(dve.tensor_reduce(MX[:, t], pc, AX, ALU.max))
            done(dve.tensor_tensor(pc, pc, MX[:, t].unsqueeze(2).broadcast_to([P, 8, N_CMP]), ALU.subtract))
        st.meet()
        st.meet()
        for t in range(NT):
            pc = PC[:, t].rearrange("p (h c) -> p h c", h=8)
            done(dve.tensor_tensor(pc, pc, VIS[:, t].unsqueeze(1).broadcast_to([P, 8, 16]), ALU.mult))
            done(dve.tensor_reduce(MX[:, t], pc, AX, ALU.add))
            done(dve.tensor_scalar(MX[:, t], MX[:, t], 1e-30, None, ALU.max))
            done(dve.reciprocal(MX[:, t], MX[:, t]))
            done(dve.tensor_tensor(pc, pc, MX[:, t].unsqueeze(2).broadcast_to([P, 8, 16]), ALU.mult))
        st.meet()
        turn(plan["pc"])
        st.meet()
        st.meet()
        for t in range(NT):
            for g in range(2):
                gt = GATE[:, t, 12 * g:12 * g + 12].rearrange("p (r k) -> p r k", k=3)[:, :, 0]
                dve.tensor_tensor(hv(Y[:, t, g * 512:(g + 1) * 512], 4), hv(ps[:, 2 * t + g, :], 4),
                                  gt.unsqueeze(2).broadcast_to([P, 4, P]), ALU.mult)
        st.meet()
        attend(plan["as"])
        gate_by(Y[:, :, 0:1024], A_PROJ[:, :, 2584:3608])
        st.meet()
        turn(plan["y0"])
        st.meet()
        gemm(g_out[0])
        st.meet()
        layer_head("x1", g_m[1])
        side = index_side()
        st.begin(g_ci)
        gemm(g_ci, side)
        gemm(g_c, side)
        gemm(g_cz, side)
        st.meet()
        st.rest(side)
        st.meet()
        turn(plan["cq"])
        turn(plan["ck"])
        st.meet()
        attend(plan["ac"])
        gate_by(Y[:, :, 0:1536], C_PROJ[:, :, 3664:5200])
        st.meet()
        turn(plan["y1"])
        st.meet()
        gemm(g_out[1])
        st.meet()
        turn(plan["x2"])
        factors()
        st.meet()
        side = pool_side()
        st.begin(g_in2)
        gemm(g_in2, side)
        st.rest(side)
        st.meet()
        st.meet()
        for c in range(8):
            dve.wait_ge(mix_hi, c - c % 2 + 2)
            dve.scalar_tensor_tensor(out=hT_lo[:, c], in0=ps[:, c // 2, (c % 2) * S:(c % 2 + 1) * S],
                                     scalar=sm(176 + c), in1=hT_hi[:, c].bitcast(F32), op0=ALU.mult,
                                     op1=ALU.subtract)
        st.meet()
        turn(plan["dq"])
        turn(plan["dk"])
        st.meet()
        attend(plan["ad"])
        st.meet()
        turn(plan["y2"])
        st.meet()
        gemm(g_out2)
        st.meet()
        turn(plan["mem2"])
        factors()
        st.meet()
        gemm(g_xk)
        gemm(g_xv)
        st.meet()
        turn(plan["xk"])
        turn(plan["x3"])
        factors()
        st.meet()
        gemm(g_xq)
        st.meet()
        turn(plan["xq"])
        st.meet()
        attend(plan["ax"])
        st.meet()
        turn(plan["y3"])
        st.meet()
        for j in range(4):
            ahead(4 * co_first + j, j == 3)
            dve.wait_ge(item_used, 4 * co_first + j + 1)
            for t in range(NT):
                xs = x[:, t, j * 512:(j + 1) * 512]
                e = dve.tensor_tensor(xs, xs, ps[:, 2 * (j % 2) + t, :], ALU.add)
            e.then_inc(evac_dve, 1)
        st.meet()
        factors()
        dve.tensor_scalar(Y[:, 1], x[:, 1], sm(NR + 1), None, ALU.mult)
        st.meet()
        turn(plan["x4"])
        turn(plan["sk"])
        st.meet()

        def pq_evac(g):
            dve.wait_ge(item_used, 4 * (pq_first + g) + 4)
            dve.tensor_copy(PQT[:, 4 * g + 2:4 * g + 4], ps[:, 2 * (g % 2) + 1, :].rearrange("p (a t) -> p a t", a=2)
                            ).then_inc(evac_dve, 1)

        def top16(jobs):
            for vals, idx, data, other in jobs:
                e = dve.max(vals[:, 0:8], data)
            done(e)
            for vals, idx, data, other in jobs:
                dve.max_index(idx[:, 0:8], vals[:, 0:8], data)
            for vals, idx, data, other in jobs:
                e = dve.match_replace(other, vals[:, 0:8], data, TAKEN)
            done(e)
            yield
            for vals, idx, data, other in jobs:
                e = dve.max(vals[:, 8:16], other)
            done(e)
            for vals, idx, data, other in jobs:
                e = dve.max_index(idx[:, 8:16], vals[:, 8:16], other)
            done(e)
            yield

        def choose():
            for g in range(4):
                dve.wait_ge(key_act, g + 1)
                dve.wait_ge(key_dve, g + 1)
                for c in range(4 * g, 4 * g + 4, 2):
                    for t in range(NT):
                        yield from top16([(V16[:, t, c + i], I16U[:, 16 * t + c + i], SC[:, t, c + i],
                                           W(OTHER + i * P, P)) for i in range(2)])
            done(dve.tensor_copy(I16F.rearrange("p t c k -> p (t c) k"), I16U))
            for t in range(NT):
                vv = V16[:, t].rearrange("p (h j) k -> p h j k", j=2)
                done(dve.tensor_tensor(CAND.rearrange("p h (a b) -> p h a b", a=16),
                                       vv[:, :, 0].unsqueeze(3).broadcast_to([P, 8, 16, 16]),
                                       vv[:, :, 1].unsqueeze(2).broadcast_to([P, 8, 16, 16]), ALU.add))
                yield
                for h in range(0, 8, 2):
                    yield from top16([(SC16[:, t, h + i], CI16U[:, 0, 8 * t + h + i], CAND[:, h + i],
                                       W(OTHER + i * 2 * P, 2 * P)) for i in range(2)])
            done(dve.tensor_scalar(CI16U[:, 1], CI16U[:, 0], 4, None, ALU.logical_shift_right))
            done(dve.tensor_scalar(CI16U[:, 2], CI16U[:, 0], 15, None, ALU.bitwise_and))
            for j in range(2):
                done(dve.tensor_copy(CI16F.rearrange("p t h k -> p (t h) k"), CI16U[:, 1 + j]))
                for t in range(NT):
                    ii = I16F[:, t].rearrange("p (h j) k -> p h j k", j=2)[:, :, j]
                    pk = PICK.rearrange("p h (a b) -> p h a b", a=16)
                    done(dve.tensor_tensor(pk, CI16F[:, t].unsqueeze(3).broadcast_to([P, 8, 16, 16]),
                                           IOTA[:, 0:16].unsqueeze(1).unsqueeze(1).broadcast_to([P, 8, 16, 16]),
                                           ALU.is_equal))
                    yield
                    done(dve.tensor_tensor(pk, pk, ii.unsqueeze(2).broadcast_to([P, 8, 16, 16]), ALU.mult))
                    yield
                    done(dve.tensor_reduce(hv(KEYS[:, t, j], 8), pk, AX, ALU.add))
                    yield
            for t in range(NT):
                done(dve.tensor_copy(MXK[:, t], SC16[:, t, :, 0]))
                done(dve.tensor_tensor(SC16[:, t], SC16[:, t], MXK[:, t].unsqueeze(2).broadcast_to([P, 8, 16]),
                                       ALU.subtract))

        def take_scores(g):
            dve.wait_ge(key_ready, 2 * g + 2)
            dve.tensor_copy(SC[:, 1, 4 * g:4 * g + 4], ps[:, 5 + 2 * g % 4, :].rearrange("p (a t) -> p a t", a=4)
                            ).then_inc(key_dve, 1)

        choosing = choose()
        for g in range(4):
            for j in range(4):
                ahead(4 * (pq_first + g) + j, g == 3 and j == 3)
                if j == 1 and g > 0:
                    pq_evac(g - 1)
                if j == 2 and g > 0:
                    take_scores(g - 1)
                elif g > 1 or j > 2 and g > 0:
                    next(choosing)
                    next(choosing)
        pq_evac(3)
        take_scores(3)
        st.meet()

        LOOPS = QTR // RAW

        def u_split(i, s, q):
            split(i + (u_first[q] // 4 + (s + 2) // 4), (s + 2) % 4, 2048)

        settle()
        for n in range(QTR):
            u_split(n // 4, n % 4, 0)
            for _ in range(2):
                next(choosing, None)
        for _ in choosing:
            pass
        st.meet()
        st.meet()
        for t in range(NT):
            done(dve.tensor_reduce(MXK[:, t], SC16[:, t], AX, ALU.add))
            done(dve.reciprocal(MXK[:, t], MXK[:, t]))
            done(dve.tensor_tensor(hv(KEYS[:, t, 2], 8), SC16[:, t], MXK[:, t].unsqueeze(2).broadcast_to([P, 8, 16]),
                                   ALU.mult))
        st.meet()
        turn(plan["keys"])
        dve.drain().then_inc(gate_used, 2)
        st.meet()

        def hots(i, s, g, alone=False):
            dve.wait_ge(gate_ready, 4 * i + (g * STEPS + s + 1))
            tokens = bass.ds(4 * TG * i + TG * s, TG)
            iota = ps[:, 0, 0:P] if alone else IOTA_B
            dve.tensor_tensor(hot_e[:, s % 2], iota[:, g * QTR:(g + 1) * QTR].unsqueeze(1).broadcast_to([P, TG, QTR]),
                              E2B[:, tokens].unsqueeze(2).broadcast_to([P, TG, QTR]), ALU.is_equal
                              ).then_inc(hv_ready, 1)
            dve.tensor_tensor(hot_r[:, s % 2], iota.unsqueeze(1).broadcast_to([P, TG, P]),
                              E1B[:, tokens].unsqueeze(2).broadcast_to([P, TG, P]), ALU.is_equal
                              ).then_inc(rows_ready, 1)
            if alone:
                return
            dve.wait_ge(hv_ready, 4 * i + (g * STEPS + s + 1))
            dve.tensor_tensor(hot_g[:, s % 2], hot_e[:, s % 2].unsqueeze(1).broadcast_to([P, 3, TG, QTR]),
                              GATES[:, :, tokens].unsqueeze(3).broadcast_to([P, 3, TG, QTR]), ALU.mult
                              ).then_inc(hot_ready, 1)

        def weigh(i, s, g):
            dve.wait_ge(gate_ready, 4 * i + (g * STEPS + s + 3))
            c = CTS[g % 2][:, :, bass.ds(4 * TG * i + TG * s, TG)]
            dve.tensor_tensor(c, c, ps[:, 2 + s % 2, 0:TG * QTR].rearrange("p (t e) -> p e t", t=TG), ALU.mult
                              ).then_inc(gate_used, 1)

        def weave(q, g):
            def step(i, s, last=False):
                more = not (last and s == RAW - 1)
                if more:
                    hots(i + (s + 1) // RAW, (s + 1) % RAW, g, q is None)
                if q is not None and more:
                    u_split(i, s, q)
                weigh(i, s, g)

            if q is None:
                dve.wait_ge(flushed, 4 * g)
                dve.tensor_copy(ps[:, 0, 0:P], IOTA).then_inc(iota_ready, 1)
                dve.wait_ge(iota_ready, 1)
            hots(0, 0, g, q is None)
            with dve.Fori(0, LOOPS - 1) as i:
                for s in range(RAW):
                    step(i, s)
            for s in range(RAW):
                step(LOOPS - 1, s, True)

        dve.tensor_copy(IOTA_B, IOTA)
        dve.tensor_copy(E1B, E1T)
        dve.tensor_copy(E2B, E2T)
        done(dve.tensor_copy(GATES[:, 0], GT))
        done(dve.tensor_tensor(REST[:, 0], GT, GATES[:, 0], ALU.subtract))
        done(dve.tensor_copy(GATES[:, 1], REST[:, 0]))
        done(dve.tensor_tensor(REST[:, 1], REST[:, 0], GATES[:, 1], ALU.subtract))
        done(dve.tensor_copy(GATES[:, 2], REST[:, 1]))
        weave(1, 0)
        st.meet()
        for q in range(PARTS):
            def low_c(i, s):
                dve.wait_ge(c_hi_done, 4 * i + (q * QTR + s + 1))
                dve.tensor_tensor(c_lo[:, s % 2], CTS[q % 2][:, bass.ds(4 * i + s, 1)].rearrange("p a t -> p (a t)"),
                                  c_hi[:, s % 2].bitcast(F32), ALU.subtract).then_inc(c_lo_done, 1)

            def v_step(i, s, last):
                if not (last and s == 3):
                    low_c(i + (s + 1) // 4, (s + 1) % 4)
                if not (last and (s >= 2 and q == PARTS - 1 or s == 3)):
                    split(i + (v_first[q] // 4 + (s + 2) // 4), (s + 2) % 4, 2048)

            low_c(0, 0)
            if q + 1 < PARTS:
                u_split(LOOPS - 1, RAW - 1, q + 1)
            for s in range(RAW):
                v_step(0, s, False)
            with dve.Fori(1, LOOPS - 1) as i:
                for s in range(RAW):
                    v_step(i, s, False)
            for s in range(RAW):
                v_step(LOOPS - 1, s, True)
            st.meet()
            if q == 0:
                dve.wait_ge(moved, 16)
            for b in range(4 if q + 1 < PARTS else 8):
                y = YT[:, b // 4, (b % 4) * 512:(b % 4 + 1) * 512]
                if q == 0 or b >= 4:
                    dve.tensor_copy(y, ps[:, b, :]).then_inc(flushed, 1)
                else:
                    dve.tensor_tensor(y, y, ps[:, b, :], ALU.add).then_inc(flushed, 1)
            if q + 1 < PARTS:
                split(LOOPS - 1 + v_first[q] // 4 + 1, 1, 2048)
                weave(q + 2 if q + 2 < PARTS else None, q + 1)
                st.meet()
        dve.wait_ge(fin_in, 32)
        for b, (srcs, outs) in enumerate(plan["fin"].blocks):
            n = plan["fin"].first + b
            dve.wait_ge(turn_ready, n + 1)
            piece = slice((b % 4) * 512, (b % 4 + 1) * 512)
            dve.tensor_tensor(FIN[:, b // 4, piece], ps[:, 4 + n % 4, :], XD[:, b // 4, piece], ALU.add
                              ).then_inc(turn_dve, 1)
        dve.wait_ge(fin_sum, 8)
        done(dve.tensor_reduce(sm(136, 2), sm(128, 8).rearrange("p (t b) -> p t b", t=NT), AX, ALU.add))
        dve.tensor_scalar(sm(136, 2), sm(136, 2), 1.0 / D, EPS, ALU.mult, ALU.add).then_inc(fin_var, 1)
        dve.wait_ge(fin_sd, 1)
        done(dve.reciprocal(sm(136, 2), sm(138, 2)))
        for t in range(NT):
            dve.scalar_tensor_tensor(out=FIN[:, t], in0=FIN[:, t], scalar=sm(136 + t), in1=GFIN,
                                     op0=ALU.mult, op1=ALU.mult).then_inc(dve_out, 1)


def kernel(**inputs):
    from concourse import bacc as _bacc
    from concourse.bass_utils import run_bass_kernel_spmd as _run

    c = np.ascontiguousarray
    a = {k: np.asarray(v) for k, v in inputs.items()}
    rows = [a.pop("mem_norm_gain")[None], a.pop("norm_gain")] + [
        a.pop(k) for k in ("g_mix_2", "g_mem_2", "g_cross_2", "g_ffn_2")]
    a["gains"] = c(np.concatenate(rows).reshape(7, KC, P).transpose(2, 0, 1))
    a["pool_scale_2"] = c(a["pool_scale_2"].reshape(8, P).T)
    a["positions_2"] = c(a["positions_2"].reshape(NT, P).T)
    a["pe_t"] = c(a.pop("nsa_cmp_pos")[0].transpose(2, 0, 1))
    a["cmp_w2"] = c(a.pop("nsa_cmp_w2")[0].reshape(2, 2, P, P).transpose(2, 0, 1, 3))
    a["sub_keys"] = c(np.stack([a.pop("sub_keys_1_2")[0], a.pop("sub_keys_2_2")[0]]))
    a["mem"], a["mem_2"] = a["mem"][0], a["mem_2"][0]
    def cut(w, step=COLS):
        rows, width = w.shape
        out_ = []
        for c0 in range(0, width, step):
            g = w[:, c0:c0 + step]
            out_.append(g.reshape(rows // (4 * P), 4, P, g.shape[1]).transpose(0, 2, 1, 3).reshape(-1))
        return np.concatenate(out_)

    for l in range(2):
        a[f"mem_w_kv.{l}"] = cut(a["mem_w_kv"][l])
        a[f"w_out.{l}"] = cut(a["w_out"][l])
    del a["mem_w_kv"], a["w_out"]
    w = a.pop("even_w_in")[0]
    for c0, c1, step in ((EM, EVEN_IN, COLS), (EB, EM, COLS), (0, EA_Z, STEP_A), (EA_Z, EB, COLS)):
        a[f"even_w.{c0}"] = cut(w[:, c0:c1], step)
    w = a.pop("odd_w_in")[0]
    for c0, c1, step in ((OM, ODD_IN, COLS), (OI, OZ, STEP_CI), (0, OI, COLS), (OZ, OM, COLS)):
        a[f"odd_w.{c0}"] = cut(w[:, c0:c1], step)
    for k in ("w_in_2", "w_out_2", "w_ck_2", "w_cv_2", "w_cq_2"):
        a[f"{k}.0"] = cut(a.pop(k)[0])
    a["w_co_2"] = cut(a["w_co_2"][0]).reshape(4, P, 2048)
    a["w_pq_2"] = cut(a["w_pq_2"][0]).reshape(4, 4, P, 2048)
    a["cmp_w1"] = c(a.pop("nsa_cmp_w1")[0].reshape(2, 4, 8, P, CMP_HID).transpose(0, 1, 3, 2, 4)).reshape(2, 4, P, 2048)
    a["w_u_t"] = c(a.pop("w_u_2")[0].reshape(E1, E1, KC, P).transpose(1, 3, 2, 0)).reshape(E1, P, KC * E1)
    a.update(CONSTS)

    nc = _bacc.Bacc("TRN2", target_bir_lowering=False, num_devices=1)
    arrays, aps = {}, {}
    for k, v in a.items():
        v = c(v)
        arrays[f"in_{k}"] = v
        aps[k] = nc.dram_tensor(f"in_{k}", v.shape, mybir.dt.from_np(v.dtype), kind="ExternalInput").ap()
    o = nc.dram_tensor("out_0", (1, S, D), F32, kind="ExternalOutput").ap()
    build(nc, aps, o)
    r = _run(nc, [arrays], core_ids=[0])
    return r.results[0]["out_0"]
```
